# Optimizing a Trainium2 kernel written in Bass

```python
import jax, jax.numpy as jnp
from jax import lax
import numpy as np

D_MODEL = 1024
BATCH = 1
SEQ = 512
DEPTH = 2
DEC_BATCH = 1
DEC_SEQ = 64
PAST_LEN = 512

CHUNK = 64
N_MIXERS = 2
N_SSD_LAYERS = (DEPTH + 1) // 2
N_CMLP_LAYERS = DEPTH // 2
SSD_D_INNER = 2 * D_MODEL
SSD_HEAD_DIM = 64
SSD_HEADS = SSD_D_INNER // SSD_HEAD_DIM
SSD_GROUPS = 8
SSD_STATE = 128
SSD_CONV = 4
SSD_CONV_DIM = SSD_D_INNER + 2 * SSD_GROUPS * SSD_STATE
SSD_IN_DIM = SSD_D_INNER + SSD_CONV_DIM + SSD_HEADS
CM_BLOCK = 128
CM_WIDTH = 2 * D_MODEL
CM_GROUPS = 8
FFN_HIDDEN = 4 * D_MODEL
DN_ALPHA = (2 * DEPTH) ** 0.25
DN_BETA = (8 * DEPTH) ** -0.25
LN_EPS = 1e-5

kernel_name = "hybrid_ssd_chunk_gmlp_streaming_step"

def layer_norm(x, g, b):
    xf = x.astype(jnp.float32)
    mu = jnp.mean(xf, axis=-1, keepdims=True)
    var = jnp.mean(jnp.square(xf - mu), axis=-1, keepdims=True)
    return ((xf - mu) * lax.rsqrt(var + LN_EPS) * g + b).astype(x.dtype)

def causal_conv_silu(xbc, prev, w, b):
    L = xbc.shape[1]
    full = jnp.concatenate([prev.astype(xbc.dtype), xbc], axis=1)
    acc = full[:, 0:L] * w[0]
    for k in range(1, SSD_CONV):
        acc = acc + full[:, k:k + L] * w[k]
    return jax.nn.silu(acc + b), full[:, -(SSD_CONV - 1):]

def ssd_scan(xh, dt, A, Bm, Cm, h0):
    b, L, H, P = xh.shape
    G, N = Bm.shape[2], Bm.shape[3]
    R = H // G
    Q = CHUNK if L % CHUNK == 0 else L
    nc = L // Q

    def to_blocks(t):
        return jnp.moveaxis(t.reshape((b, nc, Q) + t.shape[2:]), 1, 0)

    xdt = (xh.astype(jnp.float32) * dt[..., None]).reshape(b, L, G, R, P)
    dA = (dt * A).reshape(b, L, G, R)
    xs = (to_blocks(xdt), to_blocks(dA), to_blocks(Bm.astype(jnp.float32)), to_blocks(Cm.astype(jnp.float32)))
    causal = jnp.tril(jnp.ones((Q, Q), dtype=bool))[None, :, :, None, None]

    def step(h, inp):
        xc, dac, bc, cc = inp
        acum = jnp.cumsum(dac, axis=1)
        seg = acum[:, :, None] - acum[:, None, :]
        decay = jnp.exp(jnp.where(causal, seg, -jnp.inf))
        cb = jnp.einsum('btgn,bsgn->btsg', cc, bc)
        y_diag = jnp.einsum('btsg,btsgr,bsgrp->btgrp', cb, decay, xc)
        y_off = jnp.einsum('btgn,bgrpn,btgr->btgrp', cc, h, jnp.exp(acum))
        a_last = acum[:, -1]
        w_in = jnp.exp(a_last[:, None] - acum)
        h_new = h * jnp.exp(a_last)[..., None, None] + jnp.einsum('bsgn,bsgr,bsgrp->bgrpn', bc, w_in, xc)
        return h_new, y_diag + y_off

    hT, ys = lax.scan(step, h0.astype(jnp.float32).reshape(b, G, R, P, N), xs)
    y = jnp.moveaxis(ys, 0, 1).reshape(b, L, H, P)
    return y, hT.reshape(b, H, P, N)

def ssd_mixer(x, conv_prev, h0, w_in, conv_w, conv_b, dt_bias, a_log, d_skip, norm_w, w_out):
    b, L, _ = x.shape
    proj = x @ w_in
    z = proj[..., :SSD_D_INNER]
    xbc = proj[..., SSD_D_INNER:SSD_D_INNER + SSD_CONV_DIM]
    dt_raw = proj[..., SSD_D_INNER + SSD_CONV_DIM:]
    xbc, conv_new = causal_conv_silu(xbc, conv_prev, conv_w, conv_b)
    xs = xbc[..., :SSD_D_INNER].reshape(b, L, SSD_HEADS, SSD_HEAD_DIM)
    Bm = xbc[..., SSD_D_INNER:SSD_D_INNER + SSD_GROUPS * SSD_STATE].reshape(b, L, SSD_GROUPS, SSD_STATE)
    Cm = xbc[..., SSD_D_INNER + SSD_GROUPS * SSD_STATE:].reshape(b, L, SSD_GROUPS, SSD_STATE)
    dt = jax.nn.softplus(dt_raw.astype(jnp.float32) + dt_bias.astype(jnp.float32))
    A = -jnp.exp(a_log.astype(jnp.float32))
    y, hT = ssd_scan(xs, dt, A, Bm, Cm, h0)
    y = y + d_skip.astype(jnp.float32)[:, None] * xs.astype(jnp.float32)
    g = y.reshape(b, L, SSD_D_INNER) * jax.nn.silu(z.astype(jnp.float32))
    gg = g.reshape(b, L, SSD_GROUPS, SSD_D_INNER // SSD_GROUPS)
    gg = gg * lax.rsqrt(jnp.mean(jnp.square(gg), axis=-1, keepdims=True) + LN_EPS)
    normed = (gg.reshape(b, L, SSD_D_INNER) * norm_w).astype(x.dtype)
    return normed @ w_out, conv_new, hT.astype(h0.dtype)

def chunk_mlp_mixer(x, w_in, b_in, ln_g, ln_b, w_s, b_s, w_out):
    b, L, _ = x.shape
    h = jax.nn.gelu(x @ w_in + b_in)
    u, v = h[..., :CM_WIDTH], h[..., CM_WIDTH:]
    v = layer_norm(v, ln_g, ln_b)
    nb = L // CM_BLOCK if L % CM_BLOCK == 0 else 1
    blk = L // nb
    mask = jnp.tril(jnp.ones((blk, blk), dtype=bool))
    ws = jnp.where(mask, w_s[:, :blk, :blk], 0.0)
    vb = v.reshape(b, nb, blk, CM_GROUPS, CM_WIDTH // CM_GROUPS)
    s = jnp.einsum('gts,bnsgc->bntgc', ws, vb) + jnp.swapaxes(b_s[:, :blk], 0, 1)[None, None, :, :, None]
    out = u * s.reshape(b, L, CM_WIDTH)
    return out @ w_out, v

def sq_relu_ffn(x, w1, w2):
    return jnp.square(jax.nn.relu(x @ w1)) @ w2

def run_trunk(x, conv_prev, h0, ssd_w_in, ssd_conv_w, ssd_conv_b, ssd_dt_bias, ssd_a_log, ssd_d, ssd_norm_w, ssd_w_out,
              cm_w_in, cm_b_in, cm_ln_g, cm_ln_b, cm_w_s, cm_b_s, cm_w_out, ffn_w1, ffn_w2, ln1_g, ln1_b, ln2_g, ln2_b):
    conv_out, h_out, v_out = [], [], []
    for i in range(DEPTH):
        j = i // N_MIXERS
        if i % N_MIXERS == 0:
            mix, c_new, h_new = ssd_mixer(x, conv_prev[j], h0[j], ssd_w_in[j], ssd_conv_w[j], ssd_conv_b[j], ssd_dt_bias[j],
                                          ssd_a_log[j], ssd_d[j], ssd_norm_w[j], ssd_w_out[j])
            conv_out.append(c_new)
            h_out.append(h_new)
        else:
            mix, v_rows = chunk_mlp_mixer(x, cm_w_in[j], cm_b_in[j], cm_ln_g[j], cm_ln_b[j], cm_w_s[j], cm_b_s[j], cm_w_out[j])
            v_out.append(v_rows)
        x = layer_norm(DN_ALPHA * x + mix, ln1_g[i], ln1_b[i])
        x = layer_norm(DN_ALPHA * x + sq_relu_ffn(x, ffn_w1[i], ffn_w2[i]), ln2_g[i], ln2_b[i])
    return x, conv_out, h_out, v_out

def setup_inputs(seed: int = 0) -> dict:
    key = jax.random.key(seed)
    ks = jax.random.split(key, 32)
    f32 = jnp.float32

    def nrm(k, shape, scale):
        return jax.random.normal(k, shape, f32) * scale

    nS, nC = N_SSD_LAYERS, N_CMLP_LAYERS
    dt0 = jnp.exp(jax.random.uniform(ks[8], (nS, SSD_HEADS), f32, np.log(1e-3), np.log(1e-1)))
    dt_bias = dt0 + jnp.log(-jnp.expm1(-dt0))
    return {
        "x_prompt": nrm(ks[0], (BATCH, SEQ, D_MODEL), 1.0),
        "x_sample": nrm(ks[1], (DEC_BATCH, DEC_SEQ, D_MODEL), 1.0),
        "state_ssm": nrm(ks[2], (nS, DEC_BATCH, SSD_HEADS, SSD_HEAD_DIM, SSD_STATE), 0.5),
        "state_conv": nrm(ks[3], (nS, DEC_BATCH, SSD_CONV - 1, SSD_CONV_DIM), 1.0),
        "ssd_w_in": nrm(ks[4], (nS, D_MODEL, SSD_IN_DIM), D_MODEL ** -0.5),
        "ssd_conv_w": nrm(ks[5], (nS, SSD_CONV, SSD_CONV_DIM), SSD_CONV ** -0.5),
        "ssd_conv_b": nrm(ks[6], (nS, SSD_CONV_DIM), 0.02),
        "ssd_dt_bias": dt_bias,
        "ssd_a_log": jnp.log(jax.random.uniform(ks[9], (nS, SSD_HEADS), f32, 1.0, 16.0)),
        "ssd_d": 1.0 + nrm(ks[10], (nS, SSD_HEADS), 0.1),
        "ssd_norm_w": 1.0 + nrm(ks[11], (nS, SSD_D_INNER), 0.02),
        "ssd_w_out": nrm(ks[12], (nS, SSD_D_INNER, D_MODEL), SSD_D_INNER ** -0.5 * DN_BETA),
        "cm_w_in": nrm(ks[13], (nC, D_MODEL, 2 * CM_WIDTH), D_MODEL ** -0.5),
        "cm_b_in": nrm(ks[14], (nC, 2 * CM_WIDTH), 0.02),
        "cm_ln_g": 1.0 + nrm(ks[15], (nC, CM_WIDTH), 0.02),
        "cm_ln_b": nrm(ks[16], (nC, CM_WIDTH), 0.02),
        "cm_w_s": nrm(ks[17], (nC, CM_GROUPS, CM_BLOCK, CM_BLOCK), CM_BLOCK ** -0.5),
        "cm_b_s": 1.0 + nrm(ks[18], (nC, CM_GROUPS, CM_BLOCK), 0.1),
        "cm_w_out": nrm(ks[19], (nC, CM_WIDTH, D_MODEL), CM_WIDTH ** -0.5 * DN_BETA),
        "ffn_w1": nrm(ks[20], (DEPTH, D_MODEL, FFN_HIDDEN), D_MODEL ** -0.5),
        "ffn_w2": nrm(ks[21], (DEPTH, FFN_HIDDEN, D_MODEL), FFN_HIDDEN ** -0.5 * DN_BETA),
        "ln1_g": 1.0 + nrm(ks[22], (DEPTH, D_MODEL), 0.02),
        "ln1_b": nrm(ks[23], (DEPTH, D_MODEL), 0.02),
        "ln2_g": 1.0 + nrm(ks[24], (DEPTH, D_MODEL), 0.02),
        "ln2_b": nrm(ks[25], (DEPTH, D_MODEL), 0.02),
    }

def reference(x_prompt, x_sample, state_ssm, state_conv, ssd_w_in, ssd_conv_w, ssd_conv_b, ssd_dt_bias, ssd_a_log, ssd_d,
              ssd_norm_w, ssd_w_out, cm_w_in, cm_b_in, cm_ln_g, cm_ln_b, cm_w_s, cm_b_s, cm_w_out, ffn_w1, ffn_w2,
              ln1_g, ln1_b, ln2_g, ln2_b):
    weights = (ssd_w_in, ssd_conv_w, ssd_conv_b, ssd_dt_bias, ssd_a_log, ssd_d, ssd_norm_w, ssd_w_out,
               cm_w_in, cm_b_in, cm_ln_g, cm_ln_b, cm_w_s, cm_b_s, cm_w_out, ffn_w1, ffn_w2, ln1_g, ln1_b, ln2_g, ln2_b)
    b_p = x_prompt.shape[0]
    conv0 = jnp.zeros((N_SSD_LAYERS, b_p, SSD_CONV - 1, SSD_CONV_DIM), x_prompt.dtype)
    h00 = jnp.zeros((N_SSD_LAYERS, b_p, SSD_HEADS, SSD_HEAD_DIM, SSD_STATE), x_prompt.dtype)
    y_prompt, conv_p, h_p, _ = run_trunk(x_prompt, conv0, h00, *weights)
    y_sample, conv_s, h_s, v_s = run_trunk(x_sample, state_conv, state_ssm, *weights)
    ssm_prompt = jnp.stack(h_p)
    conv_prompt = jnp.stack(conv_p)
    ssm_sample = jnp.stack(h_s)
    conv_sample = jnp.stack(conv_s)
    v_rows_sample = jnp.stack(v_s)
    return (y_prompt, y_sample, ssm_prompt, conv_prompt, ssm_sample, conv_sample, v_rows_sample)


_drawn_inputs = setup_inputs


def setup_inputs(seed=0):
    import zlib

    import numpy as np

    out = dict(_drawn_inputs(seed))
    spreads = {}
    factors = {'ssd_norm_w': 7.215, 'cm_ln_g': 2.752, 'cm_ln_b': 2.901}
    for name, (base, spread) in spreads.items():
        noise = np.random.default_rng([zlib.crc32(name.encode()), seed]).standard_normal(out[name].shape)
        drawn = base * np.exp(spread * noise) if base else spread * noise
        out[name] = __import__('jax').numpy.asarray(drawn.astype(out[name].dtype))
    for name, factor in factors.items():
        out[name] = (out[name] * factor).astype(out[name].dtype)
    return out
```

```python
from contextlib import ExitStack

import concourse.bass as bass
from concourse import mybir

F32 = mybir.dt.float32
F32R = mybir.dt.float32r
ALU = mybir.AluOpType
ACT = mybir.ActivationFunctionType

P = 128
D = 1024
KT = D // P
TP, TS = 512, 64
T = TP + TS
HT = T // 2
UNIT = 1024
HALO = 3
RAW = HALO + TP + HALO + TS
CONV = RAW - HALO
GROUPS, HPG, HD, NST = 8, 4, 64, 128
HEADS = GROUPS * HPG
Q = 128
NCH = 5
ALPHA = (2 * 2) ** 0.25
EPS = 1e-5
BLK = 128
NTOK = 5
CMW = 2048

U_SSD = 1
U_WOUT = U_SSD + 6 * GROUPS
U_FFN0 = U_WOUT + 16
U_V = U_FFN0 + 64
U_U = U_V + 16
U_CMOUT = U_U + 16
U_FFN1 = U_CMOUT + 16
UNITS = U_FFN1 + 64

PV_CONV = 0
PV_GRP = PV_CONV + GROUPS * 20
PV_BU = PV_GRP + GROUPS * 4
PV_LN = PV_BU + 16
PV_DTB = PV_LN + 4 * 16
PV_ALOG = PV_DTB + 1
PV_N = PV_ALOG + 1

DT_OUT = 7
DT_ACUM = 14
DT_STEPS = 15

ORDER = [0, 4, 1, 2, 3]


def cols(n):
    c = ORDER[n]
    return c * Q, (TS if c == 4 else Q)


def slot_turn(u):
    return (u if u < U_V else u - 16) // 2


FFN_BLOCKS = [("up", 0), ("up", 1), ("down", 0), ("up", 2), ("down", 1), ("up", 3), ("down", 2), ("down", 3)]


class Semaphores:

    def __init__(self, sem):
        self.tick_zero = sem("tick_zero")
        self.w_in0 = sem("w_in0")
        self.w_in1 = sem("w_in1")
        self.w_hi = sem("w_hi")
        self.w_ready = sem("w_ready")
        self.gemm_done = sem("gemm_done")
        self.slot_evac0 = sem("slot_evac0")
        self.slot_evac1 = sem("slot_evac1")
        self.x_in0 = sem("x_in0")
        self.x_in1 = sem("x_in1")
        self.x_in2 = sem("x_in2")
        self.x_in3 = sem("x_in3")
        self.pv_in = sem("pv_in")
        self.chalo_in = sem("chalo_in")
        self.x_hi = sem("x_hi")
        self.x_lo = sem("x_lo")
        self.consts = sem("consts")
        self.tokd_zero = sem("tokd_zero")
        self.raw_zero = sem("raw_zero")
        self.dt_act = sem("dt_act")
        self.dt_dve = sem("dt_dve")
        self.tok_t = sem("tok_t")
        self.tokd_ready = sem("tokd_ready")
        self.acum_out = sem("acum_out")
        self.acb_in = sem("acb_in")
        self.hs_in = sem("hs_in")
        self.hs_out = sem("hs_out")
        self.hp_out = sem("hp_out")
        self.cpar_ready = sem("cpar_ready")
        self.gdt_ready = sem("gdt_ready")
        self.gpar_ready = sem("gpar_ready")
        self.win_arg = sem("win_arg")
        self.win_exp = sem("win_exp")
        self.dtw_ready = sem("dtw_ready")
        self.conv_tap = sem("conv_tap")
        self.silu_ready = sem("silu_ready")
        self.dec_sub = sem("dec_sub")
        self.dec_arg = sem("dec_arg")
        self.dec_exp = sem("dec_exp")
        self.ea_ready = sem("ea_ready")
        self.cs_ready = sem("cs_ready")
        self.s1_done = sem("s1_done")
        self.cbm_ready = sem("cbm_ready")
        self.xw_ready = sem("xw_ready")
        self.m_ready = sem("m_ready")
        self.s_done = sem("s_done")
        self.y_evac = sem("y_evac")
        self.hdec_ready = sem("hdec_ready")
        self.h_ready = sem("h_ready")
        self.gate_ready = sem("gate_ready")
        self.sq_ready = sem("sq_ready")
        self.ms_done = sem("ms_done")
        self.ms_ln = sem("ms_ln")
        self.rms_ready = sem("rms_ready")
        self.yn_f = sem("yn_f")
        self.yn_hi = sem("yn_hi")
        self.yn_lo = sem("yn_lo")
        self.ctail_ready = sem("ctail_ready")
        self.tail_out = sem("tail_out")
        self.hid_ready = sem("hid_ready")
        self.hid_hi = sem("hid_hi")
        self.hid_lo = sem("hid_lo")
        self.res_ready = sem("res_ready")
        self.stat_zero = sem("stat_zero")
        self.sum1_ready = sem("sum1_ready")
        self.sqr_ready = sem("sqr_ready")
        self.sum2_ready = sem("sum2_ready")
        self.stat_done = sem("stat_done")
        self.msq_ready = sem("msq_ready")
        self.var_ready = sem("var_ready")
        self.var_ln = sem("var_ln")
        self.rstd_ready = sem("rstd_ready")
        self.mr_ready = sem("mr_ready")
        self.nrm_a = sem("nrm_a")
        self.nrm_b = sem("nrm_b")
        self.nrm_x = sem("nrm_x")
        self.x_round = sem("x_round")
        self.y_out0 = sem("y_out0")
        self.y_out1 = sem("y_out1")
        self.bb_in = sem("bb_in")
        self.gam_in = sem("gam_in")
        self.bet_in = sem("bet_in")
        self.ws_in = sem("ws_in")
        self.bs_in = sem("bs_in")
        self.ws_masked = sem("ws_masked")
        self.v_done = sem("v_done")
        self.v_bias = sem("v_bias")
        self.v_gelu = sem("v_gelu")
        self.v_stat = sem("v_stat")
        self.v_mv = sem("v_mv")
        self.v_ln = sem("v_ln")
        self.v_rs = sem("v_rs")
        self.v_zero = sem("v_zero")
        self.v_moved = sem("v_moved")
        self.wsm_ready = sem("wsm_ready")
        self.vm_n = sem("vm_n")
        self.vm_g = sem("vm_g")
        self.vm_ready = sem("vm_ready")
        self.vrow_out0 = sem("vrow_out0")
        self.vrow_out1 = sem("vrow_out1")
        self.mix_done = sem("mix_done")
        self.s_bias = sem("s_bias")
        self.uv_ready = sem("uv_ready")
        self.uv_hi = sem("uv_hi")
        self.uv_lo = sem("uv_lo")


class Memory:

    def __init__(self, nc, ctx):
        base = (nc.sbuf_base + 63) // 64 * 64
        end = nc.sbuf_usable_end
        self.at = base

        def put(name, shape, dt=F32, offset=None):
            n = 4
            for s in shape[1:]:
                n *= s
            where = self.at if offset is None else (offset + 31) // 32 * 32
            assert where + n <= end, (name, where + n - end)
            if offset is None:
                self.at += (n + 31) // 32 * 32
            return nc.alloc_sbuf_tensor_at(name, shape, dt, offset=where)

        self.xh = put("xh", [P, KT, T], F32R)
        self.xl = put("xl", [P, KT, T], F32R)
        h0 = self.at
        self.hh = put("hh", [P, 16, T], F32R)
        l0 = self.at
        self.hl = put("hl", [P, 16, T], F32R)
        self.wraw = put("wraw", [P, 2, UNIT])
        self.wh = put("wh", [P, 2, UNIT], F32R)
        self.wl = put("wl", [P, 2, UNIT], F32R)
        self.pv = put("pv", [P, PV_N])
        self.ident = put("ident", [P, P])
        self.ones = put("ones", [P, P])
        self.causal = put("causal", [P, P])
        self.eps = put("eps", [P, 1])
        self.nega = put("nega", [P, 1])
        self.tick = put("tick", [P, 2])

        t0 = self.at

        self.raw = put("raw", [P, 2, RAW])
        self.acc = put("acc", [P, 4, CONV])
        self.act = put("act", [P, 4, T])
        self.zs = put("zs", [P, 2, T])
        self.acb = put("acb", [P, HPG, T])
        self.y = put("y", [P, 2, T])
        self.sq = put("sq", [P, 2, T])
        self.rms = put("rms", [P, T])
        self.ea = put("ea", [P, 2, HPG, Q])
        self.btok = put("btok", [P, 2, NST])
        self.cbm = put("cbm", [P, 2, Q])
        self.xdt = put("xdt", [P, 2, HPG * HD])
        self.xw = put("xw", [P, 2, HPG * HD])
        self.hp = put("hp", [P, HPG * HD])
        self.hs = put("hs", [P, HPG * HD])
        self.hsn = put("hsn", [P, HPG * HD])
        self.hdec = put("hdec", [P, HPG * HD])
        self.tokd = put("tokd", [P, NCH, 2 * HEADS])
        self.gdt = put("gdt", [P, NCH, HPG])
        self.gac = put("gac", [P, NCH, HPG])
        self.win = put("win", [P, NCH, HPG])
        self.dtw = put("dtw", [P, NCH, HPG])
        self.cpar = put("cpar", [P, 4, 5])
        self.gpar = put("gpar", [P, 4])
        self.ctail = put("ctail", [P, GROUPS, 4, 2, HALO])
        self.chalo = put("chalo", [P, GROUPS, 4, HALO])
        self.dec = put("dec", [P, 2, HPG, Q], offset=h0 + 14 * T * 4)
        self.cs = put("cs", [P, 2, HPG, Q], offset=l0 + 14 * T * 4)
        self.xr = put("xr", [P, KT, T], offset=t0)
        self.dtt = put("dtt", [P, 8, T], offset=t0 + 2 * RAW * 4)

        row = T * 4
        self.r = put("r", [P, KT, T], offset=t0)
        self.rt = put("rt", [P, 2, T], offset=t0 + 8 * row)
        self.rl = put("rl", [P, 2, T], offset=t0 + 10 * row + 96)
        self.hq = put("hq", [P, 2, T], offset=t0 + 12 * row + 96)
        self.s1 = put("s1", [P, T], offset=t0 + 14 * row + 96)
        self.s2 = put("s2", [P, T], offset=t0 + 15 * row + 96)
        e0 = t0 + 20 * row + 96 + 64
        self.msq = put("msq", [P, T], offset=e0)
        self.rstd = put("rstd", [P, T], offset=e0 + row)
        self.mr = put("mr", [P, T], offset=e0 + 2 * row)
        self.na = put("na", [P, 2, T], offset=e0 + 3 * row)
        self.xf = put("xf", [P, 2, T], offset=e0 + 5 * row)
        self.sqm = put("sqm", [P, 2, T], offset=e0 + 8 * row)

        self.gam = put("gam", [P, CMW], offset=t0)
        self.bet = put("bet", [P, CMW], offset=t0 + CMW * 4)
        g0 = t0 + 8 * row
        vrow = NTOK * P * 4
        self.v1 = put("v1", [P, 8, NTOK, P], offset=g0)
        self.v2 = put("v2", [P, 2, 16 * T], offset=h0)
        self.bb = put("bb", [P, CMW], offset=l0)
        g0 += 8 * vrow
        self.vm = put("vm", [P, 2, NTOK, P], offset=g0)
        g0 += 2 * vrow
        self.wsm = put("wsm", [P, BLK], offset=g0)
        g0 += BLK * 4
        self.wst = put("wst", [P, 8, BLK], offset=g0)
        g0 += 8 * BLK * 4
        self.bsb = put("bsb", [P, 8, BLK], offset=g0)
        g0 += 8 * BLK * 4
        self.ug = put("ug", [P, 2, T], offset=g0)
        g0 += 2 * row
        self.sb = put("sb", [P, 2, T], offset=g0)
        g0 += 2 * row
        self.vst = put("vst", [P, NTOK, 4, 6], offset=g0)
        g0 += NTOK * 4 * 6 * 4
        self.vmv = put("vmv", [P, NTOK, 2], offset=g0)
        g0 += 64
        self.vrs = put("vrs", [P, NTOK, 1], offset=g0)

        self.ps = ctx.enter_context(nc.psum_tensor("ps", [P, 8, 512], F32))
        self.acum_dram = nc.dram_tensor("acum_scratch", [HEADS, T], F32).ap()

        self.sem = S = Semaphores(lambda name: ctx.enter_context(nc.semaphore(name)))
        self.w_in = [S.w_in0, S.w_in1]
        self.slot_evac = [S.slot_evac0, S.slot_evac1]
        self.x_in = [S.x_in0, S.x_in1, S.x_in2, S.x_in3]
        self.y_out = [S.y_out0, S.y_out1]
        self.vrow_out = [S.vrow_out0, S.vrow_out1]


def wait(engine, sem, value):
    if not isinstance(value, int) or value > 0:
        engine.wait_ge(sem, value)


def one(t, i):
    if isinstance(i, int):
        return t[:, i]
    v = t[:, bass.ds(i, 1)]
    if len(v.shape) == 3:
        return v.rearrange("p a t -> p (a t)")
    if len(v.shape) == 4:
        return v.rearrange("p a b t -> p (a b) t")
    return v.rearrange("p a b c t -> p (a b) c t")


def halves(ap):
    return ap.rearrange("p (h t) -> p h t", h=2)


def bank_pair(m, s):
    return m.ps[:, 2 * s:2 * s + 2, 0:HT]


def spread(ap, n):
    return ap.unsqueeze(2).to_broadcast([ap.shape[0], ap.shape[1], n])


def repeat(ap, n):
    return ap.unsqueeze(1).to_broadcast([ap.shape[0], n, ap.shape[1]])



def sync_program(sp, m, A):
    S = m.sem
    sp.dma_start(m.wraw[:, 0], A["wstream"][0]).then_inc(m.w_in[0], 16)
    for n in range(4):
        sp.dma_start(m.xr[:, 2 * n:2 * n + 2], A["x"][:, 2 * n:2 * n + 2]).then_inc(m.x_in[n], 16)
    sp.dma_start(m.wraw[:, 1], A["wstream"][1]).then_inc(m.w_in[1], 16)
    sp.wait_ge(S.w_ready, 1)
    sp.dma_start(m.wraw[:, 0], A["wstream"][2]).then_inc(m.w_in[0], 16)
    with sp.Fori(0, (UNITS - 3) // 2) as i:
        for j in range(2):
            s = (3 + j) % 2
            sp.wait_ge(S.w_ready, 2 * i + (j + 2))
            src = A["wstream"][bass.ds(2 * i + (3 + j), 1)].rearrange("a p n -> p (a n)")
            sp.dma_start(m.wraw[:, s], src).then_inc(m.w_in[s], 16)
    with sp.Fori(0, KT // 2) as i:
        for j in range(2):
            sp.wait_ge(S.nrm_x, 2 * i + (24 + j + 1))
            sp.dma_start(one(A["y"], 2 * i + j), one(m.r, 2 * i + j)).then_inc(m.y_out[j], 16)
    for j in range(2):
        sp.wait_ge(m.y_out[j], 16 * KT // 2)
        sp.wait_ge(m.vrow_out[j], 16 * 8)
    sp.wait_ge(S.tail_out, 16)
    sp.wait_ge(S.hs_out, 16 * GROUPS)
    sp.wait_ge(S.hp_out, 16 * GROUPS)
    sp.wait_ge(S.acum_out, 16)



def pool_program(pool, m, A):
    S = m.sem

    def split(u, s, arrived):
        pool.wait_ge(m.w_in[s], arrived)
        wait(pool, S.gemm_done, u - 1)
        pool.tensor_tensor(m.tick[:, 1:2], m.tick[:, 0:1], m.tick[:, 0:1], ALU.add)
        pool.tensor_scalar(m.wh[:, s], m.wraw[:, s], 1.0, 1.0, ALU.mult, ALU.mult).then_inc(S.w_hi, 1)
        pool.wait_ge(S.w_hi, u + 1)
        pool.tensor_tensor(m.wl[:, s], m.wraw[:, s], m.wh[:, s], ALU.subtract).then_inc(S.w_ready, 1)

    def run(u0, n):
        with pool.Fori(0, n) as i:
            for j in range(2):
                u = u0 + j
                split(2 * i + u, u % 2, 16 * i + 16 * (u // 2 + 1))

    pool.memset(m.tick[:, :], 0.0).then_inc(S.tick_zero, 1)
    pool.wait_ge(S.tick_zero, 1)
    split(0, 0, 16)
    pool.memset(m.ident[:, :], 0.0).then_inc(S.consts, 1)
    pool.memset(m.causal[:, :], 1.0).then_inc(S.consts, 1)
    pool.memset(m.ones[:, :], 1.0).then_inc(S.consts, 1)
    pool.memset(m.eps[:, :], EPS).then_inc(S.consts, 1)
    pool.memset(m.tokd[:, NCH - 1, :], 0.0).then_inc(S.tokd_zero, 1)
    pool.wait_ge(S.consts, 2)
    pool.affine_select(out=m.ident[:, :], in_=m.ident[:, :], compare_op=ALU.not_equal, fill=1.0, base=0,
                       pattern=[[-1, P]], channel_multiplier=1).then_inc(S.consts, 1)
    pool.affine_select(out=m.causal[:, :], in_=m.causal[:, :], compare_op=ALU.is_ge, fill=0.0, base=0,
                       pattern=[[1, P]], channel_multiplier=-1).then_inc(S.consts, 1)
    split(1, 1, 16)
    split(2, 0, 32)
    run(3, (U_U - 3) // 2)
    pool.wait_ge(S.ws_in, 16)
    pool.affine_select(out=m.wst[:, :, :], in_=m.wst[:, :, :], compare_op=ALU.is_ge, fill=0.0, base=0,
                       pattern=[[0, 8], [1, BLK]], channel_multiplier=-1).then_inc(S.ws_masked, 1)
    run(U_U, (UNITS - U_U) // 2)



def tensor_program(pe, m, A):
    S = m.sem
    mm = pe.matmul

    def unit(u, s, turn, xh, xl):
        pe.wait_ge(S.w_ready, u + 1)
        wait(pe, m.slot_evac[s], turn)
        for h in range(2):
            out = m.ps[:, 2 * s + h, 0:HT]
            for k in range(KT):
                w_hi, w_lo = m.wh[:, s, k * P:(k + 1) * P], m.wl[:, s, k * P:(k + 1) * P]
                x_hi, x_lo = xh[:, k, h * HT:(h + 1) * HT], xl[:, k, h * HT:(h + 1) * HT]
                mm(out, w_hi, x_hi, start=(k == 0), stop=False)
                mm(out, w_hi, x_lo, start=False, stop=False)
                last = mm(out, w_lo, x_hi, start=False, stop=(k == KT - 1))
        last.then_inc(S.gemm_done, 1)

    def run(u0, n, xh, xl):
        with pe.Fori(0, n) as i:
            for j in range(2):
                unit(2 * i + (u0 + j), (u0 + j) % 2, i + slot_turn(u0 + j), xh, xl)

    pe.wait_ge(S.x_lo, KT)
    for u in range(6):
        unit(u, u % 2, slot_turn(u), m.xh, m.xl)
    pe.wait_ge(S.dt_dve, DT_STEPS)
    pe.wait_ge(S.consts, 6)
    for c in range(NCH):
        n = TS if c == 4 else Q
        last = pe.transpose(m.ps[0:n, 4 + c // 4, (c % 4) * P:(c % 4) * P + P],
                            m.dtt[:, DT_OUT, c * Q:c * Q + n], m.ident[:, :])
    last.then_inc(S.tok_t, 1)
    unit(6, 0, slot_turn(6), m.xh, m.xl)

    def chunk_in(g, n):
        t0, q = cols(n)
        b = m.ps[:, 4 + n % 2, :]
        if n == 0:
            pe.wait_ge(S.silu_ready, 4 * g + 4)
            wait(pe, S.ms_ln, g)
            pe.wait_ge(S.tokd_ready, 2)
        if n in (2, 4):
            pe.wait_ge(S.xw_ready, 5 * g + (n - 1))
        if n == 3:
            pe.wait_ge(S.y_evac, 5 * g + 2)
        mm(b[0:q, 0:q], m.act[:, 0, t0:t0 + q], m.act[:, 1, t0:t0 + q], start=True, stop=True)
        for j, tile in enumerate((0, 2, 3)):
            last = pe.transpose(b[0:q, (j + 1) * P:(j + 2) * P], m.act[:, tile, t0:t0 + q], m.ident[:, :])
        last.then_inc(S.s1_done, 1)

    def chunk_out(g, n):
        t0, q = cols(n)
        k = n % 2
        yb = m.ps[:, 5 if n == 1 else 6, :]
        h = m.hs if n == 1 else m.hp
        pe.wait_ge(S.m_ready, 5 * g + (n + 1))
        if n == 0:
            wait(pe, S.h_ready, 5 * g)
        else:
            pe.wait_ge(S.cs_ready, 4 * g + n)
            pe.wait_ge(S.h_ready, 5 * g + n)
        if n == 1:
            pe.wait_ge(S.hs_in, 16 * g + 16)
        mm(m.ps[:, 7, 0:HPG * HD], m.btok[0:q, k, :], m.xw[0:q, k, :], start=True, stop=True)
        for j in range(2):
            for p in range(2):
                e = 2 * j + p
                out = yb[p * HD:(p + 1) * HD, j * Q:j * Q + q]
                last = mm(out, m.xdt[0:q, k, e * HD:(e + 1) * HD], m.dec[0:q, k, e, 0:q], start=True, stop=(n == 0))
                if n > 0:
                    last = mm(out, h[:, e * HD:(e + 1) * HD], m.cs[:, k, e, 0:q], start=False, stop=True)
        last.then_inc(S.s_done, 1)

    def mean_squares(g):
        pe.wait_ge(S.sq_ready, g + 1)
        for h in range(2):
            for j in range(2):
                last = mm(m.ps[:, 4 + h, 0:HT], m.ones[:, :], m.sq[:, j, h * HT:(h + 1) * HT],
                          start=(j == 0), stop=(j == 1))
        last.then_inc(S.ms_done, 1)

    def group(g, more):
        def nxt(j):
            if more:
                u0 = U_SSD + 6 + j
                unit(6 * g + u0, u0 % 2, 3 * g + slot_turn(u0), m.xh, m.xl)

        chunk_in(g, 0)
        chunk_in(g, 1)
        nxt(0)
        chunk_out(g, 0)
        chunk_out(g, 1)
        chunk_in(g, 2)
        nxt(1)
        chunk_out(g, 2)
        chunk_in(g, 3)
        nxt(2)
        chunk_out(g, 3)
        chunk_in(g, 4)
        nxt(3)
        chunk_out(g, 4)
        nxt(4)
        if more:
            mean_squares(g)
        nxt(5)

    group(0, True)
    with pe.Fori(1, GROUPS - 1) as g:
        group(g, True)
    group(GROUPS - 1, False)

    pe.wait_ge(S.yn_lo, GROUPS // 2)
    run(U_WOUT, 3, m.hh[:, 0:8], m.hl[:, 0:8])
    mean_squares(GROUPS - 1)
    run(U_WOUT + 6, 1, m.hh[:, 0:8], m.hl[:, 0:8])
    pe.wait_ge(S.yn_lo, GROUPS)
    run(U_WOUT + 8, 4, m.hh[:, 8:16], m.hl[:, 8:16])

    def layer_norm_sums(n):
        pe.wait_ge(S.sum1_ready, 8 * n + 8)
        for h in range(2):
            mm(m.ps[:, 4 + h, 0:HT], m.ones[:, :], m.s1[:, h * HT:(h + 1) * HT], start=True, stop=True)
        pe.wait_ge(S.sum2_ready, 8 * n + 8)
        for h in range(2):
            last = mm(m.ps[:, 6 + h, 0:HT], m.ones[:, :], m.s2[:, h * HT:(h + 1) * HT], start=True, stop=True)
        last.then_inc(S.stat_done, 1)

    def ffn(layer, u0):
        pe.wait_ge(S.x_lo, 8 * (2 * layer + 2))
        for b, (kind, c) in enumerate(FFN_BLOCKS):
            if kind == "up":
                run(u0 + 8 * b, 4, m.xh, m.xl)
            else:
                pe.wait_ge(S.hid_lo, 32 * layer + 8 * (c + 1))
                k = 8 * (c % 2)
                run(u0 + 8 * b, 4, m.hh[:, k:k + 8], m.hl[:, k:k + 8])

    layer_norm_sums(0)
    ffn(0, U_FFN0)
    layer_norm_sums(1)

    def v_block(b):
        for kp in range(4):
            s = (U_V + kp) % 2
            pe.wait_ge(S.w_ready, 4 * b + (U_V + kp + 1))
            for t in range(NTOK):
                n = TS if t == 4 else P
                if kp == 0:
                    wait(pe, S.v_gelu, 5 * b + (t - 4))
                out = m.ps[0:n, t, :]
                for kk in range(2):
                    k = 2 * kp + kk
                    x_hi, x_lo = m.xh[:, k, t * P:t * P + n], m.xl[:, k, t * P:t * P + n]
                    w_hi, w_lo = m.wh[:, s, kk * 512:kk * 512 + 512], m.wl[:, s, kk * 512:kk * 512 + 512]
                    mm(out, x_hi, w_hi, start=(k == 0), stop=False)
                    mm(out, x_hi, w_lo, start=False, stop=False)
                    last = mm(out, x_lo, w_hi, start=False, stop=(k == 7))
                if kp == 3 and t < 4:
                    last.then_inc(S.v_done, 1)
            last.then_inc(S.gemm_done, 1)

    pe.wait_ge(S.x_lo, 8 * 3)
    v_block(0)
    with pe.Fori(1, 4) as b:
        v_block(b)

    pe.wait_ge(S.v_gelu, 5 * 3 + 4)
    with pe.Fori(0, 8) as i:
        for j in range(2):
            u = U_U + j
            unit(2 * i + u, u % 2, i + slot_turn(u), m.xh, m.xl)
            pe.wait_ge(S.wsm_ready, i + 1)
            pe.wait_ge(S.vm_ready, 2 * i + (j + 1))
            for t in range(4):
                mm(m.ps[:, 4 + 2 * j, t * BLK:(t + 1) * BLK], m.vm[:, j, t, :], m.wsm[:, :], start=True, stop=True)
            mm(m.ps[:, 5 + 2 * j, 0:TS], m.vm[0:TS, j, 4, :], m.wsm[0:TS, 0:TS],
               start=True, stop=True).then_inc(S.mix_done, 1)
    for c in range(2):
        pe.wait_ge(S.uv_lo, 8 * c + 8)
        run(U_CMOUT + 8 * c, 4, m.hh[:, 8 * c:8 * c + 8], m.hl[:, 8 * c:8 * c + 8])
    layer_norm_sums(2)
    ffn(1, U_FFN1)
    layer_norm_sums(3)



def scalar_program(act, m, A):
    S = m.sem
    f = act.activation

    act.dma_start(m.pv[:, :], A["pv"]).then_inc(S.pv_in, 16)
    act.dma_start(m.chalo[:, :, :, :], A["conv_halo"]).then_inc(S.chalo_in, 16)
    for k in range(KT):
        act.wait_ge(m.x_in[k // 2], 16)
        f(m.xh[:, k], m.xr[:, k], ACT.Copy).then_inc(S.x_hi, 1)
    act.wait_ge(S.pv_in, 16)
    f(m.nega[:, :], m.pv[:, PV_ALOG:PV_ALOG + 1], ACT.Exp).then_inc(S.dt_act, 1)
    act.wait_ge(m.slot_evac[0], 1)
    f(m.dtt[:, 1], m.dtt[:, 0], ACT.Abs).then_inc(S.dt_act, 1)
    act.wait_ge(S.dt_act, 2)
    f(m.dtt[:, 2], m.dtt[:, 1], ACT.Exp, scale=-1.0).then_inc(S.dt_act, 1)
    act.wait_ge(S.dt_dve, 2)
    f(m.dtt[:, 4], m.dtt[:, 3], ACT.Ln).then_inc(S.dt_act, 1)

    def raw_tile(g, j, u):
        s = u % 2 if isinstance(u, int) else (U_SSD + j) % 2
        k = j % 2
        act.wait_ge(S.gemm_done, u + 1)
        wait(act, S.conv_tap, 16 * g + 4 * (j - 1))
        r = m.raw[:, k]
        halo = m.chalo[:, g, j] if isinstance(g, int) else m.chalo[:, bass.ds(g, 1), j].rearrange("p a c -> p (a c)")
        f(r[:, HALO + TP:2 * HALO + TP], halo, ACT.Copy)
        f(r[:, HALO:HALO + HT], m.ps[:, 2 * s, 0:HT], ACT.Copy)
        f(r[:, HALO + HT:HALO + TP], m.ps[:, 2 * s + 1, 0:TP - HT], ACT.Copy)
        f(r[:, 2 * HALO + TP:RAW], m.ps[:, 2 * s + 1, TP - HT:HT], ACT.Copy).then_inc(m.slot_evac[s], 1)

    def silu_z(g, j, u):
        s = (U_SSD + 4 + j) % 2
        act.wait_ge(S.gemm_done, u + 1)
        wait(act, S.gate_ready, g)
        f(halves(m.zs[:, j]), bank_pair(m, s), ACT.Silu).then_inc(m.slot_evac[s], 1)

    def silu_conv(g):
        wait(act, S.h_ready, 5 * g)
        for b in range(2):
            act.wait_ge(S.conv_tap, 16 * g + (8 * b + 8))
            f(m.act[:, 2 * b:2 * b + 2, 0:TP], m.acc[:, 2 * b:2 * b + 2, 0:TP], ACT.Silu).then_inc(S.silu_ready, 1)
            f(m.act[:, 2 * b:2 * b + 2, TP:T], m.acc[:, 2 * b:2 * b + 2, TP + HALO:CONV],
              ACT.Silu).then_inc(S.silu_ready, 1)

    def load_group(g):
        rows = A["acum"][4 * g:4 * g + 4] if isinstance(g, int) else A["acum"][bass.ds(4 * g, 4)]
        wait(act, S.dec_sub, 5 * g)
        wait(act, S.ea_ready, 4 * g)
        act.dma_start(m.acb[:, :, :], rows.unsqueeze(0).to_broadcast([P, HPG, T])).then_inc(S.acb_in, 16)
        wait(act, S.h_ready, 5 * g - 3)
        src = A["ssm_in"][:, bass.ds(HPG * HD * g, HPG * HD)] if not isinstance(g, int) else \
            A["ssm_in"][:, HPG * HD * g:HPG * HD * (g + 1)]
        act.dma_start(m.hs[:, :], src).then_inc(S.hs_in, 16)

    def exp_acum(g, n):
        t0, q = cols(n)
        act.wait_ge(S.acb_in, 16 * g + 16)
        wait(act, S.h_ready, 5 * g + {1: 0, 2: 0, 3: 2, 4: 3}[n])
        f(m.ea[:, n % 2, :, 0:q], m.acb[:, :, t0:t0 + q], ACT.Exp).then_inc(S.ea_ready, 1)

    def exp_win(g):
        act.wait_ge(S.win_arg, 2 * g + 2)
        f(m.win[:, :, :], m.win[:, :, :], ACT.Exp).then_inc(S.win_exp, 1)

    def exp_decay(g, n):
        q = cols(n)[1]
        act.wait_ge(S.dec_arg, 5 * g + (n + 1))
        f(m.dec[0:q, n % 2, :, 0:q], m.dec[0:q, n % 2, :, 0:q], ACT.Exp).then_inc(S.dec_exp, 1)

    def rms(g):
        act.wait_ge(S.ms_done, g + 1)
        wait(act, S.yn_f, 2 * g)
        f(halves(m.rms[:, :]), m.ps[:, 4:6, 0:HT], ACT.Ln, bias=m.eps[:, :], scale=1.0 / (HPG * HD)).then_inc(S.ms_ln, 1)
        act.wait_ge(S.ms_ln, g + 1)
        f(m.rms[:, :], m.rms[:, :], ACT.Exp, scale=-0.5).then_inc(S.rms_ready, 1)

    act.wait_ge(S.x_lo, KT)
    act.wait_ge(S.chalo_in, 16)
    for j in range(4):
        raw_tile(0, j, U_SSD + j)
    act.wait_ge(S.dt_dve, DT_ACUM)
    act.dma_start(A["acum"], m.dtt[32:64, DT_OUT, :]).then_inc(S.acum_out, 16)
    act.wait_ge(S.acum_out, 16)
    load_group(0)
    act.wait_ge(S.consts, 6)
    exp_acum(0, 1)
    exp_acum(0, 2)
    exp_win(0)
    silu_z(0, 0, U_SSD + 4)
    act.wait_ge(S.tok_t, 1)
    silu_conv(0)
    silu_z(0, 1, U_SSD + 5)

    def group(g, more):
        exp_decay(g, 0)
        exp_decay(g, 1)
        if more:
            raw_tile(g + 1, 0, 6 * g + (U_SSD + 6))
        exp_decay(g, 2)
        exp_acum(g, 3)
        if more:
            raw_tile(g + 1, 1, 6 * g + (U_SSD + 7))
        exp_decay(g, 3)
        exp_acum(g, 4)
        if more:
            raw_tile(g + 1, 2, 6 * g + (U_SSD + 8))
        exp_decay(g, 4)
        if more:
            load_group(g + 1)
        dst = A["ssm_s"][:, bass.ds(HPG * HD * g, HPG * HD)] if not isinstance(g, int) else \
            A["ssm_s"][:, HPG * HD * g:HPG * HD * (g + 1)]
        act.wait_ge(S.h_ready, 5 * g + 2)
        act.dma_start(dst, m.hsn[:, :]).then_inc(S.hs_out, 16)
        if more:
            raw_tile(g + 1, 3, 6 * g + (U_SSD + 9))
        dst = A["ssm_p"][:, bass.ds(HPG * HD * g, HPG * HD)] if not isinstance(g, int) else \
            A["ssm_p"][:, HPG * HD * g:HPG * HD * (g + 1)]
        act.wait_ge(S.h_ready, 5 * g + 5)
        act.dma_start(dst, m.hp[:, :]).then_inc(S.hp_out, 16)
        act.wait_ge(S.gate_ready, g + 1)
        wait(act, S.ms_done, g)
        f(m.sq[:, :, :], m.y[:, :, :], ACT.Square).then_inc(S.sq_ready, 1)
        if more:
            exp_acum(g + 1, 1)
            exp_acum(g + 1, 2)
            exp_win(g + 1)
            rms(g)
            silu_z(g + 1, 0, 6 * g + (U_SSD + 10))
            silu_conv(g + 1)
            silu_z(g + 1, 1, 6 * g + (U_SSD + 11))

    group(0, True)
    with act.Fori(1, GROUPS - 1) as g:
        group(g, True)
    group(GROUPS - 1, False)
    rms(GROUPS - 1)
    act.wait_ge(S.ctail_ready, 2 * 4 * GROUPS)
    act.dma_start(A["conv_tail"], m.ctail[:, :, :, :, :]).then_inc(S.tail_out, 16)

    def squares(n, u0):
        with act.Fori(0, KT // 2) as i:
            for j in range(2):
                s = (u0 + j) % 2
                act.wait_ge(m.slot_evac[s], i + (slot_turn(u0 + j) + 1))
                act.wait_ge(S.stat_zero, 2 * n + 2)
                if n > 0:
                    act.wait_ge(S.sum2_ready, 2 * i + (8 * n + j - 1))
                f(m.sqm[:, j], one(m.r, 2 * i + j), ACT.Square).then_inc(S.sqr_ready, 1)

    def layer_norm(n):
        act.wait_ge(S.stat_done, n + 1)
        f(halves(m.msq[:, :]), m.ps[:, 4:6, 0:HT], ACT.Square, scale=1.0 / D).then_inc(S.msq_ready, 1)
        act.wait_ge(S.var_ready, 2 * n + 2)
        f(m.msq[:, :], m.msq[:, :], ACT.Ln, bias=m.eps[:, :]).then_inc(S.var_ln, 1)
        act.wait_ge(S.var_ln, n + 1)
        f(m.rstd[:, :], m.msq[:, :], ACT.Exp, scale=-0.5).then_inc(S.rstd_ready, 1)
        with act.Fori(0, KT // 2) as i:
            for j in range(2):
                act.wait_ge(S.nrm_b, 2 * i + (8 * n + j + 1))
                gain = m.pv[:, bass.ds(2 * i + (PV_LN + 16 * n + j), 1)]
                bias = m.pv[:, bass.ds(2 * i + (PV_LN + 16 * n + 8 + j), 1)]
                out = m.xf[:, j] if n < 3 else one(m.r, 2 * i + j)
                f(out, m.na[:, j], ACT.Identity, bias=bias, scale=gain).then_inc(S.nrm_x, 1)
                if n < 3:
                    act.wait_ge(S.nrm_x, 2 * i + (8 * n + j + 1))
                    f(one(m.xh, 2 * i + j), m.xf[:, j], ACT.Copy).then_inc(S.x_round, 1)

    def ffn(layer, u0):
        for b, (kind, c) in enumerate(FFN_BLOCKS):
            if kind == "up":
                with act.Fori(0, 4) as i:
                    for j in range(2):
                        u = u0 + 8 * b + j
                        before = 32 * layer + 8 * c + j
                        act.wait_ge(S.gemm_done, 2 * i + (u + 1))
                        if before >= 2:
                            act.wait_ge(S.hid_ready, 2 * i + (before - 1))
                        f(halves(m.rl[:, j]), bank_pair(m, u % 2), ACT.Relu).then_inc(m.slot_evac[u % 2], 1)
                        act.wait_ge(S.hid_ready, 2 * i + (before + 1))
                        f(one(m.hh, 2 * i + (8 * (c % 2) + j)), m.hq[:, j], ACT.Copy).then_inc(S.hid_hi, 1)
            elif c == 3:
                squares(2 * layer + 1, u0 + 8 * b)

    act.wait_ge(S.tail_out, 16)
    squares(0, U_WOUT + 8)
    layer_norm(0)
    ffn(0, U_FFN0)
    act.wait_ge(S.gemm_done, U_V)
    act.dma_start(m.bb[:, :], A["bias_v"].to_broadcast([P, CMW])).then_inc(S.bb_in, 16)
    layer_norm(1)
    act.wait_ge(S.x_lo, 24)
    act.dma_start(m.gam[:, :], A["ln_gain"].to_broadcast([P, CMW])).then_inc(S.gam_in, 16)
    act.dma_start(m.bet[:, :], A["ln_bias"].to_broadcast([P, CMW])).then_inc(S.bet_in, 16)
    act.dma_start(m.wst[:, :, :], A["w_spatial"]).then_inc(S.ws_in, 16)
    act.dma_start(m.bsb[:, :, :], A["b_spatial"].to_broadcast([P, 8 * BLK]).rearrange("p (g t) -> p g t", g=8)
                  ).then_inc(S.bs_in, 16)
    act.wait_ge(S.v_zero, 4)
    for part, place in ((0, "v1"), (1, "v2")):
        with act.Fori(0, 2) as i:
            for t in range(NTOK):
                n = TS if t == 4 else P
                act.wait_ge(S.v_bias, 5 * i + (10 * part + t + 1))
                if part == 0:
                    dst = m.v1[0:n, bass.ds(4 * i, 4), t, :]
                else:
                    dst = m.v2[0:n, bass.ds(i, 1), 8 * T:8 * T + 4 * NTOK * P].rearrange(
                        "p a (m t c) -> p (a m) t c", t=NTOK, c=P)[:, :, t, :]
                f(dst, m.ps[0:n, t, :].rearrange("p (m c) -> p m c", c=P), ACT.Gelu_apprx_tanh).then_inc(S.v_gelu, 1)
    act.wait_ge(S.v_mv, NTOK)
    f(m.vrs[:, :, :], m.vmv[:, :, 1:2], ACT.Ln, bias=m.eps[:, :]).then_inc(S.v_ln, 1)
    act.wait_ge(S.v_ln, 1)
    f(m.vrs[:, :, :], m.vrs[:, :, :], ACT.Exp, scale=-0.5).then_inc(S.v_rs, 1)

    def u_tile(i, j):
        u = U_U + j
        act.wait_ge(S.vm_ready, 2 * i + (j + 1))
        act.dma_start(A["v_rows"][:, bass.ds(2 * i + j, 1)].rearrange("p a c -> p (a c)") if not isinstance(i, int)
                      else A["v_rows"][:, 2 * i + j], m.vm[0:TS, j, 4, :]).then_inc(m.vrow_out[j], 16)
        act.wait_ge(S.gemm_done, 2 * i + (u + 1))
        wait(act, S.uv_ready, 2 * i + (j - 1))
        bias = m.pv[:, bass.ds(2 * i + (PV_BU + j), 1)] if not isinstance(i, int) else m.pv[:, PV_BU + j:PV_BU + j + 1]
        f(halves(m.ug[:, j]), bank_pair(m, u % 2), ACT.Gelu_apprx_tanh, bias=bias).then_inc(m.slot_evac[u % 2], 1)
        act.wait_ge(S.uv_ready, 2 * i + (j + 1))
        f(one(m.hh, 2 * i + j), m.sb[:, j], ACT.Copy).then_inc(S.uv_hi, 1)

    u_tile(0, 0)
    u_tile(0, 1)
    with act.Fori(1, 8) as i:
        u_tile(i, 0)
        u_tile(i, 1)
    squares(2, U_CMOUT + 8)
    layer_norm(2)
    ffn(1, U_FFN1)
    layer_norm(3)



def vector_program(dve, m, A):
    S = m.sem
    tt, ts, stt, cp = dve.tensor_tensor, dve.tensor_scalar, dve.scalar_tensor_tensor, dve.tensor_copy

    for k in range(KT):
        dve.wait_ge(S.x_hi, k + 1)
        tt(m.xl[:, k], m.xr[:, k], m.xh[:, k], ALU.subtract).then_inc(S.x_lo, 1)
    dve.wait_ge(S.x_lo, KT)
    dve.memset(m.raw[:, :, 0:HALO], 0.0).then_inc(S.raw_zero, 1)

    d = m.dtt
    dve.wait_ge(S.pv_in, 16)
    dve.wait_ge(S.dt_act, 1)
    ts(m.nega[:, :], m.nega[:, :], -1.0, None, ALU.mult).then_inc(S.dt_dve, 1)
    dve.wait_ge(S.gemm_done, 1)
    ts(halves(d[:, 0]), bank_pair(m, 0), m.pv[:, PV_DTB:PV_DTB + 1], None, ALU.add).then_inc(m.slot_evac[0], 1)
    dve.wait_ge(S.dt_act, 3)
    ts(d[:, 3], d[:, 2], 1.0, None, ALU.add).then_inc(S.dt_dve, 1)
    dve.wait_ge(S.dt_dve, 2)
    ts(d[:, 5], d[:, 3], 1.0, None, ALU.subtract).then_inc(S.dt_dve, 1)
    dve.reciprocal(d[:, 6], d[:, 3]).then_inc(S.dt_dve, 1)
    dve.wait_ge(S.dt_dve, 4)
    tt(d[:, 5], d[:, 2], d[:, 5], ALU.subtract).then_inc(S.dt_dve, 1)
    dve.wait_ge(S.dt_dve, 5)
    tt(d[:, 5], d[:, 5], d[:, 6], ALU.mult).then_inc(S.dt_dve, 1)
    dve.wait_ge(S.dt_dve, 6)
    dve.wait_ge(S.dt_act, 4)
    stt(d[:, 1], d[:, 0], 0.0, d[:, 5], ALU.max, ALU.add).then_inc(S.dt_dve, 1)
    dve.wait_ge(S.dt_dve, 7)
    tt(d[:, 1], d[:, 1], d[:, 4], ALU.add).then_inc(S.dt_dve, 1)
    dve.wait_ge(S.dt_dve, 8)
    ts(d[:, 2], d[:, 1], m.nega[:, :], None, ALU.mult).then_inc(S.dt_dve, 1)
    dve.wait_ge(S.dt_dve, 9)
    dve.wait_ge(S.consts, 6)
    for c in range(NCH):
        q = TS if c == 4 else Q
        dve.tensor_tensor_scan(d[:, DT_OUT, c * Q:c * Q + q], m.ones[:, 0:q], d[:, 2, c * Q:c * Q + q],
                               0.0, ALU.mult, ALU.add).then_inc(S.dt_dve, 1)
    dve.wait_ge(S.dt_dve, DT_ACUM)
    cp(d[0:32, DT_OUT, :], d[0:32, 1, :]).then_inc(S.dt_dve, 1)

    def conv_params(g):
        a = 20 * g + PV_CONV
        src = m.pv[:, a:a + 20] if isinstance(g, int) else m.pv[:, bass.ds(a, 20)]
        wait(dve, S.conv_tap, 16 * g)
        cp(m.cpar[:, :, :].rearrange("p a b -> p (a b)"), src).then_inc(S.cpar_ready, 1)

    def conv(g, j):
        s = (U_SSD + j) % 2
        u = U_SSD + j
        r, a = m.raw[:, j % 2], m.acc[:, j]
        turn = slot_turn(u)
        dve.wait_ge(m.slot_evac[s], 3 * g + (turn + 1))
        dve.wait_ge(S.cpar_ready, g + 1)
        for b, at in enumerate((TP, RAW - HALO)):
            dst = m.ctail[:, g, j, b] if isinstance(g, int) else \
                m.ctail[:, bass.ds(g, 1), j, b].rearrange("p a c -> p (a c)")
            cp(dst, r[:, at:at + HALO]).then_inc(S.ctail_ready, 1)
        if j == 0:
            wait(dve, S.silu_ready, 4 * g)
            dve.wait_ge(S.raw_zero, 1)
        ts(a, r[:, 0:CONV], m.cpar[:, j, 0:1], m.cpar[:, j, 4:5], ALU.mult, ALU.add).then_inc(S.conv_tap, 1)
        for k in range(1, 4):
            dve.wait_ge(S.conv_tap, 16 * g + (4 * j + k))
            stt(a, r[:, k:k + CONV], m.cpar[:, j, k:k + 1], a, ALU.mult, ALU.add).then_inc(S.conv_tap, 1)

    def group_columns(g):
        dve.wait_ge(S.tokd_ready, 2)
        for dst, at in ((m.gdt, 0), (m.gac, HEADS)):
            src = m.tokd[:, :, at + 4 * g:at + 4 * g + 4] if isinstance(g, int) else \
                m.tokd[:, :, bass.ds(4 * g + at, 4)]
            wait(dve, S.m_ready, 5 * g)
            cp(dst[:, :, :], src).then_inc(S.gdt_ready, 1)
        dve.wait_ge(S.gdt_ready, 2 * g + 2)
        dve.wait_ge(S.acb_in, 16 * g + 16)
        last = m.acb[:, :, 0:TP].rearrange("p h (c q) -> p c h q", q=Q)[:, :, :, Q - 1]
        tt(m.win[:, 0:4, :], last, m.gac[:, 0:4, :], ALU.subtract).then_inc(S.win_arg, 1)
        tt(m.win[:, 4, :], m.acb[:, :, T - 1], m.gac[:, 4, :], ALU.subtract).then_inc(S.win_arg, 1)
        dve.wait_ge(S.win_exp, g + 1)
        tt(m.dtw[:, :, :], m.gdt[:, :, :], m.win[:, :, :], ALU.mult).then_inc(S.dtw_ready, 1)

    def skip_params(g):
        a = 4 * g + PV_GRP
        src = m.pv[:, a:a + 4] if isinstance(g, int) else m.pv[:, bass.ds(a, 4)]
        wait(dve, S.yn_f, 2 * g)
        cp(m.gpar[:, :], src).then_inc(S.gpar_ready, 1)

    conv_params(0)
    conv(0, 0)
    conv(0, 1)
    conv(0, 2)
    conv(0, 3)
    dve.wait_ge(S.tok_t, 1)
    dve.wait_ge(S.tokd_zero, 1)
    cp(m.tokd[:, 0:4, :], m.ps[:, 4, :].rearrange("p (c e) -> p c e", e=P)[:, :, 0:2 * HEADS]).then_inc(S.tokd_ready, 1)
    cp(m.tokd[0:TS, 4, :], m.ps[0:TS, 5, 0:2 * HEADS]).then_inc(S.tokd_ready, 1)
    group_columns(0)
    skip_params(0)

    def before(g, n):
        t0, q = cols(n)
        k = n % 2
        c = ORDER[n]
        dec = m.dec[0:q, k, :, 0:q]
        if n == 0:
            dve.wait_ge(S.acb_in, 16 * g + 16)
            dve.wait_ge(S.gdt_ready, 2 * g + 2)
            wait(dve, S.s_done, 5 * g)
        if n >= 2:
            dve.wait_ge(S.s_done, 5 * g + (n - 1))
        tt(dec, m.acb[0:q, :, t0:t0 + q], spread(m.gac[0:q, c, :], q), ALU.subtract).then_inc(S.dec_sub, 1)
        dve.wait_ge(S.dec_sub, 5 * g + (n + 1))
        ts(dec, dec, 0.0, None, ALU.min).then_inc(S.dec_arg, 1)
        if n > 0:
            dve.wait_ge(S.ea_ready, 4 * g + n)
            dve.wait_ge(S.silu_ready, 4 * g + 4)
            tt(m.cs[:, k, :, 0:q], repeat(m.act[:, 1, t0:t0 + q], HPG), m.ea[:, k, :, 0:q],
               ALU.mult).then_inc(S.cs_ready, 1)

    def operands(g, n):
        t0, q = cols(n)
        k = n % 2
        c = ORDER[n]
        b = m.ps[:, 4 + k, :]
        dve.wait_ge(S.s1_done, 5 * g + (n + 1))
        dve.wait_ge(S.consts, 6)
        tt(m.cbm[0:q, k, 0:q], b[0:q, 0:q], m.causal[0:q, 0:q], ALU.mult).then_inc(S.cbm_ready, 1)
        cp(m.btok[0:q, k, :], b[0:q, P:2 * P])
        xt = b[0:q, 2 * P:4 * P].rearrange("p (h d) -> p h d", d=HD)
        tt(m.xdt[0:q, k, :].rearrange("p (h d) -> p h d", d=HD), xt, spread(m.gdt[0:q, c, :], HD), ALU.mult)
        dve.wait_ge(S.dtw_ready, g + 1)
        tt(m.xw[0:q, k, :].rearrange("p (h d) -> p h d", d=HD), xt, spread(m.dtw[0:q, c, :], HD),
           ALU.mult).then_inc(S.xw_ready, 1)
        dve.wait_ge(S.dec_exp, 5 * g + (n + 1))
        dve.wait_ge(S.cbm_ready, 5 * g + (n + 1))
        dec = m.dec[0:q, k, :, 0:q]
        tt(dec, dec, repeat(m.cbm[0:q, k, 0:q], HPG), ALU.mult).then_inc(S.m_ready, 1)

    def after(g, n):
        t0, q = cols(n)
        k = n % 2
        yb = m.ps[:, 5 if n == 1 else 6, :]
        if n == 0:
            wait(dve, S.sq_ready, g)
            dve.wait_ge(S.gpar_ready, g + 1)
        dve.wait_ge(S.s_done, 5 * g + (n + 1))
        new = m.ps[:, 7, 0:HPG * HD].rearrange("p (h d) -> p h d", d=HD)
        old, out = (m.hs, m.hsn) if n == 1 else (m.hp, m.hp)
        hv = lambda x: x[:, :].rearrange("p (h d) -> p h d", d=HD)
        if n > 0:
            if n == 1:
                dve.wait_ge(S.hs_in, 16 * g + 16)
            tt(hv(m.hdec), hv(old), m.ea[:, k, :, q - 1:q].to_broadcast([P, HPG, HD]), ALU.mult
               ).then_inc(S.hdec_ready, 1)
        stt(m.y[:, 0, t0:t0 + q], m.act[:, 2, t0:t0 + q], m.gpar[:, 0:1], yb[:, 0:q], ALU.mult, ALU.add)
        stt(m.y[:, 1, t0:t0 + q], m.act[:, 3, t0:t0 + q], m.gpar[:, 1:2], yb[:, Q:Q + q], ALU.mult, ALU.add
            ).then_inc(S.y_evac, 1)
        if n > 0:
            dve.wait_ge(S.hdec_ready, 4 * g + n)
            if n == 1:
                wait(dve, S.hs_out, 16 * g)
            tt(hv(out), new, hv(m.hdec), ALU.add).then_inc(S.h_ready, 1)
        else:
            wait(dve, S.hp_out, 16 * g)
            cp(hv(out), new).then_inc(S.h_ready, 1)

    def gate(g):
        for j in range(2):
            s = (U_SSD + 4 + j) % 2
            dve.wait_ge(m.slot_evac[s], 3 * g + (slot_turn(U_SSD + 4 + j) + 1))
        dve.wait_ge(S.y_evac, 5 * g + 5)
        tt(m.y[:, :, :], m.y[:, :, :], m.zs[:, :, :], ALU.mult).then_inc(S.gate_ready, 1)

    def norm(g):
        dve.wait_ge(S.rms_ready, g + 1)
        dve.wait_ge(S.sq_ready, g + 1)
        for j in range(2):
            stt(m.y[:, j], m.y[:, j], m.gpar[:, 2 + j:3 + j], m.rms[:, :], ALU.mult, ALU.mult).then_inc(S.yn_f, 1)
        dve.wait_ge(S.yn_f, 2 * g + 2)
        at = slice(2 * g, 2 * g + 2) if isinstance(g, int) else bass.ds(2 * g, 2)
        cp(m.hh[:, at], m.y[:, :, :]).then_inc(S.yn_hi, 1)
        dve.wait_ge(S.yn_hi, g + 1)
        tt(m.hl[:, at], m.y[:, :, :], m.hh[:, at], ALU.subtract).then_inc(S.yn_lo, 1)

    def group(g, more):
        before(g, 0)
        before(g, 1)
        operands(g, 0)
        operands(g, 1)
        if more:
            conv_params(g + 1)
        before(g, 2)
        after(g, 0)
        after(g, 1)
        operands(g, 2)
        if more:
            conv(g + 1, 0)
        before(g, 3)
        after(g, 2)
        operands(g, 3)
        if more:
            conv(g + 1, 1)
        before(g, 4)
        after(g, 3)
        operands(g, 4)
        if more:
            conv(g + 1, 2)
        after(g, 4)
        gate(g)
        if more:
            conv(g + 1, 3)
            group_columns(g + 1)
            norm(g)
            skip_params(g + 1)

    group(0, True)
    with dve.Fori(1, GROUPS - 1) as g:
        group(g, True)
    group(GROUPS - 1, False)

    def residual_first(u0, i, j):
        u = u0 + j
        s = u % 2
        dve.wait_ge(S.gemm_done, 2 * i + (u + 1))
        stt(halves(m.rt[:, j]), halves(one(m.xh, 2 * i + j).bitcast(F32)), ALPHA, bank_pair(m, s), ALU.mult, ALU.add
            ).then_inc(m.slot_evac[s], 1)
        dve.wait_ge(m.slot_evac[s], i + (slot_turn(u) + 1))
        stt(one(m.r, 2 * i + j), one(m.xl, 2 * i + j).bitcast(F32), ALPHA, m.rt[:, j], ALU.mult, ALU.add
            ).then_inc(S.res_ready, 1)

    def residual_add(u0, i, j):
        u = u0 + j
        s = u % 2
        r = halves(one(m.r, 2 * i + j))
        dve.wait_ge(S.gemm_done, 2 * i + (u + 1))
        dve.wait_ge(m.slot_evac[1 - s], i + (slot_turn(u - 1) + 1))
        tt(r, bank_pair(m, s), r, ALU.add).then_inc(m.slot_evac[s], 1)

    def block(u0, kind, n=0):
        if kind == "first":
            with dve.Fori(0, 4) as i:
                residual_first(u0, i, 0)
                residual_first(u0, i, 1)
        elif kind == "add":
            dve.wait_ge(S.res_ready, 8 * (n + 1))
            with dve.Fori(0, 4) as i:
                residual_add(u0, i, 0)
                residual_add(u0, i, 1)
        else:
            dve.wait_ge(S.res_ready, 8 * (n + 1))
            dve.memset(m.s1[:, :], 0.0).then_inc(S.stat_zero, 1)
            dve.memset(m.s2[:, :], 0.0).then_inc(S.stat_zero, 1)
            dve.wait_ge(S.stat_zero, 2 * n + 2)
            with dve.Fori(0, 4) as i:
                for j in range(2):
                    s = (u0 + j) % 2
                    residual_add(u0, i, j)
                    dve.wait_ge(m.slot_evac[s], i + (slot_turn(u0 + j) + 1))
                    if n > 0 or j > 0:
                        dve.wait_ge(S.sum1_ready, 2 * i + (8 * n + j))
                    tt(m.s1[:, :], m.s1[:, :], one(m.r, 2 * i + j), ALU.add).then_inc(S.sum1_ready, 1)
                    dve.wait_ge(S.sqr_ready, 2 * i + (8 * n + j + 1))
                    tt(m.s2[:, :], m.s2[:, :], m.sqm[:, j], ALU.add).then_inc(S.sum2_ready, 1)

    def layer_norm(n):
        dve.wait_ge(S.msq_ready, n + 1)
        stt(halves(m.msq[:, :]), m.ps[:, 6:8, 0:HT], 1.0 / D, halves(m.msq[:, :]), ALU.mult, ALU.subtract
            ).then_inc(S.var_ready, 1)
        dve.wait_ge(S.var_ready, 2 * n + 1)
        ts(m.msq[:, :], m.msq[:, :], 0.0, None, ALU.max).then_inc(S.var_ready, 1)
        dve.wait_ge(S.rstd_ready, n + 1)
        stt(halves(m.mr[:, :]), m.ps[:, 4:6, 0:HT], 1.0 / D, halves(m.rstd[:, :]), ALU.mult, ALU.mult
            ).then_inc(S.mr_ready, 1)
        dve.wait_ge(S.mr_ready, n + 1)
        with dve.Fori(0, KT // 2) as i:
            for j in range(2):
                if n > 0 or j > 0:
                    dve.wait_ge(S.nrm_x, 2 * i + (8 * n + j - 1)) if 8 * n + j - 1 > 0 else None
                tt(m.na[:, j], one(m.r, 2 * i + j), m.rstd[:, :], ALU.mult).then_inc(S.nrm_a, 1)
            for j in range(2):
                dve.wait_ge(S.nrm_a, 2 * i + (8 * n + j + 1))
                tt(m.na[:, j], m.na[:, j], m.mr[:, :], ALU.subtract).then_inc(S.nrm_b, 1)
            if n < 3:
                for j in range(2):
                    dve.wait_ge(S.x_round, 2 * i + (8 * n + j + 1))
                    tt(one(m.xl, 2 * i + j), m.xf[:, j], one(m.xh, 2 * i + j), ALU.subtract).then_inc(S.x_lo, 1)

    def ffn(layer, u0):
        for b, (kind, c) in enumerate(FFN_BLOCKS):
            if kind == "up":
                with dve.Fori(0, 4) as i:
                    for j in range(2):
                        u = u0 + 8 * b + j
                        done = 32 * layer + 8 * c + j
                        dve.wait_ge(m.slot_evac[u % 2], i + (slot_turn(u) + 1))
                        if done >= 2:
                            dve.wait_ge(S.hid_lo, 2 * i + (done - 1))
                        tt(m.hq[:, j], m.rl[:, j], m.rl[:, j], ALU.mult).then_inc(S.hid_ready, 1)
                        dve.wait_ge(S.hid_hi, 2 * i + (done + 1))
                        k = 2 * i + (8 * (c % 2) + j)
                        tt(one(m.hl, k), m.hq[:, j], one(m.hh, k), ALU.subtract).then_inc(S.hid_lo, 1)
            else:
                block(u0 + 8 * b, "first" if c == 0 else "last" if c == 3 else "add", 2 * layer + 1)

    with dve.Fori(0, 3) as i:
        residual_first(U_WOUT, i, 0)
        residual_first(U_WOUT, i, 1)
    norm(GROUPS - 1)
    with dve.Fori(3, 4) as i:
        residual_first(U_WOUT, i, 0)
        residual_first(U_WOUT, i, 1)
    block(U_WOUT + 8, "last", 0)
    layer_norm(0)
    ffn(0, U_FFN0)
    layer_norm(1)

    dve.wait_ge(S.x_lo, 24)
    dve.memset(m.v1[TS:P, :, 4, :], 0.0).then_inc(S.v_zero, 1)
    dve.wait_ge(S.gemm_done, U_V)
    v2 = m.v2[TS:P, :, 8 * T:8 * T + 4 * NTOK * P].rearrange("p a (m t c) -> p a m t c", t=NTOK, c=P)
    for a in range(2):
        dve.memset(v2[:, a, :, 4, :], 0.0).then_inc(S.v_zero, 1)
    dve.memset(m.vmv[:, :, :], 0.0).then_inc(S.v_zero, 1)
    dve.wait_ge(S.bb_in, 16)

    def v_bias(b, t):
        n = TS if t == 4 else P
        if t < 4:
            dve.wait_ge(S.v_done, 4 * b + (t + 1))
        else:
            dve.wait_ge(S.gemm_done, 4 * b + (U_V + 4))
        bank = m.ps[0:n, t, :]
        row = m.bb[0:n, bass.ds(512 * b, 512)] if not isinstance(b, int) else m.bb[0:n, 512 * b:512 * (b + 1)]
        tt(bank, bank, row, ALU.add).then_inc(S.v_bias, 1)

    for part in range(2):
        with dve.Fori(0, 2) as i:
            for t in range(NTOK):
                v_bias(i + 2 * part, t)
                if t > 0:
                    v_stats(dve, m, part, i, t - 1)
            v_stats(dve, m, part, i, NTOK - 1)
    dve.wait_ge(S.v_stat, 20)
    dve.wait_ge(S.v_zero, 4)
    for t in range(NTOK):
        n = TS if t == 4 else P
        dve.bn_aggr(m.vmv[0:n, t, :], m.vst[0:n, t, :, :].rearrange("p a b -> p (a b)")).then_inc(S.v_mv, 1)
    dve.wait_ge(S.v_rs, 1)
    dve.wait_ge(S.v_mv, NTOK)
    dve.wait_ge(S.gam_in, 16)
    dve.wait_ge(S.bet_in, 16)
    dve.wait_ge(S.bs_in, 16)

    def norm_v(k, kv, j):
        if not isinstance(k, int):
            dve.wait_ge(m.vrow_out[j], 8 * (k - j))
        for t in range(NTOK):
            src = m.v1[:, kv, t, :] if isinstance(kv, int) else m.v1[:, bass.ds(kv, 1), t, :].rearrange("p a c -> p (a c)")
            o = ts(m.vm[:, j, t, :], src, m.vmv[:, t, 0:1], m.vrs[:, t, 0:1], ALU.subtract, ALU.mult)
        o.then_inc(S.vm_n, 1)
        cut = (lambda x: x[:, k * P:(k + 1) * P]) if isinstance(k, int) else (lambda x: x[:, bass.ds(P * k, P)])
        dve.wait_ge(S.vm_n, k + 1)
        tt(m.vm[:, j], m.vm[:, j], repeat(cut(m.gam), NTOK), ALU.mult).then_inc(S.vm_g, 1)
        dve.wait_ge(S.vm_g, k + 1)
        tt(m.vm[:, j], m.vm[:, j], repeat(cut(m.bet), NTOK), ALU.add).then_inc(S.vm_ready, 1)

    def spatial_weights(g):
        cp(m.wsm[:, :], m.wst[:, g, :] if isinstance(g, int) else m.wst[:, bass.ds(g, 1), :].rearrange("p a c -> p (a c)")
           ).then_inc(S.wsm_ready, 1)

    def mix(i, j):
        row = m.bsb[:, bass.ds(i, 1), :].rearrange("p a c -> p (a c)") if not isinstance(i, int) else m.bsb[:, i, :]
        u = U_U + j
        dve.wait_ge(S.mix_done, 2 * i + (j + 1))
        tt(m.sb[:, j, 0:TP].rearrange("p (n t) -> p n t", t=BLK),
           m.ps[:, 4 + 2 * j, :].rearrange("p (n t) -> p n t", t=BLK), repeat(row, 4), ALU.add).then_inc(S.s_bias, 1)
        tt(m.sb[:, j, TP:T], m.ps[:, 5 + 2 * j, 0:TS], row[:, 0:TS], ALU.add).then_inc(S.s_bias, 1)
        dve.wait_ge(S.s_bias, 4 * i + (2 * j + 2))
        dve.wait_ge(m.slot_evac[u % 2], i + (slot_turn(u) + 1))
        tt(m.sb[:, j], m.sb[:, j], m.ug[:, j], ALU.mult).then_inc(S.uv_ready, 1)
        dve.wait_ge(S.uv_hi, 2 * i + (j + 1))
        k = 2 * i + j
        tt(one(m.hl, k), m.sb[:, j], one(m.hh, k), ALU.subtract).then_inc(S.uv_lo, 1)

    dve.wait_ge(S.ws_masked, 1)
    spatial_weights(0)
    norm_v(0, 0, 0)
    norm_v(1, 1, 1)
    with dve.Fori(0, 3) as i:
        mix(i, 0)
        norm_v(2 * i + 2, 2 * i + 2, 0)
        mix(i, 1)
        spatial_weights(i + 1)
        norm_v(2 * i + 3, 2 * i + 3, 1)
    dve.wait_ge(S.vm_ready, 8)
    for a in range(2):
        cp(m.v1[:, 4 * a:4 * a + 4].rearrange("p m t c -> p (m t c)"), m.v2[:, a, 8 * T:8 * T + 4 * NTOK * P]
           ).then_inc(S.v_moved, 1)
    dve.wait_ge(S.v_moved, 2)
    with dve.Fori(3, 7) as i:
        mix(i, 0)
        norm_v(2 * i + 2, 2 * i - 6, 0)
        mix(i, 1)
        spatial_weights(i + 1)
        norm_v(2 * i + 3, 2 * i - 5, 1)
    mix(7, 0)
    mix(7, 1)
    block(U_CMOUT, "first")
    block(U_CMOUT + 8, "last", 2)
    layer_norm(2)
    ffn(1, U_FFN1)
    layer_norm(3)


def v_stats(dve, m, part, i, t):
    S = m.sem
    n = TS if t == 4 else P
    dve.wait_ge(S.v_gelu, 5 * i + (10 * part + t + 1))
    if part == 0:
        src = m.v1[0:n, bass.ds(4 * i, 4), t, :]
    else:
        src = m.v2[0:n, bass.ds(i, 1), 8 * T:8 * T + 4 * NTOK * P].rearrange(
            "p a (m t c) -> p (a m) t c", t=NTOK, c=P)[:, :, t, :]
    dst = m.vst[0:n, t, bass.ds(i + 2 * part, 1), :].rearrange("p a b -> p (a b)")
    dve.bn_stats(dst, src).then_inc(S.v_stat, 1)



def encoder_program(nc, A):
    with ExitStack() as ctx:
        m = Memory(nc, ctx)
        A = dict(A, acum=m.acum_dram)
        block = ctx.enter_context(nc.Block())

        @block.sync
        def _(eng):
            sync_program(eng, m, A)

        @block.gpsimd
        def _(eng):
            pool_program(eng, m, A)

        @block.scalar
        def _(eng):
            scalar_program(eng, m, A)

        @block.tensor
        def _(eng):
            tensor_program(eng, m, A)

        @block.vector
        def _(eng):
            vector_program(eng, m, A)



def stream_units(w):
    k, n = w.shape
    return w.reshape(k // UNIT, KT, P, n // P, P).transpose(0, 3, 2, 1, 4).reshape(-1, P, UNIT)


def tiles(v):
    return v.reshape(v.shape[:-1] + (-1, P)).transpose((len(v.shape),) + tuple(range(len(v.shape))))


def kernel(x_prompt, x_sample, state_ssm, state_conv, ssd_w_in, ssd_conv_w, ssd_conv_b, ssd_dt_bias, ssd_a_log, ssd_d,
           ssd_norm_w, ssd_w_out, cm_w_in, cm_b_in, cm_ln_g, cm_ln_b, cm_w_s, cm_b_s, cm_w_out, ffn_w1, ffn_w2,
           ln1_g, ln1_b, ln2_g, ln2_b):
    import numpy as np
    import concourse.bacc as bacc
    from concourse.bass_utils import run_bass_kernel_spmd

    f = np.ascontiguousarray
    di = 2 * D
    w_in = ssd_w_in[0]
    z, x, b, c = (stream_units(w_in[:, at:at + n]) for at, n in
                  ((0, di), (di, di), (2 * di, GROUPS * NST), (2 * di + GROUPS * NST, GROUPS * NST)))
    dt = stream_units(np.concatenate([w_in[:, -HEADS:]] * 4, axis=1))
    parts = [dt]
    for g in range(GROUPS):
        parts += [b[g:g + 1], c[g:g + 1], x[2 * g:2 * g + 2], z[2 * g:2 * g + 2]]
    parts.append(stream_units(ssd_w_out[0]))

    def ffn(layer):
        up, down = stream_units(ffn_w1[layer]), stream_units(ffn_w2[layer])
        return [(up if kind == "up" else down)[8 * k:8 * k + 8] for kind, k in FFN_BLOCKS]

    parts += ffn(0)
    v = cm_w_in[0][:, CMW:]
    parts.append(v.reshape(4, 2, P, 4, 512).transpose(3, 0, 2, 1, 4).reshape(16, P, UNIT))
    parts.append(stream_units(cm_w_in[0][:, :CMW]))
    parts.append(stream_units(cm_w_out[0]))
    parts += ffn(1)
    wstream = f(np.concatenate(parts))

    conv = np.concatenate([ssd_conv_w[0], ssd_conv_b], axis=0)
    by_tile = tiles(conv).transpose(0, 2, 1)
    conv_g = np.stack([by_tile[:, [16 + g, 24 + g, 2 * g, 2 * g + 1]] for g in range(GROUPS)], axis=1)
    skip = tiles(np.repeat(ssd_d[0], HD))
    grp = np.concatenate([skip.reshape(P, GROUPS, 2), tiles(ssd_norm_w[0]).reshape(P, GROUPS, 2)], axis=2)
    lns = np.stack([np.concatenate([tiles(a[i]), tiles(q[i])], axis=1)
                    for i in range(2) for a, q in ((ln1_g, ln1_b), (ln2_g, ln2_b))], axis=1)
    pv = f(np.concatenate([
        conv_g.reshape(P, -1), grp.reshape(P, -1), tiles(cm_b_in[0, :CMW]), lns.reshape(P, -1),
        np.concatenate([ssd_dt_bias[0]] * 4)[:, None], np.concatenate([ssd_a_log[0]] * 4)[:, None]], axis=1))
    assert pv.shape == (P, PV_N)

    halo = tiles(state_conv[0, 0]).transpose(0, 2, 1)
    halo = np.stack([halo[:, [16 + g, 24 + g, 2 * g, 2 * g + 1]] for g in range(GROUPS)], axis=1)
    xt = np.concatenate([x_prompt[0], x_sample[0]], axis=0)
    arrays = {
        "wstream": wstream,
        "x": f(xt.T.reshape(KT, P, T).transpose(1, 0, 2)),
        "pv": pv,
        "conv_halo": f(halo),
        "ssm_in": f(state_ssm[0, 0].transpose(2, 0, 1).reshape(NST, HEADS * HD)),
        "bias_v": f(cm_b_in[:, CMW:]),
        "ln_gain": f(cm_ln_g),
        "ln_bias": f(cm_ln_b),
        "w_spatial": f(cm_w_s[0].transpose(2, 0, 1)),
        "b_spatial": f(cm_b_s[0].reshape(1, -1)),
    }
    outs = {
        "y": (P, KT, T), "ssm_p": (NST, HEADS * HD), "ssm_s": (NST, HEADS * HD),
        "conv_tail": (P, GROUPS, 4, 2, HALO), "v_rows": (TS, 16, P),
    }
    nc = bacc.Bacc("TRN2", target_bir_lowering=False, num_devices=1)
    A = {n: nc.dram_tensor(n, a.shape, mybir.dt.from_np(a.dtype), kind="ExternalInput").ap() for n, a in arrays.items()}
    A.update({n: nc.dram_tensor("out_" + n, s, F32, kind="ExternalOutput").ap() for n, s in outs.items()})
    encoder_program(nc, A)
    got = run_bass_kernel_spmd(nc, [arrays], core_ids=[0]).results[0]

    y = got["out_y"].transpose(1, 0, 2).reshape(D, T).T
    tail = got["out_conv_tail"]
    rows = tail.transpose(3, 4, 1, 2, 0)
    xs = rows[:, :, :, 2:4].reshape(2, HALO, di)
    bs = rows[:, :, :, 0].reshape(2, HALO, -1)
    cs = rows[:, :, :, 1].reshape(2, HALO, -1)
    new_rows = np.concatenate([xs, bs, cs], axis=2)
    ssm = [got[n].reshape(NST, HEADS, HD).transpose(1, 2, 0)[None, None] for n in ("out_ssm_p", "out_ssm_s")]
    return (f(y[None, :TP]), f(y[None, TP:]), f(ssm[0]), f(new_rows[0][None, None]), f(ssm[1]), f(new_rows[1][None, None]),
            f(got["out_v_rows"].reshape(1, 1, TS, CMW)))
```

```python
from contextlib import ExitStack

import concourse.bass as bass
from concourse import mybir

F32 = mybir.dt.float32
F32R = mybir.dt.float32r
ALU = mybir.AluOpType
ACT = mybir.ActivationFunctionType

P = 128
D = 1024
KT = D // P
TP, TS = 512, 64
T = TP + TS
HT = T // 2
UNIT = 1024
RING = 4
HALO = 3
RAW = HALO + TP + HALO + TS
CONV = RAW - HALO
GROUPS, HPG, HD, NST = 8, 4, 64, 128
HEADS = GROUPS * HPG
Q = 128
NCH = 5
ALPHA = (2 * 2) ** 0.25
EPS = 1e-5
BLK = 128
NTOK = 5
V_BANK = [0, 2, 1, 3, 4]
CMW = 2048

U_SSD = 1
U_WOUT = U_SSD + 6 * GROUPS
U_FFN0 = U_WOUT + 16
U_V = U_FFN0 + 64
U_U = U_V + 16
U_CMOUT = U_U + 16
U_FFN1 = U_CMOUT + 16
UNITS = U_FFN1 + 64

PV_CONV = 0
PV_GRP = PV_CONV + GROUPS * 20
PV_BU = PV_GRP + GROUPS * 4
PV_LN = PV_BU + 16
PV_DTB = PV_LN + 4 * 16
PV_ALOG = PV_DTB + 1
PV_N = PV_ALOG + 1

DT_OUT = 7
DT_ACUM = 14
DT_STEPS = 15

ORDER = [0, 4, 1, 2, 3]


def cols(n):
    c = ORDER[n]
    return c * Q, (TS if c == 4 else Q)


def slot_turn(u):
    return (u if u < U_V else u - 16) // 2


FFN_BLOCKS = [("up", 0), ("up", 1), ("down", 0), ("up", 2), ("down", 1), ("up", 3), ("down", 2), ("down", 3)]


class Semaphores:

    def __init__(self, sem):
        self.tick_zero = sem("tick_zero")
        self.w_in0 = sem("w_in0")
        self.w_in1 = sem("w_in1")
        self.w_in2 = sem("w_in2")
        self.w_in3 = sem("w_in3")
        self.w_hi = sem("w_hi")
        self.w_ready = sem("w_ready")
        self.gemm_done = sem("gemm_done")
        self.slot_evac0 = sem("slot_evac0")
        self.slot_evac1 = sem("slot_evac1")
        self.x_in0 = sem("x_in0")
        self.x_in1 = sem("x_in1")
        self.x_in2 = sem("x_in2")
        self.x_in3 = sem("x_in3")
        self.pv_in = sem("pv_in")
        self.chalo_in = sem("chalo_in")
        self.x_hi = sem("x_hi")
        self.x_lo = sem("x_lo")
        self.consts = sem("consts")
        self.tokd_zero = sem("tokd_zero")
        self.raw_zero = sem("raw_zero")
        self.dt_act = sem("dt_act")
        self.dt_dve = sem("dt_dve")
        self.tok_t = sem("tok_t")
        self.tokd_ready = sem("tokd_ready")
        self.acum_out = sem("acum_out")
        self.acb_in = sem("acb_in")
        self.hs_in = sem("hs_in")
        self.hs_out = sem("hs_out")
        self.hp_out = sem("hp_out")
        self.cpar_ready = sem("cpar_ready")
        self.gdt_ready = sem("gdt_ready")
        self.gpar_ready = sem("gpar_ready")
        self.win_arg = sem("win_arg")
        self.win_exp = sem("win_exp")
        self.dtw_ready = sem("dtw_ready")
        self.conv_tap = sem("conv_tap")
        self.silu_ready = sem("silu_ready")
        self.dec_sub = sem("dec_sub")
        self.dec_arg = sem("dec_arg")
        self.dec_exp = sem("dec_exp")
        self.ea_ready = sem("ea_ready")
        self.cs_ready = sem("cs_ready")
        self.s1_done = sem("s1_done")
        self.cbm_ready = sem("cbm_ready")
        self.xw_ready = sem("xw_ready")
        self.m_ready = sem("m_ready")
        self.s_done = sem("s_done")
        self.y_evac = sem("y_evac")
        self.hdec_ready = sem("hdec_ready")
        self.h_ready = sem("h_ready")
        self.gate_ready = sem("gate_ready")
        self.sq_ready = sem("sq_ready")
        self.ms_done = sem("ms_done")
        self.ms_ln = sem("ms_ln")
        self.rms_ready = sem("rms_ready")
        self.yn_f = sem("yn_f")
        self.yn_hi = sem("yn_hi")
        self.yn_lo = sem("yn_lo")
        self.ctail_ready = sem("ctail_ready")
        self.tail_out = sem("tail_out")
        self.hid_ready = sem("hid_ready")
        self.hid_hi = sem("hid_hi")
        self.hid_lo = sem("hid_lo")
        self.res_ready = sem("res_ready")
        self.stat_zero = sem("stat_zero")
        self.sum1_ready = sem("sum1_ready")
        self.sqr_ready = sem("sqr_ready")
        self.sum2_ready = sem("sum2_ready")
        self.stat_done = sem("stat_done")
        self.msq_ready = sem("msq_ready")
        self.var_ready = sem("var_ready")
        self.var_ln = sem("var_ln")
        self.rstd_ready = sem("rstd_ready")
        self.mr_ready = sem("mr_ready")
        self.nrm_a = sem("nrm_a")
        self.nrm_b = sem("nrm_b")
        self.nrm_x = sem("nrm_x")
        self.half_done = sem("half_done")
        self.res_half = sem("res_half")
        self.x_lo_pool = sem("x_lo_pool")
        self.y_out = sem("y_out")
        self.bb_in = sem("bb_in")
        self.gam_in = sem("gam_in")
        self.bet_in = sem("bet_in")
        self.ws_in = sem("ws_in")
        self.bs_in = sem("bs_in")
        self.ws_masked = sem("ws_masked")
        self.v_done = sem("v_done")
        self.v_bias = sem("v_bias")
        self.v_gelu = sem("v_gelu")
        self.v_stat = sem("v_stat")
        self.v_mv = sem("v_mv")
        self.v_ln = sem("v_ln")
        self.v_rs = sem("v_rs")
        self.v_zero = sem("v_zero")
        self.v_moved = sem("v_moved")
        self.wsm_ready = sem("wsm_ready")
        self.vm_n = sem("vm_n")
        self.vm_g = sem("vm_g")
        self.vm_ready = sem("vm_ready")
        self.vrow_out0 = sem("vrow_out0")
        self.vrow_out1 = sem("vrow_out1")
        self.mix_done = sem("mix_done")
        self.s_bias = sem("s_bias")
        self.uv_ready = sem("uv_ready")
        self.uv_hi = sem("uv_hi")
        self.uv_lo = sem("uv_lo")


class Memory:

    def __init__(self, nc, ctx):
        base = (nc.sbuf_base + 63) // 64 * 64
        end = nc.sbuf_usable_end
        self.at = base

        def put(name, shape, dt=F32, offset=None):
            n = 4
            for s in shape[1:]:
                n *= s
            where = self.at if offset is None else (offset + 31) // 32 * 32
            assert where + n <= end, (name, where + n - end)
            if offset is None:
                self.at += (n + 31) // 32 * 32
            return nc.alloc_sbuf_tensor_at(name, shape, dt, offset=where)

        self.xh = put("xh", [P, KT, T], F32R)
        self.xl = put("xl", [P, KT, T], F32R)
        h0 = self.at
        self.hh = put("hh", [P, 16, T], F32R)
        l0 = self.at
        self.hl = put("hl", [P, 16, T], F32R)
        w0 = self.at
        self.wraw = put("wraw", [P, RING, UNIT])
        self.wl = put("wl", [P, RING, UNIT], F32R, offset=w0)
        self.wh = put("wh", [P, RING, UNIT], F32R)
        self.pv = put("pv", [P, PV_N])
        self.ident = put("ident", [P, P])
        self.ones = put("ones", [P, P])
        self.causal = put("causal", [P, P])
        self.eps = put("eps", [P, 1])
        self.nega = put("nega", [P, 1])
        self.tick = put("tick", [P, 2])

        t0 = self.at

        self.raw = put("raw", [P, 2, RAW])
        self.acc = put("acc", [P, 4, CONV])
        self.act = put("act", [P, 4, T])
        self.zs = put("zs", [P, 2, T])
        self.acb = put("acb", [P, HPG, T])
        self.y = put("y", [P, 2, T])
        self.sq = put("sq", [P, 2, T])
        self.rms = put("rms", [P, T])
        self.ea = put("ea", [P, 2, HPG, Q])
        self.btok = put("btok", [P, 2, NST])
        self.cbm = put("cbm", [P, 2, Q])
        self.xdt = put("xdt", [P, 2, HPG * HD])
        self.xw = put("xw", [P, 2, HPG * HD])
        self.hp = put("hp", [P, HPG * HD])
        self.hs = put("hs", [P, HPG * HD])
        self.hsn = put("hsn", [P, HPG * HD])
        self.hdec = put("hdec", [P, HPG * HD])
        self.tokd = put("tokd", [P, NCH, 2 * HEADS])
        self.gdt = put("gdt", [P, NCH, HPG])
        self.gac = put("gac", [P, NCH, HPG])
        self.win = put("win", [P, NCH, HPG])
        self.dtw = put("dtw", [P, NCH, HPG])
        self.cpar = put("cpar", [P, 4, 5])
        self.gpar = put("gpar", [P, 4])
        self.ctail = put("ctail", [P, GROUPS, 4, 2, HALO])
        self.chalo = put("chalo", [P, GROUPS, 4, HALO])
        self.dec = put("dec", [P, 2, HPG, Q], offset=h0 + 14 * T * 4)
        self.cs = put("cs", [P, 2, HPG, Q], offset=l0 + 14 * T * 4)
        self.xr = put("xr", [P, KT, T], offset=t0)
        self.dtt = put("dtt", [P, 8, T], offset=t0 + 2 * RAW * 4)

        row = T * 4
        self.r = put("r", [P, KT, T], offset=t0)
        self.rl = put("rl", [P, 2, T], offset=t0 + 8 * row)
        self.hq = put("hq", [P, 2, T], offset=t0 + 10 * row)
        self.s1 = put("s1", [P, 2, HT], offset=t0 + 12 * row)
        self.s2 = put("s2", [P, 2, HT], offset=t0 + 13 * row)
        self.msq = put("msq", [P, 2, HT], offset=t0 + 14 * row)
        self.rstd = put("rstd", [P, 2, HT], offset=t0 + 15 * row)
        self.mr = put("mr", [P, 2, HT], offset=t0 + 16 * row)
        self.na = put("na", [P, 4, HT], offset=t0 + 17 * row)
        self.xf = put("xf", [P, 4, HT], offset=t0 + 19 * row)
        self.sqm = put("sqm", [P, 2, T], offset=t0 + 21 * row)

        self.gam = put("gam", [P, CMW], offset=t0)
        self.bet = put("bet", [P, CMW], offset=t0 + CMW * 4)
        g0 = t0 + 8 * row
        vrow = NTOK * P * 4
        self.v1 = put("v1", [P, 8, NTOK, P], offset=g0)
        self.v2 = put("v2", [P, 2, 16 * T], offset=h0)
        self.bb = put("bb", [P, CMW], offset=l0)
        g0 += 8 * vrow
        self.vm = put("vm", [P, 2, NTOK, P], offset=g0)
        g0 += 2 * vrow
        self.wsm = put("wsm", [P, BLK], offset=g0)
        g0 += BLK * 4
        self.wst = put("wst", [P, 8, BLK], offset=g0)
        g0 += 8 * BLK * 4
        self.bsb = put("bsb", [P, 8, BLK], offset=g0)
        g0 += 8 * BLK * 4
        self.ug = put("ug", [P, 2, T], offset=g0)
        g0 += 2 * row
        self.sb = put("sb", [P, 2, T], offset=g0)
        g0 += 2 * row
        self.vst = put("vst", [P, NTOK, 4, 6], offset=g0)
        g0 += NTOK * 4 * 6 * 4
        self.vmv = put("vmv", [P, NTOK, 2], offset=g0)
        g0 += 64
        self.vrs = put("vrs", [P, NTOK, 1], offset=g0)

        self.ps = ctx.enter_context(nc.psum_tensor("ps", [P, 8, 512], F32))
        self.acum_dram = nc.dram_tensor("acum_scratch", [HEADS, T], F32).ap()

        self.sem = S = Semaphores(lambda name: ctx.enter_context(nc.semaphore(name)))
        self.w_in = [S.w_in0, S.w_in1, S.w_in2, S.w_in3]
        self.slot_evac = [S.slot_evac0, S.slot_evac1]
        self.x_in = [S.x_in0, S.x_in1, S.x_in2, S.x_in3]
        self.vrow_out = [S.vrow_out0, S.vrow_out1]


def wait(engine, sem, value):
    if not isinstance(value, int) or value > 0:
        engine.wait_ge(sem, value)


def one(t, i):
    if isinstance(i, int):
        return t[:, i]
    v = t[:, bass.ds(i, 1)]
    if len(v.shape) == 3:
        return v.rearrange("p a t -> p (a t)")
    if len(v.shape) == 4:
        return v.rearrange("p a b t -> p (a b) t")
    return v.rearrange("p a b c t -> p (a b) c t")


def wait_x(engine, m, n, h, k):
    if h == 0 or k % 2:
        engine.wait_ge(m.sem.x_lo_pool, 12 * n + (k + 1 if h == 0 else 8 + (k + 1) // 2))
    else:
        engine.wait_ge(m.sem.x_lo, KT + 4 * n + k // 2 + 1)


def half_of(t, k, h):
    return t[:, k, h * HT:(h + 1) * HT]


def x_lo(engine, m, n, h, k):
    S = m.sem
    engine.wait_ge(S.nrm_x, 16 * n + 8 * h + k + 1)
    engine.tensor_tensor(half_of(m.xl, k, h), m.xf[:, k % 4], half_of(m.xh, k, h), ALU.subtract
                         ).then_inc(S.x_lo_pool if h == 0 or k % 2 else S.x_lo, 1)


def halves(ap):
    return ap.rearrange("p (h t) -> p h t", h=2)


def bank_pair(m, s):
    return m.ps[:, 2 * s:2 * s + 2, 0:HT]


def spread(ap, n):
    return ap.unsqueeze(2).to_broadcast([ap.shape[0], ap.shape[1], n])


def repeat(ap, n):
    return ap.unsqueeze(1).to_broadcast([ap.shape[0], n, ap.shape[1]])



def sync_program(sp, m, A):
    S = m.sem
    sp.dma_start(m.wraw[:, 0], A["wstream"][0]).then_inc(m.w_in[0], 16)
    for n in range(4):
        sp.dma_start(m.xr[:, 2 * n:2 * n + 2], A["x"][:, 2 * n:2 * n + 2]).then_inc(m.x_in[n], 16)
    for u in range(1, RING):
        sp.dma_start(m.wraw[:, u], A["wstream"][u]).then_inc(m.w_in[u], 16)

    def load(u, s):
        sp.wait_ge(S.gemm_done, u - 3)
        src = A["wstream"][u] if isinstance(u, int) else A["wstream"][bass.ds(u, 1)].rearrange("a p n -> p (a n)")
        sp.dma_start(m.wraw[:, s], src).then_inc(m.w_in[s], 16)

    with sp.Fori(0, (UNITS - 1) // RING - 1) as i:
        for s in range(RING):
            load(4 * i + (RING + s), s)
    load(UNITS - 1, 0)
    for h in range(2):
        for k in range(0, KT, 2):
            sp.wait_ge(S.nrm_x, 16 * 3 + 8 * h + k + 2)
            sp.dma_start(A["y"][:, k:k + 2, h * HT:(h + 1) * HT], m.r[:, k:k + 2, h * HT:(h + 1) * HT]).then_inc(S.y_out, 16)
    sp.wait_ge(S.y_out, 16 * 8)
    for j in range(2):
        sp.wait_ge(m.vrow_out[j], 16 * 8)
    sp.wait_ge(S.tail_out, 16)
    sp.wait_ge(S.hs_out, 16 * GROUPS)
    sp.wait_ge(S.hp_out, 16 * GROUPS)
    sp.wait_ge(S.acum_out, 16)



def pool_program(pool, m, A):
    S = m.sem

    def split(u, s, arrived):
        pool.wait_ge(m.w_in[s], arrived)
        pool.tensor_tensor(m.tick[:, 1:2], m.tick[:, 0:1], m.tick[:, 0:1], ALU.add)
        pool.tensor_scalar(m.wh[:, s], m.wraw[:, s], 1.0, 1.0, ALU.mult, ALU.mult).then_inc(S.w_hi, 1)
        pool.wait_ge(S.w_hi, u + 1)
        pool.tensor_tensor(m.wl[:, s], m.wraw[:, s], m.wh[:, s], ALU.subtract).then_inc(S.w_ready, 1)

    def split_one(u):
        split(u, u % RING, 16 * (u // RING + 1))

    def run(u0, n):
        with pool.Fori(0, n) as i:
            for j in range(RING):
                u = u0 + j
                split(4 * i + u, u % RING, 16 * i + 16 * (u // RING + 1))

    def norm(n, u0):
        split_one(u0)
        split_one(u0 + 1)
        for k in range(KT):
            if n == 1 and k == 4:
                split_one(u0 + 2)
            x_lo(pool, m, n, 0, k)
        if n != 1:
            split_one(u0 + 2)
        else:
            split_one(u0 + 3)
        for k in range(1, KT, 2):
            x_lo(pool, m, n, 1, k)
        if n != 1:
            split_one(u0 + 3)

    pool.memset(m.tick[:, :], 0.0).then_inc(S.tick_zero, 1)
    pool.wait_ge(S.tick_zero, 1)
    split_one(0)
    pool.memset(m.ident[:, :], 0.0).then_inc(S.consts, 1)
    pool.memset(m.causal[:, :], 1.0).then_inc(S.consts, 1)
    pool.memset(m.ones[:, :], 1.0).then_inc(S.consts, 1)
    pool.memset(m.eps[:, :], EPS).then_inc(S.consts, 1)
    pool.memset(m.tokd[:, NCH - 1, :], 0.0).then_inc(S.tokd_zero, 1)
    pool.wait_ge(S.consts, 2)
    pool.affine_select(out=m.ident[:, :], in_=m.ident[:, :], compare_op=ALU.not_equal, fill=1.0, base=0,
                       pattern=[[-1, P]], channel_multiplier=1).then_inc(S.consts, 1)
    pool.affine_select(out=m.causal[:, :], in_=m.causal[:, :], compare_op=ALU.is_ge, fill=0.0, base=0,
                       pattern=[[1, P]], channel_multiplier=-1).then_inc(S.consts, 1)
    run(1, (U_FFN0 - 1) // RING)
    norm(0, U_FFN0)
    run(U_FFN0 + 4, (U_V - U_FFN0) // RING - 1)
    norm(1, U_V)
    run(U_V + 4, 1)
    pool.wait_ge(S.ws_in, 16)
    pool.affine_select(out=m.wst[:, :, :], in_=m.wst[:, :, :], compare_op=ALU.is_ge, fill=0.0, base=0,
                       pattern=[[0, 8], [1, BLK]], channel_multiplier=-1).then_inc(S.ws_masked, 1)
    run(U_V + 8, (U_FFN1 - U_V) // RING - 2)
    norm(2, U_FFN1)
    run(U_FFN1 + 4, (UNITS - U_FFN1) // RING - 1)



def tensor_program(pe, m, A):
    S = m.sem
    mm = pe.matmul

    def products(out, w, k, x, start, stop):
        w_hi, w_lo = m.wh[:, w, k * P:(k + 1) * P], m.wl[:, w, k * P:(k + 1) * P]
        mm(out, w_hi, x[0], start=start, stop=False)
        mm(out, w_hi, x[1], start=False, stop=False)
        return mm(out, w_lo, x[0], start=False, stop=stop)

    def unit(u, w, turn, xh, xl, each=None):
        s = w % 2
        pe.wait_ge(S.w_ready, u + 1)
        wait(pe, m.slot_evac[s], turn)
        steps = [(h, k) for h in range(2) for k in range(KT)] if each is None else \
            [(h, k) for k in range(KT) for h in range(2)]
        for h, k in steps:
            if each is not None and h == 0:
                each(k)
            last = products(m.ps[:, 2 * s + h, 0:HT], w, k, (half_of(xh, k, h), half_of(xl, k, h)), k == 0, k == KT - 1)
        last.then_inc(S.gemm_done, 1)

    def run_few(u0, n, xh, xl):
        for u in range(u0, u0 + n):
            unit(u, u % RING, slot_turn(u), xh, xl)

    def run(u0, n, xh, xl):
        with pe.Fori(0, n) as i:
            for j in range(RING):
                unit(4 * i + (u0 + j), (u0 + j) % RING, 2 * i + slot_turn(u0 + j), xh, xl)

    def layer_norm_sums(n, h):
        pe.wait_ge(S.sum1_ready, 10 * n + 8 + 2 * h)
        mm(m.ps[:, 4 + h, 0:HT], m.ones[:, :], m.s1[:, h], start=True, stop=True)
        pe.wait_ge(S.sum2_ready, 10 * n + 8 + 2 * h)
        mm(m.ps[:, 6 + h, 0:HT], m.ones[:, :], m.s2[:, h], start=True, stop=True).then_inc(S.stat_done, 1)

    def last_block(n, u0, xh, xl):
        run_few(u0, 6, xh, xl)
        for h in range(2):
            for u in (u0 + 6, u0 + 7):
                s = u % 2
                if h == 0:
                    pe.wait_ge(S.w_ready, u + 1)
                    pe.wait_ge(m.slot_evac[s], slot_turn(u))
                for k in range(KT):
                    last = products(m.ps[:, 2 * s + h, 0:HT], u % RING, k, (half_of(xh, k, h), half_of(xl, k, h)),
                                    k == 0, k == KT - 1)
                last.then_inc(S.gemm_done if h else S.half_done, 1)
                if h == 1 and u == u0 + 6:
                    layer_norm_sums(n, 0)

    def first_pair(n, u0):
        for h in range(2):
            for k in range(KT):
                if h == 0 and k == 2:
                    layer_norm_sums(n, 1)
                wait_x(pe, m, n, h, k)
                for u in (u0, u0 + 1):
                    s = u % 2
                    if k == 0:
                        pe.wait_ge(S.w_ready, u + 1)
                        if h == 1:
                            pe.wait_ge(m.slot_evac[s], slot_turn(u))
                    last = products(m.ps[:, 2 * s + h, 0:HT], u % RING, k, (half_of(m.xh, k, h), half_of(m.xl, k, h)),
                                    k == 0, k == KT - 1)
                    if h == 1 and k == KT - 1:
                        last.then_inc(S.gemm_done, 1)

    unit(0, 0, 0, m.xh, m.xl, each=lambda k: pe.wait_ge(S.x_lo, k + 1))
    run_few(1, 5, m.xh, m.xl)
    pe.wait_ge(S.dt_dve, DT_STEPS)
    pe.wait_ge(S.consts, 6)
    for c in range(NCH):
        n = TS if c == 4 else Q
        last = pe.transpose(m.ps[0:n, 4 + c // 4, (c % 4) * P:(c % 4) * P + P],
                            m.dtt[:, DT_OUT, c * Q:c * Q + n], m.ident[:, :])
    last.then_inc(S.tok_t, 1)
    run_few(6, 1, m.xh, m.xl)

    def chunk_in(g, n):
        t0, q = cols(n)
        b = m.ps[:, 4 + n % 2, :]
        if n == 0:
            pe.wait_ge(S.silu_ready, 4 * g + 4)
            wait(pe, S.ms_ln, g)
            pe.wait_ge(S.tokd_ready, 2)
        if n in (2, 4):
            pe.wait_ge(S.xw_ready, 5 * g + (n - 1))
        if n == 3:
            pe.wait_ge(S.y_evac, 5 * g + 2)
        mm(b[0:q, 0:q], m.act[:, 0, t0:t0 + q], m.act[:, 1, t0:t0 + q], start=True, stop=True)
        for j, tile in enumerate((0, 2, 3)):
            last = pe.transpose(b[0:q, (j + 1) * P:(j + 2) * P], m.act[:, tile, t0:t0 + q], m.ident[:, :])
        last.then_inc(S.s1_done, 1)

    def chunk_out(g, n):
        t0, q = cols(n)
        k = n % 2
        yb = m.ps[:, 5 if n == 1 else 6, :]
        h = m.hs if n == 1 else m.hp
        pe.wait_ge(S.m_ready, 5 * g + (n + 1))
        if n == 0:
            wait(pe, S.h_ready, 5 * g)
        else:
            pe.wait_ge(S.cs_ready, 4 * g + n)
            pe.wait_ge(S.h_ready, 5 * g + n)
        if n == 1:
            pe.wait_ge(S.hs_in, 16 * g + 16)
        mm(m.ps[:, 7, 0:HPG * HD], m.btok[0:q, k, :], m.xw[0:q, k, :], start=True, stop=True)
        for j in range(2):
            for p in range(2):
                e = 2 * j + p
                out = yb[p * HD:(p + 1) * HD, j * Q:j * Q + q]
                last = mm(out, m.xdt[0:q, k, e * HD:(e + 1) * HD], m.dec[0:q, k, e, 0:q], start=True, stop=(n == 0))
                if n > 0:
                    last = mm(out, h[:, e * HD:(e + 1) * HD], m.cs[:, k, e, 0:q], start=False, stop=True)
        last.then_inc(S.s_done, 1)

    def mean_squares(g):
        pe.wait_ge(S.sq_ready, g + 1)
        for h in range(2):
            for j in range(2):
                last = mm(m.ps[:, 4 + h, 0:HT], m.ones[:, :], m.sq[:, j, h * HT:(h + 1) * HT],
                          start=(j == 0), stop=(j == 1))
        last.then_inc(S.ms_done, 1)

    def group(g, even, last=False):
        def nxt(j):
            if last:
                run_few(U_WOUT + j, 1, m.hh[:, 0:8], m.hl[:, 0:8])
            else:
                u0 = U_SSD + 6 + j
                unit(6 * g + u0, (u0 + (0 if even else 6)) % RING, 3 * g + slot_turn(u0), m.xh, m.xl)

        chunk_in(g, 0)
        chunk_in(g, 1)
        nxt(0)
        chunk_out(g, 0)
        chunk_out(g, 1)
        chunk_in(g, 2)
        nxt(1)
        chunk_out(g, 2)
        chunk_in(g, 3)
        nxt(2)
        chunk_out(g, 3)
        chunk_in(g, 4)
        nxt(3)
        chunk_out(g, 4)
        nxt(4)
        mean_squares(g)
        nxt(5)

    group(0, True)
    with pe.Fori(0, (GROUPS - 2) // 2) as i:
        group(2 * i + 1, False)
        group(2 * i + 2, True)
    pe.wait_ge(S.yn_lo, GROUPS // 2)
    group(GROUPS - 1, False, last=True)
    run_few(U_WOUT + 6, 2, m.hh[:, 0:8], m.hl[:, 0:8])
    pe.wait_ge(S.yn_lo, GROUPS)
    last_block(0, U_WOUT + 8, m.hh[:, 8:16], m.hl[:, 8:16])

    def ffn(layer, u0):
        n = 2 * layer
        first_pair(n, u0)
        run_few(u0 + 2, 2, m.xh, m.xl)
        run(u0 + 4, 3, m.xh, m.xl)
        for b, (kind, c) in enumerate(FFN_BLOCKS):
            k = 8 * (c % 2)
            if kind == "down":
                pe.wait_ge(S.hid_lo, 32 * layer + 8 * (c + 1))
                if c == 3:
                    last_block(n + 1, u0 + 8 * b, m.hh[:, k:k + 8], m.hl[:, k:k + 8])
                else:
                    run(u0 + 8 * b, 2, m.hh[:, k:k + 8], m.hl[:, k:k + 8])
            elif b > 1:
                run(u0 + 8 * b, 2, m.xh, m.xl)

    ffn(0, U_FFN0)

    def v_products(t, kp, kk):
        n = TS if t == 4 else P
        s, k = (U_V + kp) % RING, 2 * kp + kk
        out = m.ps[0:n, V_BANK[t], :]
        x_hi, x_lo = m.xh[:, k, t * P:t * P + n], m.xl[:, k, t * P:t * P + n]
        w_hi, w_lo = m.wh[:, s, kk * 512:kk * 512 + 512], m.wl[:, s, kk * 512:kk * 512 + 512]
        mm(out, x_hi, w_hi, start=(k == 0), stop=False)
        mm(out, x_hi, w_lo, start=False, stop=False)
        return mm(out, x_lo, w_hi, start=False, stop=(k == KT - 1))

    def v_first():
        for tiles_of in ((0, 1), (2, 3, 4)):
            h = 0 if tiles_of[0] == 0 else 1
            for k in range(KT):
                if h == 0 and k == 2:
                    layer_norm_sums(1, 1)
                wait_x(pe, m, 1, h, k)
                pe.wait_ge(S.w_ready, U_V + k // 2 + 1)
                for t in tiles_of:
                    last = v_products(t, k // 2, k % 2)
                    if t == 4 and k % 2:
                        last.then_inc(S.gemm_done, 1)
                    elif t < 4 and k == KT - 1:
                        last.then_inc(S.v_done, 1)

    def v_block(b):
        for kp in range(4):
            pe.wait_ge(S.w_ready, 4 * b + (U_V + kp + 1))
            for t in range(NTOK):
                if kp == 0:
                    pe.wait_ge(S.v_gelu, 5 * b + (t - 4))
                for kk in range(2):
                    last = v_products(t, kp, kk)
                if kp == 3 and t < 4:
                    last.then_inc(S.v_done, 1)
            last.then_inc(S.gemm_done, 1)

    v_first()
    with pe.Fori(1, 4) as b:
        v_block(b)

    pe.wait_ge(S.v_gelu, 5 * 3 + 4)
    with pe.Fori(0, 4) as i:
        for n in range(4):
            u, j = U_U + n, n % 2
            unit(4 * i + u, u % RING, 2 * i + slot_turn(u), m.xh, m.xl)
            pe.wait_ge(S.wsm_ready, 2 * i + (n // 2 + 1))
            pe.wait_ge(S.vm_ready, 4 * i + (n + 1))
            for t in range(4):
                mm(m.ps[:, 4 + 2 * j, t * BLK:(t + 1) * BLK], m.vm[:, j, t, :], m.wsm[:, :], start=True, stop=True)
            mm(m.ps[:, 5 + 2 * j, 0:TS], m.vm[0:TS, j, 4, :], m.wsm[0:TS, 0:TS],
               start=True, stop=True).then_inc(S.mix_done, 1)
    pe.wait_ge(S.uv_lo, 8)
    run(U_CMOUT, 2, m.hh[:, 0:8], m.hl[:, 0:8])
    pe.wait_ge(S.uv_lo, 16)
    last_block(2, U_CMOUT + 8, m.hh[:, 8:16], m.hl[:, 8:16])
    ffn(1, U_FFN1)
    layer_norm_sums(3, 1)



def scalar_program(act, m, A):
    S = m.sem
    f = act.activation

    act.dma_start(m.pv[:, :], A["pv"]).then_inc(S.pv_in, 16)
    act.dma_start(m.chalo[:, :, :, :], A["conv_halo"]).then_inc(S.chalo_in, 16)
    for k in range(KT):
        act.wait_ge(m.x_in[k // 2], 16)
        f(m.xh[:, k], m.xr[:, k], ACT.Copy).then_inc(S.x_hi, 1)
    act.wait_ge(S.pv_in, 16)
    f(m.nega[:, :], m.pv[:, PV_ALOG:PV_ALOG + 1], ACT.Exp).then_inc(S.dt_act, 1)
    act.wait_ge(m.slot_evac[0], 1)
    f(m.dtt[:, 1], m.dtt[:, 0], ACT.Abs).then_inc(S.dt_act, 1)
    act.wait_ge(S.dt_act, 2)
    f(m.dtt[:, 2], m.dtt[:, 1], ACT.Exp, scale=-1.0).then_inc(S.dt_act, 1)
    act.wait_ge(S.dt_dve, 2)
    f(m.dtt[:, 4], m.dtt[:, 3], ACT.Ln).then_inc(S.dt_act, 1)

    def raw_tile(g, j, u):
        s = u % 2 if isinstance(u, int) else (U_SSD + j) % 2
        k = j % 2
        act.wait_ge(S.gemm_done, u + 1)
        wait(act, S.conv_tap, 16 * g + 4 * (j - 1))
        r = m.raw[:, k]
        halo = m.chalo[:, g, j] if isinstance(g, int) else m.chalo[:, bass.ds(g, 1), j].rearrange("p a c -> p (a c)")
        f(r[:, HALO + TP:2 * HALO + TP], halo, ACT.Copy)
        f(r[:, HALO:HALO + HT], m.ps[:, 2 * s, 0:HT], ACT.Copy)
        f(r[:, HALO + HT:HALO + TP], m.ps[:, 2 * s + 1, 0:TP - HT], ACT.Copy)
        f(r[:, 2 * HALO + TP:RAW], m.ps[:, 2 * s + 1, TP - HT:HT], ACT.Copy).then_inc(m.slot_evac[s], 1)

    def silu_z(g, j, u):
        s = (U_SSD + 4 + j) % 2
        act.wait_ge(S.gemm_done, u + 1)
        wait(act, S.gate_ready, g)
        f(halves(m.zs[:, j]), bank_pair(m, s), ACT.Silu).then_inc(m.slot_evac[s], 1)

    def silu_conv(g):
        wait(act, S.h_ready, 5 * g)
        for b in range(2):
            act.wait_ge(S.conv_tap, 16 * g + (8 * b + 8))
            f(m.act[:, 2 * b:2 * b + 2, 0:TP], m.acc[:, 2 * b:2 * b + 2, 0:TP], ACT.Silu).then_inc(S.silu_ready, 1)
            f(m.act[:, 2 * b:2 * b + 2, TP:T], m.acc[:, 2 * b:2 * b + 2, TP + HALO:CONV],
              ACT.Silu).then_inc(S.silu_ready, 1)

    def load_group(g):
        rows = A["acum"][4 * g:4 * g + 4] if isinstance(g, int) else A["acum"][bass.ds(4 * g, 4)]
        wait(act, S.dec_sub, 5 * g)
        wait(act, S.ea_ready, 4 * g)
        act.dma_start(m.acb[:, :, :], rows.unsqueeze(0).to_broadcast([P, HPG, T])).then_inc(S.acb_in, 16)
        wait(act, S.h_ready, 5 * g - 3)
        src = A["ssm_in"][:, bass.ds(HPG * HD * g, HPG * HD)] if not isinstance(g, int) else \
            A["ssm_in"][:, HPG * HD * g:HPG * HD * (g + 1)]
        act.dma_start(m.hs[:, :], src).then_inc(S.hs_in, 16)

    def exp_acum(g, n):
        t0, q = cols(n)
        act.wait_ge(S.acb_in, 16 * g + 16)
        wait(act, S.h_ready, 5 * g + {1: 0, 2: 0, 3: 2, 4: 3}[n])
        f(m.ea[:, n % 2, :, 0:q], m.acb[:, :, t0:t0 + q], ACT.Exp).then_inc(S.ea_ready, 1)

    def exp_win(g):
        act.wait_ge(S.win_arg, 2 * g + 2)
        f(m.win[:, :, :], m.win[:, :, :], ACT.Exp).then_inc(S.win_exp, 1)

    def exp_decay(g, n):
        q = cols(n)[1]
        act.wait_ge(S.dec_arg, 5 * g + (n + 1))
        f(m.dec[0:q, n % 2, :, 0:q], m.dec[0:q, n % 2, :, 0:q], ACT.Exp).then_inc(S.dec_exp, 1)

    def rms(g):
        act.wait_ge(S.ms_done, g + 1)
        wait(act, S.yn_f, 2 * g)
        f(halves(m.rms[:, :]), m.ps[:, 4:6, 0:HT], ACT.Ln, bias=m.eps[:, :], scale=1.0 / (HPG * HD)).then_inc(S.ms_ln, 1)
        act.wait_ge(S.ms_ln, g + 1)
        f(m.rms[:, :], m.rms[:, :], ACT.Exp, scale=-0.5).then_inc(S.rms_ready, 1)

    act.wait_ge(S.x_lo, KT)
    act.wait_ge(S.chalo_in, 16)
    for j in range(4):
        raw_tile(0, j, U_SSD + j)
    act.wait_ge(S.dt_dve, DT_ACUM)
    act.dma_start(A["acum"], m.dtt[32:64, DT_OUT, :]).then_inc(S.acum_out, 16)
    act.wait_ge(S.acum_out, 16)
    load_group(0)
    act.wait_ge(S.consts, 6)
    exp_acum(0, 1)
    exp_acum(0, 2)
    exp_win(0)
    silu_z(0, 0, U_SSD + 4)
    act.wait_ge(S.tok_t, 1)
    silu_conv(0)
    silu_z(0, 1, U_SSD + 5)

    def group(g, more):
        exp_decay(g, 0)
        exp_decay(g, 1)
        if more:
            raw_tile(g + 1, 0, 6 * g + (U_SSD + 6))
        exp_decay(g, 2)
        exp_acum(g, 3)
        if more:
            raw_tile(g + 1, 1, 6 * g + (U_SSD + 7))
        exp_decay(g, 3)
        exp_acum(g, 4)
        if more:
            raw_tile(g + 1, 2, 6 * g + (U_SSD + 8))
        exp_decay(g, 4)
        if more:
            load_group(g + 1)
        dst = A["ssm_s"][:, bass.ds(HPG * HD * g, HPG * HD)] if not isinstance(g, int) else \
            A["ssm_s"][:, HPG * HD * g:HPG * HD * (g + 1)]
        act.wait_ge(S.h_ready, 5 * g + 2)
        act.dma_start(dst, m.hsn[:, :]).then_inc(S.hs_out, 16)
        if more:
            raw_tile(g + 1, 3, 6 * g + (U_SSD + 9))
        dst = A["ssm_p"][:, bass.ds(HPG * HD * g, HPG * HD)] if not isinstance(g, int) else \
            A["ssm_p"][:, HPG * HD * g:HPG * HD * (g + 1)]
        act.wait_ge(S.h_ready, 5 * g + 5)
        act.dma_start(dst, m.hp[:, :]).then_inc(S.hp_out, 16)
        act.wait_ge(S.gate_ready, g + 1)
        wait(act, S.ms_done, g)
        f(m.sq[:, :, :], m.y[:, :, :], ACT.Square).then_inc(S.sq_ready, 1)
        if more:
            exp_acum(g + 1, 1)
            exp_acum(g + 1, 2)
            exp_win(g + 1)
            rms(g)
            silu_z(g + 1, 0, 6 * g + (U_SSD + 10))
            silu_conv(g + 1)
            silu_z(g + 1, 1, 6 * g + (U_SSD + 11))

    group(0, True)
    with act.Fori(1, GROUPS - 1) as g:
        group(g, True)
    group(GROUPS - 1, False)
    rms(GROUPS - 1)
    act.wait_ge(S.ctail_ready, 2 * 4 * GROUPS)
    act.dma_start(A["conv_tail"], m.ctail[:, :, :, :, :]).then_inc(S.tail_out, 16)

    def square(n, idx):
        wait(act, S.sum2_ready, 10 * n + (idx - 1))
        j = idx % 2
        out, src = (m.sqm[:, j], m.r[:, idx]) if idx < 6 else \
            (half_of(m.sqm, j, (idx - 6) // 2), half_of(m.r, 6 + j, (idx - 6) // 2))
        f(out, src, ACT.Square).then_inc(S.sqr_ready, 1)

    def layer_norm(n, u0):
        act.wait_ge(S.stat_zero, 2 * n + 2)
        for k in range(6):
            act.wait_ge(m.slot_evac[(u0 + k) % 2], slot_turn(u0 + k) + 1)
            square(n, k)

        def square_half(h, j):
            u = u0 + 6 + j
            if h == 0:
                act.wait_ge(S.res_half, 2 * n + j + 1)
            else:
                act.wait_ge(m.slot_evac[u % 2], slot_turn(u) + 1)
            square(n, 6 + 2 * h + j)

        def mean_squared(h):
            act.wait_ge(S.stat_done, 2 * n + h + 1)
            f(m.msq[:, h], m.ps[:, 4 + h, 0:HT], ACT.Square, scale=1.0 / D).then_inc(S.msq_ready, 1)

        def inverse_deviation(h):
            act.wait_ge(S.var_ready, 4 * n + 2 * h + 2)
            f(m.msq[:, h], m.msq[:, h], ACT.Ln, bias=m.eps[:, :]).then_inc(S.var_ln, 1)
            act.wait_ge(S.var_ln, 2 * n + h + 1)
            f(m.rstd[:, h], m.msq[:, h], ACT.Exp, scale=-0.5).then_inc(S.rstd_ready, 1)

        def tile(h, k):
            q = 8 * h + k
            act.wait_ge(S.nrm_b, 16 * n + q + 1)
            gain = m.pv[:, PV_LN + 16 * n + k:PV_LN + 16 * n + k + 1]
            bias = m.pv[:, PV_LN + 16 * n + 8 + k:PV_LN + 16 * n + 9 + k]
            if n < 3:
                if 16 * n + q >= 4:
                    before = (n, h, k - 4) if k >= 4 else (n, 0, k + 4) if h else (n - 1, 1, k + 4)
                    wait_x(act, m, *before)
                f(half_of(m.xh, k, h), m.na[:, k % 4], ACT.Identity, bias=bias, scale=gain)
                f(m.xf[:, k % 4], m.na[:, k % 4], ACT.Identity, bias=bias, scale=gain).then_inc(S.nrm_x, 1)
            else:
                f(half_of(m.r, k, h), m.na[:, k % 4], ACT.Identity, bias=bias, scale=gain).then_inc(S.nrm_x, 1)

        square_half(0, 0)
        square_half(0, 1)
        square_half(1, 0)
        mean_squared(0)
        inverse_deviation(0)
        tile(0, 0)
        tile(0, 1)
        square_half(1, 1)
        for k in range(2, 6):
            tile(0, k)
        mean_squared(1)
        tile(0, 6)
        tile(0, 7)
        inverse_deviation(1)
        for k in range(KT):
            tile(1, k)

    def ffn(layer, u0):
        for b, (kind, c) in enumerate(FFN_BLOCKS):
            if kind == "up":
                with act.Fori(0, 4) as i:
                    for j in range(2):
                        u = u0 + 8 * b + j
                        before = 32 * layer + 8 * c + j
                        act.wait_ge(S.gemm_done, 2 * i + (u + 1))
                        if before >= 2:
                            act.wait_ge(S.hid_ready, 2 * i + (before - 1))
                        f(halves(m.rl[:, j]), bank_pair(m, u % 2), ACT.Relu).then_inc(m.slot_evac[u % 2], 1)
                        act.wait_ge(S.hid_ready, 2 * i + (before + 1))
                        f(one(m.hh, 2 * i + (8 * (c % 2) + j)), m.hq[:, j], ACT.Copy).then_inc(S.hid_hi, 1)

    act.wait_ge(S.tail_out, 16)
    layer_norm(0, U_WOUT + 8)
    ffn(0, U_FFN0)
    layer_norm(1, U_V - 8)
    act.dma_start(m.bb[:, :], A["bias_v"].to_broadcast([P, CMW])).then_inc(S.bb_in, 16)
    wait_x(act, m, 1, 1, 6)
    wait_x(act, m, 1, 1, 7)
    act.dma_start(m.gam[:, :], A["ln_gain"].to_broadcast([P, CMW])).then_inc(S.gam_in, 16)
    act.dma_start(m.bet[:, :], A["ln_bias"].to_broadcast([P, CMW])).then_inc(S.bet_in, 16)
    act.dma_start(m.wst[:, :, :], A["w_spatial"]).then_inc(S.ws_in, 16)
    act.dma_start(m.bsb[:, :, :], A["b_spatial"].to_broadcast([P, 8 * BLK]).rearrange("p (g t) -> p g t", g=8)
                  ).then_inc(S.bs_in, 16)
    act.wait_ge(S.v_zero, 4)
    for part, place in ((0, "v1"), (1, "v2")):
        with act.Fori(0, 2) as i:
            for t in range(NTOK):
                n = TS if t == 4 else P
                act.wait_ge(S.v_bias, 5 * i + (10 * part + t + 1))
                if part == 0:
                    dst = m.v1[0:n, bass.ds(4 * i, 4), t, :]
                else:
                    dst = m.v2[0:n, bass.ds(i, 1), 8 * T:8 * T + 4 * NTOK * P].rearrange(
                        "p a (m t c) -> p (a m) t c", t=NTOK, c=P)[:, :, t, :]
                f(dst, m.ps[0:n, V_BANK[t], :].rearrange("p (m c) -> p m c", c=P), ACT.Gelu_apprx_tanh).then_inc(S.v_gelu, 1)
    act.wait_ge(S.v_mv, NTOK)
    f(m.vrs[:, :, :], m.vmv[:, :, 1:2], ACT.Ln, bias=m.eps[:, :]).then_inc(S.v_ln, 1)
    act.wait_ge(S.v_ln, 1)
    f(m.vrs[:, :, :], m.vrs[:, :, :], ACT.Exp, scale=-0.5).then_inc(S.v_rs, 1)

    def u_tile(i, j):
        u = U_U + j
        act.wait_ge(S.vm_ready, 2 * i + (j + 1))
        act.dma_start(A["v_rows"][:, bass.ds(2 * i + j, 1)].rearrange("p a c -> p (a c)") if not isinstance(i, int)
                      else A["v_rows"][:, 2 * i + j], m.vm[0:TS, j, 4, :]).then_inc(m.vrow_out[j], 16)
        act.wait_ge(S.gemm_done, 2 * i + (u + 1))
        wait(act, S.uv_ready, 2 * i + (j - 1))
        bias = m.pv[:, bass.ds(2 * i + (PV_BU + j), 1)] if not isinstance(i, int) else m.pv[:, PV_BU + j:PV_BU + j + 1]
        f(halves(m.ug[:, j]), bank_pair(m, u % 2), ACT.Gelu_apprx_tanh, bias=bias).then_inc(m.slot_evac[u % 2], 1)
        act.wait_ge(S.uv_ready, 2 * i + (j + 1))
        f(one(m.hh, 2 * i + j), m.sb[:, j], ACT.Copy).then_inc(S.uv_hi, 1)

    u_tile(0, 0)
    u_tile(0, 1)
    with act.Fori(1, 8) as i:
        u_tile(i, 0)
        u_tile(i, 1)
    layer_norm(2, U_CMOUT + 8)
    ffn(1, U_FFN1)
    layer_norm(3, UNITS - 8)



def vector_program(dve, m, A):
    S = m.sem
    tt, ts, stt, cp = dve.tensor_tensor, dve.tensor_scalar, dve.scalar_tensor_tensor, dve.tensor_copy

    for k in range(KT):
        dve.wait_ge(S.x_hi, k + 1)
        tt(m.xl[:, k], m.xr[:, k], m.xh[:, k], ALU.subtract).then_inc(S.x_lo, 1)
    dve.wait_ge(S.x_lo, KT)
    dve.memset(m.raw[:, :, 0:HALO], 0.0).then_inc(S.raw_zero, 1)

    d = m.dtt
    dve.wait_ge(S.pv_in, 16)
    dve.wait_ge(S.dt_act, 1)
    ts(m.nega[:, :], m.nega[:, :], -1.0, None, ALU.mult).then_inc(S.dt_dve, 1)
    dve.wait_ge(S.gemm_done, 1)
    ts(halves(d[:, 0]), bank_pair(m, 0), m.pv[:, PV_DTB:PV_DTB + 1], None, ALU.add).then_inc(m.slot_evac[0], 1)
    dve.wait_ge(S.dt_act, 3)
    ts(d[:, 3], d[:, 2], 1.0, None, ALU.add).then_inc(S.dt_dve, 1)
    dve.wait_ge(S.dt_dve, 2)
    ts(d[:, 5], d[:, 3], 1.0, None, ALU.subtract).then_inc(S.dt_dve, 1)
    dve.reciprocal(d[:, 6], d[:, 3]).then_inc(S.dt_dve, 1)
    dve.wait_ge(S.dt_dve, 4)
    tt(d[:, 5], d[:, 2], d[:, 5], ALU.subtract).then_inc(S.dt_dve, 1)
    dve.wait_ge(S.dt_dve, 5)
    tt(d[:, 5], d[:, 5], d[:, 6], ALU.mult).then_inc(S.dt_dve, 1)
    dve.wait_ge(S.dt_dve, 6)
    dve.wait_ge(S.dt_act, 4)
    stt(d[:, 1], d[:, 0], 0.0, d[:, 5], ALU.max, ALU.add).then_inc(S.dt_dve, 1)
    dve.wait_ge(S.dt_dve, 7)
    tt(d[:, 1], d[:, 1], d[:, 4], ALU.add).then_inc(S.dt_dve, 1)
    dve.wait_ge(S.dt_dve, 8)
    ts(d[:, 2], d[:, 1], m.nega[:, :], None, ALU.mult).then_inc(S.dt_dve, 1)
    dve.wait_ge(S.dt_dve, 9)
    dve.wait_ge(S.consts, 6)
    for c in range(NCH):
        q = TS if c == 4 else Q
        dve.tensor_tensor_scan(d[:, DT_OUT, c * Q:c * Q + q], m.ones[:, 0:q], d[:, 2, c * Q:c * Q + q],
                               0.0, ALU.mult, ALU.add).then_inc(S.dt_dve, 1)
    dve.wait_ge(S.dt_dve, DT_ACUM)
    cp(d[0:32, DT_OUT, :], d[0:32, 1, :]).then_inc(S.dt_dve, 1)

    def conv_params(g):
        a = 20 * g + PV_CONV
        src = m.pv[:, a:a + 20] if isinstance(g, int) else m.pv[:, bass.ds(a, 20)]
        wait(dve, S.conv_tap, 16 * g)
        cp(m.cpar[:, :, :].rearrange("p a b -> p (a b)"), src).then_inc(S.cpar_ready, 1)

    def conv(g, j):
        s = (U_SSD + j) % 2
        u = U_SSD + j
        r, a = m.raw[:, j % 2], m.acc[:, j]
        turn = slot_turn(u)
        dve.wait_ge(m.slot_evac[s], 3 * g + (turn + 1))
        dve.wait_ge(S.cpar_ready, g + 1)
        for b, at in enumerate((TP, RAW - HALO)):
            dst = m.ctail[:, g, j, b] if isinstance(g, int) else \
                m.ctail[:, bass.ds(g, 1), j, b].rearrange("p a c -> p (a c)")
            cp(dst, r[:, at:at + HALO]).then_inc(S.ctail_ready, 1)
        if j == 0:
            wait(dve, S.silu_ready, 4 * g)
            dve.wait_ge(S.raw_zero, 1)
        ts(a, r[:, 0:CONV], m.cpar[:, j, 0:1], m.cpar[:, j, 4:5], ALU.mult, ALU.add).then_inc(S.conv_tap, 1)
        for k in range(1, 4):
            dve.wait_ge(S.conv_tap, 16 * g + (4 * j + k))
            stt(a, r[:, k:k + CONV], m.cpar[:, j, k:k + 1], a, ALU.mult, ALU.add).then_inc(S.conv_tap, 1)

    def group_columns(g):
        dve.wait_ge(S.tokd_ready, 2)
        for dst, at in ((m.gdt, 0), (m.gac, HEADS)):
            src = m.tokd[:, :, at + 4 * g:at + 4 * g + 4] if isinstance(g, int) else \
                m.tokd[:, :, bass.ds(4 * g + at, 4)]
            wait(dve, S.m_ready, 5 * g)
            cp(dst[:, :, :], src).then_inc(S.gdt_ready, 1)
        dve.wait_ge(S.gdt_ready, 2 * g + 2)
        dve.wait_ge(S.acb_in, 16 * g + 16)
        last = m.acb[:, :, 0:TP].rearrange("p h (c q) -> p c h q", q=Q)[:, :, :, Q - 1]
        tt(m.win[:, 0:4, :], last, m.gac[:, 0:4, :], ALU.subtract).then_inc(S.win_arg, 1)
        tt(m.win[:, 4, :], m.acb[:, :, T - 1], m.gac[:, 4, :], ALU.subtract).then_inc(S.win_arg, 1)
        dve.wait_ge(S.win_exp, g + 1)
        tt(m.dtw[:, :, :], m.gdt[:, :, :], m.win[:, :, :], ALU.mult).then_inc(S.dtw_ready, 1)

    def skip_params(g):
        a = 4 * g + PV_GRP
        src = m.pv[:, a:a + 4] if isinstance(g, int) else m.pv[:, bass.ds(a, 4)]
        wait(dve, S.yn_f, 2 * g)
        cp(m.gpar[:, :], src).then_inc(S.gpar_ready, 1)

    conv_params(0)
    conv(0, 0)
    conv(0, 1)
    conv(0, 2)
    conv(0, 3)
    dve.wait_ge(S.tok_t, 1)
    dve.wait_ge(S.tokd_zero, 1)
    cp(m.tokd[:, 0:4, :], m.ps[:, 4, :].rearrange("p (c e) -> p c e", e=P)[:, :, 0:2 * HEADS]).then_inc(S.tokd_ready, 1)
    cp(m.tokd[0:TS, 4, :], m.ps[0:TS, 5, 0:2 * HEADS]).then_inc(S.tokd_ready, 1)
    group_columns(0)
    skip_params(0)

    def before(g, n):
        t0, q = cols(n)
        k = n % 2
        c = ORDER[n]
        dec = m.dec[0:q, k, :, 0:q]
        if n == 0:
            dve.wait_ge(S.acb_in, 16 * g + 16)
            dve.wait_ge(S.gdt_ready, 2 * g + 2)
            wait(dve, S.s_done, 5 * g)
        if n >= 2:
            dve.wait_ge(S.s_done, 5 * g + (n - 1))
        tt(dec, m.acb[0:q, :, t0:t0 + q], spread(m.gac[0:q, c, :], q), ALU.subtract).then_inc(S.dec_sub, 1)
        dve.wait_ge(S.dec_sub, 5 * g + (n + 1))
        ts(dec, dec, 0.0, None, ALU.min).then_inc(S.dec_arg, 1)
        if n > 0:
            dve.wait_ge(S.ea_ready, 4 * g + n)
            dve.wait_ge(S.silu_ready, 4 * g + 4)
            tt(m.cs[:, k, :, 0:q], repeat(m.act[:, 1, t0:t0 + q], HPG), m.ea[:, k, :, 0:q],
               ALU.mult).then_inc(S.cs_ready, 1)

    def operands(g, n):
        t0, q = cols(n)
        k = n % 2
        c = ORDER[n]
        b = m.ps[:, 4 + k, :]
        dve.wait_ge(S.s1_done, 5 * g + (n + 1))
        dve.wait_ge(S.consts, 6)
        tt(m.cbm[0:q, k, 0:q], b[0:q, 0:q], m.causal[0:q, 0:q], ALU.mult).then_inc(S.cbm_ready, 1)
        cp(m.btok[0:q, k, :], b[0:q, P:2 * P])
        xt = b[0:q, 2 * P:4 * P].rearrange("p (h d) -> p h d", d=HD)
        tt(m.xdt[0:q, k, :].rearrange("p (h d) -> p h d", d=HD), xt, spread(m.gdt[0:q, c, :], HD), ALU.mult)
        dve.wait_ge(S.dtw_ready, g + 1)
        tt(m.xw[0:q, k, :].rearrange("p (h d) -> p h d", d=HD), xt, spread(m.dtw[0:q, c, :], HD),
           ALU.mult).then_inc(S.xw_ready, 1)
        dve.wait_ge(S.dec_exp, 5 * g + (n + 1))
        dve.wait_ge(S.cbm_ready, 5 * g + (n + 1))
        dec = m.dec[0:q, k, :, 0:q]
        tt(dec, dec, repeat(m.cbm[0:q, k, 0:q], HPG), ALU.mult).then_inc(S.m_ready, 1)

    def after(g, n):
        t0, q = cols(n)
        k = n % 2
        yb = m.ps[:, 5 if n == 1 else 6, :]
        if n == 0:
            wait(dve, S.sq_ready, g)
            dve.wait_ge(S.gpar_ready, g + 1)
        dve.wait_ge(S.s_done, 5 * g + (n + 1))
        new = m.ps[:, 7, 0:HPG * HD].rearrange("p (h d) -> p h d", d=HD)
        old, out = (m.hs, m.hsn) if n == 1 else (m.hp, m.hp)
        hv = lambda x: x[:, :].rearrange("p (h d) -> p h d", d=HD)
        if n > 0:
            if n == 1:
                dve.wait_ge(S.hs_in, 16 * g + 16)
            tt(hv(m.hdec), hv(old), m.ea[:, k, :, q - 1:q].to_broadcast([P, HPG, HD]), ALU.mult
               ).then_inc(S.hdec_ready, 1)
        stt(m.y[:, 0, t0:t0 + q], m.act[:, 2, t0:t0 + q], m.gpar[:, 0:1], yb[:, 0:q], ALU.mult, ALU.add)
        stt(m.y[:, 1, t0:t0 + q], m.act[:, 3, t0:t0 + q], m.gpar[:, 1:2], yb[:, Q:Q + q], ALU.mult, ALU.add
            ).then_inc(S.y_evac, 1)
        if n > 0:
            dve.wait_ge(S.hdec_ready, 4 * g + n)
            if n == 1:
                wait(dve, S.hs_out, 16 * g)
            tt(hv(out), new, hv(m.hdec), ALU.add).then_inc(S.h_ready, 1)
        else:
            wait(dve, S.hp_out, 16 * g)
            cp(hv(out), new).then_inc(S.h_ready, 1)

    def gate(g):
        for j in range(2):
            s = (U_SSD + 4 + j) % 2
            dve.wait_ge(m.slot_evac[s], 3 * g + (slot_turn(U_SSD + 4 + j) + 1))
        dve.wait_ge(S.y_evac, 5 * g + 5)
        tt(m.y[:, :, :], m.y[:, :, :], m.zs[:, :, :], ALU.mult).then_inc(S.gate_ready, 1)

    def norm(g):
        dve.wait_ge(S.rms_ready, g + 1)
        dve.wait_ge(S.sq_ready, g + 1)
        for j in range(2):
            stt(m.y[:, j], m.y[:, j], m.gpar[:, 2 + j:3 + j], m.rms[:, :], ALU.mult, ALU.mult).then_inc(S.yn_f, 1)
        dve.wait_ge(S.yn_f, 2 * g + 2)
        at = slice(2 * g, 2 * g + 2) if isinstance(g, int) else bass.ds(2 * g, 2)
        cp(m.hh[:, at], m.y[:, :, :]).then_inc(S.yn_hi, 1)
        dve.wait_ge(S.yn_hi, g + 1)
        tt(m.hl[:, at], m.y[:, :, :], m.hh[:, at], ALU.subtract).then_inc(S.yn_lo, 1)

    def residual_first(u0, i, j, k=None):
        u = u0 + j
        s = u % 2
        k = 2 * i + j if k is None else k
        dve.wait_ge(S.gemm_done, 2 * i + (u + 1))
        stt(halves(one(m.r, k)), halves(one(m.xh, k).bitcast(F32)), ALPHA, bank_pair(m, s),
            ALU.mult, ALU.add).then_inc(m.slot_evac[s], 1)
        dve.wait_ge(m.slot_evac[s], i + (slot_turn(u) + 1))
        stt(one(m.r, k), one(m.xl, k).bitcast(F32), ALPHA, one(m.r, k), ALU.mult, ALU.add
            ).then_inc(S.res_ready, 1)

    def group(g, more):
        def nxt(j):
            if more:
                conv(g + 1, j)
            else:
                residual_first(U_WOUT, 0, j, j)

        before(g, 0)
        before(g, 1)
        operands(g, 0)
        operands(g, 1)
        if more:
            conv_params(g + 1)
        before(g, 2)
        after(g, 0)
        after(g, 1)
        operands(g, 2)
        nxt(0)
        before(g, 3)
        after(g, 2)
        operands(g, 3)
        nxt(1)
        before(g, 4)
        after(g, 3)
        operands(g, 4)
        nxt(2)
        after(g, 4)
        gate(g)
        nxt(3)
        if more:
            group_columns(g + 1)
        else:
            nxt(4)
        norm(g)
        if more:
            skip_params(g + 1)
        else:
            nxt(5)

    group(0, True)
    with dve.Fori(1, GROUPS - 1) as g:
        group(g, True)
    group(GROUPS - 1, False)

    def residual_add(u0, i, j, k=None):
        u = u0 + j
        s = u % 2
        r = halves(one(m.r, 2 * i + j if k is None else k))
        dve.wait_ge(S.gemm_done, 2 * i + (u + 1))
        dve.wait_ge(m.slot_evac[1 - s], i + (slot_turn(u - 1) + 1))
        tt(r, bank_pair(m, s), r, ALU.add).then_inc(m.slot_evac[s], 1)

    def block(u0, kind, n=0):
        if kind == "first":
            with dve.Fori(0, 4) as i:
                residual_first(u0, i, 0)
                residual_first(u0, i, 1)
        else:
            dve.wait_ge(S.res_ready, 8 * (n + 1))
            with dve.Fori(0, 4) as i:
                residual_add(u0, i, 0)
                residual_add(u0, i, 1)

    def sums(n, idx, j, s1, s2, tile, sq):
        wait(dve, S.sum1_ready, 10 * n + idx)
        tt(s1, s1, tile, ALU.add).then_inc(S.sum1_ready, 1)
        dve.wait_ge(S.sqr_ready, 10 * n + idx + 1)
        wait(dve, S.sum2_ready, 10 * n + idx)
        tt(s2, s2, sq, ALU.add).then_inc(S.sum2_ready, 1)

    def layer_norm(n, u0):
        dve.wait_ge(S.res_ready, 8 * (n + 1))
        dve.memset(m.s1[:, :, :], 0.0).then_inc(S.stat_zero, 1)
        dve.memset(m.s2[:, :, :], 0.0).then_inc(S.stat_zero, 1)
        dve.wait_ge(S.stat_zero, 2 * n + 2)
        for k in range(6):
            u = u0 + k
            residual_add(u, 0, 0, k)
            dve.wait_ge(m.slot_evac[u % 2], slot_turn(u) + 1)
            sums(n, k, k % 2, m.s1[:, :, :], m.s2[:, :, :], halves(m.r[:, k]), halves(m.sqm[:, k % 2]))

        def add_half(h, j):
            u = u0 + 6 + j
            s = u % 2
            r = half_of(m.r, 6 + j, h)
            if h == 0:
                dve.wait_ge(S.half_done, 2 * n + j + 1)
                tt(r, m.ps[:, 2 * s, 0:HT], r, ALU.add).then_inc(S.res_half, 1)
                dve.wait_ge(S.res_half, 2 * n + j + 1)
            else:
                dve.wait_ge(S.gemm_done, u + 1)
                tt(r, m.ps[:, 2 * s + 1, 0:HT], r, ALU.add).then_inc(m.slot_evac[s], 1)
                dve.wait_ge(m.slot_evac[s], slot_turn(u) + 1)
            sums(n, 6 + 2 * h + j, j, m.s1[:, h], m.s2[:, h], r, half_of(m.sqm, j, h))

        def variance(h):
            dve.wait_ge(S.msq_ready, 2 * n + h + 1)
            stt(m.msq[:, h], m.ps[:, 6 + h, 0:HT], 1.0 / D, m.msq[:, h], ALU.mult, ALU.subtract).then_inc(S.var_ready, 1)
            dve.wait_ge(S.var_ready, 4 * n + 2 * h + 1)
            ts(m.msq[:, h], m.msq[:, h], 0.0, None, ALU.max).then_inc(S.var_ready, 1)

        def scaled_mean(h):
            dve.wait_ge(S.rstd_ready, 2 * n + h + 1)
            stt(m.mr[:, h], m.ps[:, 4 + h, 0:HT], 1.0 / D, m.rstd[:, h], ALU.mult, ALU.mult).then_inc(S.mr_ready, 1)
            dve.wait_ge(S.mr_ready, 2 * n + h + 1)

        def tiles_normed(h, k0, k1):
            for k in range(k0, k1, 2):
                for kk in (k, k + 1):
                    q = 16 * n + 8 * h + kk
                    wait(dve, S.nrm_x, q - 3)
                    tt(m.na[:, kk % 4], half_of(m.r, kk, h), m.rstd[:, h], ALU.mult).then_inc(S.nrm_a, 1)
                for kk in (k, k + 1):
                    dve.wait_ge(S.nrm_a, 16 * n + 8 * h + kk + 1)
                    tt(m.na[:, kk % 4], m.na[:, kk % 4], m.mr[:, h], ALU.subtract).then_inc(S.nrm_b, 1)
                if n < 3 and h == 1 and k > 0:
                    x_lo(dve, m, n, 1, k - 2)

        add_half(0, 0)
        add_half(0, 1)
        add_half(1, 0)
        variance(0)
        scaled_mean(0)
        tiles_normed(0, 0, 2)
        add_half(1, 1)
        tiles_normed(0, 2, 6)
        variance(1)
        tiles_normed(0, 6, 8)
        scaled_mean(1)
        tiles_normed(1, 0, 8)
        if n < 3:
            x_lo(dve, m, n, 1, 6)

    def ffn(layer, u0):
        for b, (kind, c) in enumerate(FFN_BLOCKS):
            if kind == "up":
                with dve.Fori(0, 4) as i:
                    for j in range(2):
                        u = u0 + 8 * b + j
                        done = 32 * layer + 8 * c + j
                        dve.wait_ge(m.slot_evac[u % 2], i + (slot_turn(u) + 1))
                        if done >= 2:
                            dve.wait_ge(S.hid_lo, 2 * i + (done - 1))
                        tt(m.hq[:, j], m.rl[:, j], m.rl[:, j], ALU.mult).then_inc(S.hid_ready, 1)
                        dve.wait_ge(S.hid_hi, 2 * i + (done + 1))
                        k = 2 * i + (8 * (c % 2) + j)
                        tt(one(m.hl, k), m.hq[:, j], one(m.hh, k), ALU.subtract).then_inc(S.hid_lo, 1)
            elif c == 3:
                layer_norm(2 * layer + 1, u0 + 8 * b)
            else:
                block(u0 + 8 * b, "first" if c == 0 else "add", 2 * layer + 1)

    residual_first(U_WOUT + 6, 0, 0, 6)
    residual_first(U_WOUT + 6, 0, 1, 7)
    layer_norm(0, U_WOUT + 8)
    ffn(0, U_FFN0)

    wait_x(dve, m, 1, 1, 6)
    wait_x(dve, m, 1, 1, 7)
    dve.memset(m.v1[TS:P, :, 4, :], 0.0).then_inc(S.v_zero, 1)
    dve.wait_ge(S.gemm_done, U_V)
    v2 = m.v2[TS:P, :, 8 * T:8 * T + 4 * NTOK * P].rearrange("p a (m t c) -> p a m t c", t=NTOK, c=P)
    for a in range(2):
        dve.memset(v2[:, a, :, 4, :], 0.0).then_inc(S.v_zero, 1)
    dve.memset(m.vmv[:, :, :], 0.0).then_inc(S.v_zero, 1)
    dve.wait_ge(S.bb_in, 16)

    def v_bias(b, t):
        n = TS if t == 4 else P
        if t < 4:
            dve.wait_ge(S.v_done, 4 * b + (t + 1))
        else:
            dve.wait_ge(S.gemm_done, 4 * b + (U_V + 4))
        bank = m.ps[0:n, V_BANK[t], :]
        row = m.bb[0:n, bass.ds(512 * b, 512)] if not isinstance(b, int) else m.bb[0:n, 512 * b:512 * (b + 1)]
        tt(bank, bank, row, ALU.add).then_inc(S.v_bias, 1)

    for part in range(2):
        with dve.Fori(0, 2) as i:
            for t in range(NTOK):
                v_bias(i + 2 * part, t)
                if t > 0:
                    v_stats(dve, m, part, i, t - 1)
            v_stats(dve, m, part, i, NTOK - 1)
    dve.wait_ge(S.v_stat, 20)
    dve.wait_ge(S.v_zero, 4)
    for t in range(NTOK):
        n = TS if t == 4 else P
        dve.bn_aggr(m.vmv[0:n, t, :], m.vst[0:n, t, :, :].rearrange("p a b -> p (a b)")).then_inc(S.v_mv, 1)
    dve.wait_ge(S.v_rs, 1)
    dve.wait_ge(S.v_mv, NTOK)
    dve.wait_ge(S.gam_in, 16)
    dve.wait_ge(S.bet_in, 16)
    dve.wait_ge(S.bs_in, 16)

    def norm_v(k, kv, j):
        if not isinstance(k, int):
            dve.wait_ge(m.vrow_out[j], 8 * (k - j))
        for t in range(NTOK):
            src = m.v1[:, kv, t, :] if isinstance(kv, int) else m.v1[:, bass.ds(kv, 1), t, :].rearrange("p a c -> p (a c)")
            o = ts(m.vm[:, j, t, :], src, m.vmv[:, t, 0:1], m.vrs[:, t, 0:1], ALU.subtract, ALU.mult)
        o.then_inc(S.vm_n, 1)
        cut = (lambda x: x[:, k * P:(k + 1) * P]) if isinstance(k, int) else (lambda x: x[:, bass.ds(P * k, P)])
        dve.wait_ge(S.vm_n, k + 1)
        tt(m.vm[:, j], m.vm[:, j], repeat(cut(m.gam), NTOK), ALU.mult).then_inc(S.vm_g, 1)
        dve.wait_ge(S.vm_g, k + 1)
        tt(m.vm[:, j], m.vm[:, j], repeat(cut(m.bet), NTOK), ALU.add).then_inc(S.vm_ready, 1)

    def spatial_weights(g):
        cp(m.wsm[:, :], m.wst[:, g, :] if isinstance(g, int) else m.wst[:, bass.ds(g, 1), :].rearrange("p a c -> p (a c)")
           ).then_inc(S.wsm_ready, 1)

    def mix(i, j):
        row = m.bsb[:, bass.ds(i, 1), :].rearrange("p a c -> p (a c)") if not isinstance(i, int) else m.bsb[:, i, :]
        u = U_U + j
        dve.wait_ge(S.mix_done, 2 * i + (j + 1))
        tt(m.sb[:, j, 0:TP].rearrange("p (n t) -> p n t", t=BLK),
           m.ps[:, 4 + 2 * j, :].rearrange("p (n t) -> p n t", t=BLK), repeat(row, 4), ALU.add).then_inc(S.s_bias, 1)
        tt(m.sb[:, j, TP:T], m.ps[:, 5 + 2 * j, 0:TS], row[:, 0:TS], ALU.add).then_inc(S.s_bias, 1)
        dve.wait_ge(S.s_bias, 4 * i + (2 * j + 2))
        dve.wait_ge(m.slot_evac[u % 2], i + (slot_turn(u) + 1))
        tt(m.sb[:, j], m.sb[:, j], m.ug[:, j], ALU.mult).then_inc(S.uv_ready, 1)
        dve.wait_ge(S.uv_hi, 2 * i + (j + 1))
        k = 2 * i + j
        tt(one(m.hl, k), m.sb[:, j], one(m.hh, k), ALU.subtract).then_inc(S.uv_lo, 1)

    dve.wait_ge(S.ws_masked, 1)
    spatial_weights(0)
    norm_v(0, 0, 0)
    norm_v(1, 1, 1)
    with dve.Fori(0, 3) as i:
        mix(i, 0)
        norm_v(2 * i + 2, 2 * i + 2, 0)
        mix(i, 1)
        spatial_weights(i + 1)
        norm_v(2 * i + 3, 2 * i + 3, 1)
    dve.wait_ge(S.vm_ready, 8)
    for a in range(2):
        cp(m.v1[:, 4 * a:4 * a + 4].rearrange("p m t c -> p (m t c)"), m.v2[:, a, 8 * T:8 * T + 4 * NTOK * P]
           ).then_inc(S.v_moved, 1)
    dve.wait_ge(S.v_moved, 2)
    with dve.Fori(3, 7) as i:
        mix(i, 0)
        norm_v(2 * i + 2, 2 * i - 6, 0)
        mix(i, 1)
        spatial_weights(i + 1)
        norm_v(2 * i + 3, 2 * i - 5, 1)
    mix(7, 0)
    mix(7, 1)
    block(U_CMOUT, "first")
    for j in range(2):
        dve.wait_ge(m.vrow_out[j], 16 * 8)
    layer_norm(2, U_CMOUT + 8)
    ffn(1, U_FFN1)


def v_stats(dve, m, part, i, t):
    S = m.sem
    n = TS if t == 4 else P
    dve.wait_ge(S.v_gelu, 5 * i + (10 * part + t + 1))
    if part == 0:
        src = m.v1[0:n, bass.ds(4 * i, 4), t, :]
    else:
        src = m.v2[0:n, bass.ds(i, 1), 8 * T:8 * T + 4 * NTOK * P].rearrange(
            "p a (m t c) -> p (a m) t c", t=NTOK, c=P)[:, :, t, :]
    dst = m.vst[0:n, t, bass.ds(i + 2 * part, 1), :].rearrange("p a b -> p (a b)")
    dve.bn_stats(dst, src).then_inc(S.v_stat, 1)



def encoder_program(nc, A):
    with ExitStack() as ctx:
        m = Memory(nc, ctx)
        A = dict(A, acum=m.acum_dram)
        block = ctx.enter_context(nc.Block())

        @block.sync
        def _(eng):
            sync_program(eng, m, A)

        @block.gpsimd
        def _(eng):
            pool_program(eng, m, A)

        @block.scalar
        def _(eng):
            scalar_program(eng, m, A)

        @block.tensor
        def _(eng):
            tensor_program(eng, m, A)

        @block.vector
        def _(eng):
            vector_program(eng, m, A)



def stream_units(w):
    k, n = w.shape
    return w.reshape(k // UNIT, KT, P, n // P, P).transpose(0, 3, 2, 1, 4).reshape(-1, P, UNIT)


def tiles(v):
    return v.reshape(v.shape[:-1] + (-1, P)).transpose((len(v.shape),) + tuple(range(len(v.shape))))


def kernel(x_prompt, x_sample, state_ssm, state_conv, ssd_w_in, ssd_conv_w, ssd_conv_b, ssd_dt_bias, ssd_a_log, ssd_d,
           ssd_norm_w, ssd_w_out, cm_w_in, cm_b_in, cm_ln_g, cm_ln_b, cm_w_s, cm_b_s, cm_w_out, ffn_w1, ffn_w2,
           ln1_g, ln1_b, ln2_g, ln2_b):
    import numpy as np
    import concourse.bacc as bacc
    from concourse.bass_utils import run_bass_kernel_spmd

    f = np.ascontiguousarray
    di = 2 * D
    w_in = ssd_w_in[0]
    z, x, b, c = (stream_units(w_in[:, at:at + n]) for at, n in
                  ((0, di), (di, di), (2 * di, GROUPS * NST), (2 * di + GROUPS * NST, GROUPS * NST)))
    dt = stream_units(np.concatenate([w_in[:, -HEADS:]] * 4, axis=1))
    parts = [dt]
    for g in range(GROUPS):
        parts += [b[g:g + 1], c[g:g + 1], x[2 * g:2 * g + 2], z[2 * g:2 * g + 2]]
    parts.append(stream_units(ssd_w_out[0]))

    def ffn(layer):
        up, down = stream_units(ffn_w1[layer]), stream_units(ffn_w2[layer])
        return [(up if kind == "up" else down)[8 * k:8 * k + 8] for kind, k in FFN_BLOCKS]

    parts += ffn(0)
    v = cm_w_in[0][:, CMW:]
    parts.append(v.reshape(4, 2, P, 4, 512).transpose(3, 0, 2, 1, 4).reshape(16, P, UNIT))
    parts.append(stream_units(cm_w_in[0][:, :CMW]))
    parts.append(stream_units(cm_w_out[0]))
    parts += ffn(1)
    wstream = f(np.concatenate(parts))

    conv = np.concatenate([ssd_conv_w[0], ssd_conv_b], axis=0)
    by_tile = tiles(conv).transpose(0, 2, 1)
    conv_g = np.stack([by_tile[:, [16 + g, 24 + g, 2 * g, 2 * g + 1]] for g in range(GROUPS)], axis=1)
    skip = tiles(np.repeat(ssd_d[0], HD))
    grp = np.concatenate([skip.reshape(P, GROUPS, 2), tiles(ssd_norm_w[0]).reshape(P, GROUPS, 2)], axis=2)
    lns = np.stack([np.concatenate([tiles(a[i]), tiles(q[i])], axis=1)
                    for i in range(2) for a, q in ((ln1_g, ln1_b), (ln2_g, ln2_b))], axis=1)
    pv = f(np.concatenate([
        conv_g.reshape(P, -1), grp.reshape(P, -1), tiles(cm_b_in[0, :CMW]), lns.reshape(P, -1),
        np.concatenate([ssd_dt_bias[0]] * 4)[:, None], np.concatenate([ssd_a_log[0]] * 4)[:, None]], axis=1))
    assert pv.shape == (P, PV_N)

    halo = tiles(state_conv[0, 0]).transpose(0, 2, 1)
    halo = np.stack([halo[:, [16 + g, 24 + g, 2 * g, 2 * g + 1]] for g in range(GROUPS)], axis=1)
    xt = np.concatenate([x_prompt[0], x_sample[0]], axis=0)
    arrays = {
        "wstream": wstream,
        "x": f(xt.T.reshape(KT, P, T).transpose(1, 0, 2)),
        "pv": pv,
        "conv_halo": f(halo),
        "ssm_in": f(state_ssm[0, 0].transpose(2, 0, 1).reshape(NST, HEADS * HD)),
        "bias_v": f(cm_b_in[:, CMW:]),
        "ln_gain": f(cm_ln_g),
        "ln_bias": f(cm_ln_b),
        "w_spatial": f(cm_w_s[0].transpose(2, 0, 1)),
        "b_spatial": f(cm_b_s[0].reshape(1, -1)),
    }
    outs = {
        "y": (P, KT, T), "ssm_p": (NST, HEADS * HD), "ssm_s": (NST, HEADS * HD),
        "conv_tail": (P, GROUPS, 4, 2, HALO), "v_rows": (TS, 16, P),
    }
    nc = bacc.Bacc("TRN2", target_bir_lowering=False, num_devices=1)
    A = {n: nc.dram_tensor(n, a.shape, mybir.dt.from_np(a.dtype), kind="ExternalInput").ap() for n, a in arrays.items()}
    A.update({n: nc.dram_tensor("out_" + n, s, F32, kind="ExternalOutput").ap() for n, s in outs.items()})
    encoder_program(nc, A)
    got = run_bass_kernel_spmd(nc, [arrays], core_ids=[0]).results[0]

    y = got["out_y"].transpose(1, 0, 2).reshape(D, T).T
    tail = got["out_conv_tail"]
    rows = tail.transpose(3, 4, 1, 2, 0)
    xs = rows[:, :, :, 2:4].reshape(2, HALO, di)
    bs = rows[:, :, :, 0].reshape(2, HALO, -1)
    cs = rows[:, :, :, 1].reshape(2, HALO, -1)
    new_rows = np.concatenate([xs, bs, cs], axis=2)
    ssm = [got[n].reshape(NST, HEADS, HD).transpose(1, 2, 0)[None, None] for n in ("out_ssm_p", "out_ssm_s")]
    return (f(y[None, :TP]), f(y[None, TP:]), f(ssm[0]), f(new_rows[0][None, None]), f(ssm[1]), f(new_rows[1][None, None]),
            f(got["out_v_rows"].reshape(1, 1, TS, CMW)))
```

```python
from contextlib import ExitStack

import concourse.bass as bass
from concourse import mybir

F32 = mybir.dt.float32
F32R = mybir.dt.float32r
ALU = mybir.AluOpType
ACT = mybir.ActivationFunctionType

P = 128
D = 1024
KT = D // P
TP, TS = 512, 64
T = TP + TS
HT = T // 2
UNIT = 1024
RING = 4
HALO = 3
RAW = HALO + TP + HALO + TS
CONV = RAW - HALO
GROUPS, HPG, HD, NST = 8, 4, 64, 128
HEADS = GROUPS * HPG
Q = 128
NCH = 5
ALPHA = (2 * 2) ** 0.25
EPS = 1e-5
BLK = 128
NTOK = 5
V_BANK = [0, 2, 1, 3, 4]
CMW = 2048

U_SSD = 1
U_WOUT = U_SSD + 6 * GROUPS
U_FFN0 = U_WOUT + 16
U_V = U_FFN0 + 64
U_U = U_V + 16
U_CMOUT = U_U + 16
U_FFN1 = U_CMOUT + 16
UNITS = U_FFN1 + 64

PV_CONV = 0
PV_GRP = PV_CONV + GROUPS * 20
PV_BU = PV_GRP + GROUPS * 4
PV_LN = PV_BU + 16
PV_DTB = PV_LN + 4 * 16
PV_ALOG = PV_DTB + 1
PV_N = PV_ALOG + 1

DT_OUT = 7
DT_ACUM = 14
DT_STEPS = 15

ORDER = [0, 4, 1, 2, 3]


def cols(n):
    c = ORDER[n]
    return c * Q, (TS if c == 4 else Q)


def slot_turn(u):
    return (u if u < U_V else u - 16) // 2


FFN_BLOCKS = [("up", 0), ("up", 1), ("down", 0), ("up", 2), ("down", 1), ("up", 3), ("down", 2), ("down", 3)]


class Semaphores:

    def __init__(self, sem):
        self.tick_zero = sem("tick_zero")
        self.w_in0 = sem("w_in0")
        self.w_in1 = sem("w_in1")
        self.w_in2 = sem("w_in2")
        self.w_in3 = sem("w_in3")
        self.w_hi = sem("w_hi")
        self.w_ready = sem("w_ready")
        self.gemm_done = sem("gemm_done")
        self.slot_evac0 = sem("slot_evac0")
        self.slot_evac1 = sem("slot_evac1")
        self.x_in0 = sem("x_in0")
        self.x_in1 = sem("x_in1")
        self.x_in2 = sem("x_in2")
        self.x_in3 = sem("x_in3")
        self.pv_in = sem("pv_in")
        self.chalo_in = sem("chalo_in")
        self.x_hi = sem("x_hi")
        self.x_lo = sem("x_lo")
        self.consts = sem("consts")
        self.tokd_zero = sem("tokd_zero")
        self.raw_zero = sem("raw_zero")
        self.dt_act = sem("dt_act")
        self.dt_dve = sem("dt_dve")
        self.tok_t = sem("tok_t")
        self.tokd_ready = sem("tokd_ready")
        self.acum_out = sem("acum_out")
        self.acb_in = sem("acb_in")
        self.hs_in = sem("hs_in")
        self.hs_out = sem("hs_out")
        self.hp_out = sem("hp_out")
        self.cpar_ready = sem("cpar_ready")
        self.gdt_ready = sem("gdt_ready")
        self.skip_ready = sem("skip_ready")
        self.normw_ready = sem("normw_ready")
        self.win_arg = sem("win_arg")
        self.win_exp = sem("win_exp")
        self.dtw_ready = sem("dtw_ready")
        self.conv_tap = sem("conv_tap")
        self.silu_ready = sem("silu_ready")
        self.dec_arg = sem("dec_arg")
        self.dec_exp = sem("dec_exp")
        self.ea_ready = sem("ea_ready")
        self.s1_done = sem("s1_done")
        self.cbm_ready = sem("cbm_ready")
        self.xw_ready = sem("xw_ready")
        self.m_ready = sem("m_ready")
        self.s_done = sem("s_done")
        self.y_evac = sem("y_evac")
        self.yo_ready = sem("yo_ready")
        self.y_skip = sem("y_skip")
        self.hdec_ready = sem("hdec_ready")
        self.h_ready = sem("h_ready")
        self.gate_ready = sem("gate_ready")
        self.sq_ready = sem("sq_ready")
        self.sq_sum = sem("sq_sum")
        self.ms_done = sem("ms_done")
        self.ms_ln = sem("ms_ln")
        self.rms_ready = sem("rms_ready")
        self.yn_f = sem("yn_f")
        self.yn_hi = sem("yn_hi")
        self.yn_lo = sem("yn_lo")
        self.ctail_ready = sem("ctail_ready")
        self.tail_out = sem("tail_out")
        self.hid_ready = sem("hid_ready")
        self.hid_hi = sem("hid_hi")
        self.hid_lo = sem("hid_lo")
        self.res_ready = sem("res_ready")
        self.stat_zero = sem("stat_zero")
        self.sum1_ready = sem("sum1_ready")
        self.sqr_ready = sem("sqr_ready")
        self.sqr_b_ready = sem("sqr_b_ready")
        self.sum2_ready = sem("sum2_ready")
        self.stat_done = sem("stat_done")
        self.msq_ready = sem("msq_ready")
        self.var_ready = sem("var_ready")
        self.var_ln = sem("var_ln")
        self.rstd_ready = sem("rstd_ready")
        self.mr_ready = sem("mr_ready")
        self.nrm_a = sem("nrm_a")
        self.nrm_b = sem("nrm_b")
        self.nrm_b_pool = sem("nrm_b_pool")
        self.nrm_x = sem("nrm_x")
        self.nrm_f = sem("nrm_f")
        self.half_done = sem("half_done")
        self.res_half = sem("res_half")
        self.x_lo_pool = sem("x_lo_pool")
        self.y_out = sem("y_out")
        self.bb_in = sem("bb_in")
        self.gam_in = sem("gam_in")
        self.bet_in = sem("bet_in")
        self.ws_in = sem("ws_in")
        self.bs_in = sem("bs_in")
        self.ws_masked = sem("ws_masked")
        self.v_done = sem("v_done")
        self.v_bias = sem("v_bias")
        self.v_gelu = sem("v_gelu")
        self.v_stat = sem("v_stat")
        self.v_mv = sem("v_mv")
        self.v_ln = sem("v_ln")
        self.v_rs = sem("v_rs")
        self.v_zero = sem("v_zero")
        self.v_moved = sem("v_moved")
        self.wsm_ready = sem("wsm_ready")
        self.vm_n = sem("vm_n")
        self.vm_g = sem("vm_g")
        self.vm_ready = sem("vm_ready")
        self.vrow_out0 = sem("vrow_out0")
        self.vrow_out1 = sem("vrow_out1")
        self.mix_done = sem("mix_done")
        self.s_bias = sem("s_bias")
        self.uv_ready = sem("uv_ready")
        self.uv_hi = sem("uv_hi")
        self.uv_lo = sem("uv_lo")


class Memory:

    def __init__(self, nc, ctx):
        base = (nc.sbuf_base + 63) // 64 * 64
        end = nc.sbuf_usable_end
        self.at = base

        def put(name, shape, dt=F32, offset=None):
            n = 4
            for s in shape[1:]:
                n *= s
            where = self.at if offset is None else (offset + 31) // 32 * 32
            assert where + n <= end, (name, where + n - end)
            if offset is None:
                self.at += (n + 31) // 32 * 32
            return nc.alloc_sbuf_tensor_at(name, shape, dt, offset=where)

        self.xh = put("xh", [P, KT, T], F32R)
        self.xl = put("xl", [P, KT, T], F32R)
        h0 = self.at
        self.hh = put("hh", [P, 16, T], F32R)
        l0 = self.at
        self.hl = put("hl", [P, 16, T], F32R)
        w0 = self.at
        self.wraw = put("wraw", [P, RING, UNIT])
        self.wl = put("wl", [P, RING, UNIT], F32R, offset=w0)
        self.wh = put("wh", [P, RING, UNIT], F32R)
        self.pv = put("pv", [P, PV_N])
        self.ident = put("ident", [P, P])
        self.ones = put("ones", [P, P])
        self.causal = put("causal", [P, P])
        self.eps = put("eps", [P, 1])
        self.nega = put("nega", [P, 1])
        self.tick = put("tick", [P, 2])
        self.table_load = put("table_load", [P, 1])

        t0 = self.at

        self.raw = put("raw", [P, 2, RAW])
        self.acc = put("acc", [P, 4, CONV])
        self.act = put("act", [P, 4, T])
        self.zs = put("zs", [P, 2, T])
        self.acb = put("acb", [P, HPG, T])
        self.y = put("y", [P, 2, T])
        self.gy = put("gy", [P, 2, T])
        self.rms = put("rms", [P, T])
        self.eab = put("eab", [P, 2, T])
        self.elast = put("elast", [P, HPG, NCH])
        self.btok = put("btok", [P, 2, NST])
        self.cbm = put("cbm", [P, 2, Q])
        self.xdt = put("xdt", [P, 2, HPG * HD])
        self.xw = put("xw", [P, 2, HPG * HD])
        self.hp = put("hp", [P, HPG * HD])
        self.hs = put("hs", [P, HPG * HD])
        self.hsn = put("hsn", [P, HPG * HD])
        self.hdec = put("hdec", [P, HPG * HD])
        self.tokd = put("tokd", [P, NCH, 2 * HEADS])
        self.gdt = put("gdt", [P, NCH, HPG])
        self.gac = put("gac", [P, NCH, HPG])
        self.win = put("win", [P, NCH, HPG])
        self.dtw = put("dtw", [P, NCH, HPG])
        self.cpar = put("cpar", [P, 4, 5])
        self.skip = put("skip", [P, 2])
        self.normw = put("normw", [P, 2])
        self.ctail = put("ctail", [P, GROUPS, 4, 2, HALO])
        self.chalo = put("chalo", [P, GROUPS, 4, HALO])
        self.dec = put("dec", [P, 2, HPG, Q], offset=h0 + 14 * T * 4)
        self.yo = put("yo", [P, 2, 2, Q], offset=l0 + 14 * T * 4)
        self.xr = put("xr", [P, KT, T], offset=t0)
        self.dtt = put("dtt", [P, 8, T], offset=t0 + 2 * RAW * 4)

        row = T * 4
        self.r = put("r", [P, KT, T], offset=t0)
        self.rl = put("rl", [P, 2, T], offset=t0 + 8 * row)
        self.hq = put("hq", [P, 2, T], offset=t0 + 10 * row)
        self.s1 = put("s1", [P, 2, HT], offset=t0 + 12 * row)
        self.s2 = put("s2", [P, 2, HT], offset=t0 + 13 * row)
        self.msq = put("msq", [P, 2, HT], offset=t0 + 14 * row)
        self.rstd = put("rstd", [P, 2, HT], offset=t0 + 15 * row)
        self.mr = put("mr", [P, 2, HT], offset=t0 + 16 * row)
        self.na = put("na", [P, 4, HT], offset=t0 + 17 * row)
        self.xf = put("xf", [P, 4, HT], offset=t0 + 19 * row)
        self.sqm = put("sqm", [P, 2, T], offset=t0 + 21 * row)

        self.gam = put("gam", [P, CMW], offset=t0)
        self.bet = put("bet", [P, CMW], offset=t0 + CMW * 4)
        g0 = t0 + 8 * row
        vrow = NTOK * P * 4
        self.v1 = put("v1", [P, 8, NTOK, P], offset=g0)
        self.v2 = put("v2", [P, 2, 16 * T], offset=h0)
        self.bb = put("bb", [P, CMW], offset=l0)
        g0 += 8 * vrow
        self.vm = put("vm", [P, 2, NTOK, P], offset=g0)
        g0 += 2 * vrow
        self.wsm = put("wsm", [P, BLK], offset=g0)
        g0 += BLK * 4
        self.wst = put("wst", [P, 8, BLK], offset=g0)
        g0 += 8 * BLK * 4
        self.bsb = put("bsb", [P, 8, BLK], offset=g0)
        g0 += 8 * BLK * 4
        self.ug = put("ug", [P, 2, T], offset=g0)
        g0 += 2 * row
        self.sb = put("sb", [P, 2, T], offset=g0)
        g0 += 2 * row
        self.vst = put("vst", [P, NTOK, 4, 6], offset=g0)
        g0 += NTOK * 4 * 6 * 4
        self.vmv = put("vmv", [P, NTOK, 2], offset=g0)
        g0 += 64
        self.vrs = put("vrs", [P, NTOK, 1], offset=g0)

        self.ps = ctx.enter_context(nc.psum_tensor("ps", [P, 8, 512], F32))
        self.acum_dram = nc.dram_tensor("acum_scratch", [HEADS, T], F32).ap()

        self.sem = S = Semaphores(lambda name: ctx.enter_context(nc.semaphore(name)))
        self.w_in = [S.w_in0, S.w_in1, S.w_in2, S.w_in3]
        self.slot_evac = [S.slot_evac0, S.slot_evac1]
        self.x_in = [S.x_in0, S.x_in1, S.x_in2, S.x_in3]
        self.vrow_out = [S.vrow_out0, S.vrow_out1]


def wait(engine, sem, value):
    if not isinstance(value, int) or value > 0:
        engine.wait_ge(sem, value)


def one(t, i):
    if isinstance(i, int):
        return t[:, i]
    v = t[:, bass.ds(i, 1)]
    if len(v.shape) == 3:
        return v.rearrange("p a t -> p (a t)")
    if len(v.shape) == 4:
        return v.rearrange("p a b t -> p (a b) t")
    return v.rearrange("p a b c t -> p (a b) c t")


def wait_x(engine, m, n, h, k):
    engine.wait_ge(m.sem.x_lo_pool, 16 * n + 8 * h + k + 1)


def half_of(t, k, h):
    return t[:, k, h * HT:(h + 1) * HT]


def affine_by_act(n, h, k):
    return (h == 1 or k >= 4) if n == 3 else (h == 1 and k % 2 == 0)


def wait_affine(engine, m, n, h, k):
    by_act = affine_by_act(n, h, k)
    if n < 3:
        engine.wait_ge(m.sem.nrm_x, 16 * n + 8 * h + k + 1)
    elif by_act:
        engine.wait_ge(m.sem.nrm_x, 16 * 3 + 8 * h + k - 3)
    if not by_act:
        engine.wait_ge(m.sem.nrm_f, 12 * n + (k + 1 if h == 0 else 8 + (k + 1) // 2))


def wait_centred(engine, m, n, h, k):
    if n < 3 or k % 2 == 0:
        engine.wait_ge(m.sem.nrm_b, 8 * n + 4 * h + k // 2 + 1)
    else:
        engine.wait_ge(m.sem.nrm_b_pool, 4 * h + (k + 1) // 2)


def wait_xf_slot(engine, m, n, h, k):
    if (n, h) != (0, 0) or k >= 4:
        wait_x(engine, m, *four_before(n, h, k))


def four_before(n, h, k):
    return (n, h, k - 4) if k >= 4 else (n, 0, k + 4) if h else (n - 1, 1, k + 4)


def gain_and_bias(m, n, k):
    at = PV_LN + 16 * n + k
    return m.pv[:, at:at + 1], m.pv[:, at + 8:at + 9]


def state_out(m, n):
    if n == 1:
        return m.ps[:, 5, :].rearrange("p (h a) -> p h a", a=2 * HD)[:, :, HD:]
    return m.ps[:, 7, 0:HPG * HD].rearrange("p (h d) -> p h d", d=HD)


def halves(ap):
    return ap.rearrange("p (h t) -> p h t", h=2)


def bank_pair(m, s):
    return m.ps[:, 2 * s:2 * s + 2, 0:HT]


def spread(ap, n):
    return ap.unsqueeze(2).to_broadcast([ap.shape[0], ap.shape[1], n])


def repeat(ap, n):
    return ap.unsqueeze(1).to_broadcast([ap.shape[0], n, ap.shape[1]])



def sync_program(sp, m, A):
    S = m.sem
    sp.dma_start(m.wraw[:, 0], A["wstream"][0]).then_inc(m.w_in[0], 16)
    for n in range(4):
        sp.dma_start(m.xr[:, 2 * n:2 * n + 2], A["x"][:, 2 * n:2 * n + 2]).then_inc(m.x_in[n], 16)
        if n == 2:
            sp.dma_start(m.wraw[:, 1], A["wstream"][1]).then_inc(m.w_in[1], 16)
    for u in range(2, RING):
        sp.dma_start(m.wraw[:, u], A["wstream"][u]).then_inc(m.w_in[u], 16)

    def load(u, s):
        sp.wait_ge(S.gemm_done, u - 3)
        src = A["wstream"][u] if isinstance(u, int) else A["wstream"][bass.ds(u, 1)].rearrange("a p n -> p (a n)")
        sp.dma_start(m.wraw[:, s], src).then_inc(m.w_in[s], 16)

    with sp.Fori(0, (UNITS - 1) // RING - 1) as i:
        for s in range(RING):
            load(4 * i + (RING + s), s)
    load(UNITS - 1, 0)
    for h in range(2):
        for k in range(0, KT, 2):
            wait_affine(sp, m, 3, h, k)
            wait_affine(sp, m, 3, h, k + 1)
            sp.dma_start(A["y"][:, k:k + 2, h * HT:(h + 1) * HT], m.r[:, k:k + 2, h * HT:(h + 1) * HT]).then_inc(S.y_out, 16)
    sp.wait_ge(S.y_out, 16 * 8)
    for j in range(2):
        sp.wait_ge(m.vrow_out[j], 16 * 8)
    sp.wait_ge(S.tail_out, 16)
    sp.wait_ge(S.hs_out, 16 * GROUPS)
    sp.wait_ge(S.hp_out, 16 * GROUPS)
    sp.wait_ge(S.acum_out, 16)



def pool_program(pool, m, A):
    S = m.sem

    def split(u, s, arrived):
        pool.wait_ge(m.w_in[s], arrived)
        pool.tensor_tensor(m.tick[:, 1:2], m.tick[:, 0:1], m.tick[:, 0:1], ALU.add)
        pool.tensor_scalar(m.wh[:, s], m.wraw[:, s], 1.0, 1.0, ALU.mult, ALU.mult).then_inc(S.w_hi, 1)
        pool.wait_ge(S.w_hi, u + 1)
        pool.tensor_tensor(m.wl[:, s], m.wraw[:, s], m.wh[:, s], ALU.subtract).then_inc(S.w_ready, 1)

    def split_one(u):
        split(u, u % RING, 16 * (u // RING + 1))

    def run(u0, n):
        with pool.Fori(0, n) as i:
            for j in range(RING):
                u = u0 + j
                split(4 * i + u, u % RING, 16 * i + 16 * (u // RING + 1))

    def square_b6(n, u0):
        u = u0 + 6
        pool.wait_ge(m.slot_evac[u % 2], slot_turn(u) + 1)
        pool.wait_ge(S.sum2_ready, 10 * n + 5)
        r = half_of(m.r, 6, 1)
        pool.tensor_tensor(half_of(m.sqm, 0, 1), r, r, ALU.mult).then_inc(S.sqr_b_ready, 1)

    def x_lo(n, h, k):
        wait_affine(pool, m, n, h, k)
        pool.tensor_tensor(half_of(m.xl, k, h), m.xf[:, k % 4], half_of(m.xh, k, h), ALU.subtract
                           ).then_inc(S.x_lo_pool, 1)

    def norm(n, u0):
        split_one(u0)
        split_one(u0 + 1)
        square_b6(n, u0 - 8)
        split_one(u0 + 2)
        for k in range(KT):
            if n == 1 and k == 4:
                split_one(u0 + 3)
            x_lo(n, 0, k)
        for k in range(KT):
            x_lo(n, 1, k)
        if n != 1:
            split_one(u0 + 3)

    pool.memset(m.tick[:, :], 0.0).then_inc(S.tick_zero, 1)
    pool.wait_ge(S.tick_zero, 1)
    pool.memset(m.ident[:, :], 0.0).then_inc(S.consts, 1)
    pool.memset(m.causal[:, :], 1.0).then_inc(S.consts, 1)
    pool.memset(m.ones[:, :], 1.0).then_inc(S.consts, 1)
    pool.memset(m.eps[:, :], EPS).then_inc(S.consts, 1)
    pool.memset(m.tokd[:, NCH - 1, :], 0.0).then_inc(S.tokd_zero, 1)
    pool.wait_ge(S.consts, 2)
    pool.affine_select(out=m.ident[:, :], in_=m.ident[:, :], compare_op=ALU.not_equal, fill=1.0, base=0,
                       pattern=[[-1, P]], channel_multiplier=1).then_inc(S.consts, 1)
    pool.affine_select(out=m.causal[:, :], in_=m.causal[:, :], compare_op=ALU.is_ge, fill=0.0, base=0,
                       pattern=[[1, P]], channel_multiplier=-1).then_inc(S.consts, 1)
    pool.wait_ge(S.w_ready, 1)
    run(1, (U_FFN0 - 1) // RING)
    norm(0, U_FFN0)
    run(U_FFN0 + 4, (U_V - U_FFN0) // RING - 1)
    norm(1, U_V)
    run(U_V + 4, 1)
    pool.wait_ge(S.ws_in, 16)
    pool.affine_select(out=m.wst[:, :, :], in_=m.wst[:, :, :], compare_op=ALU.is_ge, fill=0.0, base=0,
                       pattern=[[0, 8], [1, BLK]], channel_multiplier=-1).then_inc(S.ws_masked, 1)
    run(U_V + 8, (U_FFN1 - U_V) // RING - 2)
    norm(2, U_FFN1)
    run(U_FFN1 + 4, (UNITS - U_FFN1) // RING - 1)
    square_b6(3, UNITS - 8)
    for h in range(2):
        pool.wait_ge(S.mr_ready, 2 * 3 + h + 1)
        for k in range(1, KT, 2):
            pool.wait_ge(S.nrm_a, 8 * 3 + 4 * h + k // 2 + 1)
            pool.tensor_tensor(m.na[:, k % 4], m.na[:, k % 4], m.mr[:, h], ALU.subtract).then_inc(S.nrm_b_pool, 1)



def tensor_program(pe, m, A):
    S = m.sem
    mm = pe.matmul

    def products(out, w, k, x, start, stop):
        w_hi, w_lo = m.wh[:, w, k * P:(k + 1) * P], m.wl[:, w, k * P:(k + 1) * P]
        mm(out, w_hi, x[0], start=start, stop=False)
        mm(out, w_hi, x[1], start=False, stop=False)
        return mm(out, w_lo, x[0], start=False, stop=stop)

    def unit(u, w, turn, xh, xl, each=None):
        s = w % 2
        pe.wait_ge(S.w_ready, u + 1)
        wait(pe, m.slot_evac[s], turn)
        steps = [(h, k) for h in range(2) for k in range(KT)] if each is None else \
            [(h, k) for k in range(KT) for h in range(2)]
        for h, k in steps:
            if each is not None and h == 0:
                each(k)
            last = products(m.ps[:, 2 * s + h, 0:HT], w, k, (half_of(xh, k, h), half_of(xl, k, h)), k == 0, k == KT - 1)
        last.then_inc(S.gemm_done, 1)

    def run_few(u0, n, xh, xl):
        for u in range(u0, u0 + n):
            unit(u, u % RING, slot_turn(u), xh, xl)

    def run(u0, n, xh, xl):
        with pe.Fori(0, n) as i:
            for j in range(RING):
                unit(4 * i + (u0 + j), (u0 + j) % RING, 2 * i + slot_turn(u0 + j), xh, xl)

    def layer_norm_sums(n, h):
        pe.wait_ge(S.sum1_ready, 10 * n + 8 + 2 * h)
        mm(m.ps[:, 4 + h, 0:HT], m.ones[:, :], m.s1[:, h], start=True, stop=True)
        pe.wait_ge(S.sum2_ready, 10 * n + 8 + 2 * h)
        mm(m.ps[:, 6 + h, 0:HT], m.ones[:, :], m.s2[:, h], start=True, stop=True).then_inc(S.stat_done, 1)

    def last_block(n, u0, xh, xl):
        run_few(u0, 6, xh, xl)
        for h in range(2):
            for u in (u0 + 6, u0 + 7):
                s = u % 2
                if h == 0:
                    pe.wait_ge(S.w_ready, u + 1)
                    pe.wait_ge(m.slot_evac[s], slot_turn(u))
                for k in range(KT):
                    if (h, u, k) == (1, u0 + 6, 6):
                        layer_norm_sums(n, 0)
                    last = products(m.ps[:, 2 * s + h, 0:HT], u % RING, k, (half_of(xh, k, h), half_of(xl, k, h)),
                                    k == 0, k == KT - 1)
                last.then_inc(S.gemm_done if h else S.half_done, 1)

    def first_pair(n, u0):
        layer_norm_sums(n, 1)
        for h in range(2):
            for k in range(KT):
                wait_x(pe, m, n, h, k)
                for u in (u0, u0 + 1):
                    s = u % 2
                    if k == 0:
                        pe.wait_ge(S.w_ready, u + 1)
                        if h == 1:
                            pe.wait_ge(m.slot_evac[s], slot_turn(u))
                    last = products(m.ps[:, 2 * s + h, 0:HT], u % RING, k, (half_of(m.xh, k, h), half_of(m.xl, k, h)),
                                    k == 0, k == KT - 1)
                    if h == 1 and k == KT - 1:
                        last.then_inc(S.gemm_done, 1)

    unit(0, 0, 0, m.xh, m.xl, each=lambda k: pe.wait_ge(S.x_lo, k + 1))
    run_few(1, 5, m.xh, m.xl)
    pe.wait_ge(S.dt_dve, DT_STEPS)
    pe.wait_ge(S.consts, 6)
    for c in range(NCH):
        n = TS if c == 4 else Q
        last = pe.transpose(m.ps[0:n, 4 + c // 4, (c % 4) * P:(c % 4) * P + P],
                            m.dtt[:, DT_OUT, c * Q:c * Q + n], m.ident[:, :])
    last.then_inc(S.tok_t, 1)
    run_few(6, 1, m.xh, m.xl)

    def chunk_in(g, n):
        t0, q = cols(n)
        b = m.ps[:, 4 + n % 2, :]
        if n == 0:
            pe.wait_ge(S.silu_ready, 4 * g + 4)
            pe.wait_ge(S.tokd_ready, 2)
        if n in (2, 4):
            pe.wait_ge(S.xw_ready, 5 * g + (n - 1))
        if n == 3:
            pe.wait_ge(S.h_ready, 5 * g + 2)
        mm(b[0:q, 0:q], m.act[:, 0, t0:t0 + q], m.act[:, 1, t0:t0 + q], start=True, stop=True)
        for j, tile in enumerate((0, 2, 3)):
            last = pe.transpose(b[0:q, (j + 1) * P:(j + 2) * P], m.act[:, tile, t0:t0 + q], m.ident[:, :])
        last.then_inc(S.s1_done, 1)

    def chunk_out(g, n):
        t0, q = cols(n)
        k = n % 2
        yb = m.ps[:, 5 if n == 1 else 6, :]
        h = m.hs if n == 1 else m.hp
        state = state_out(m, n)
        pe.wait_ge(S.m_ready, 5 * g + (n + 1))
        if n == 0:
            wait(pe, S.h_ready, 5 * g)
            wait(pe, S.ms_ln, g)
        if n >= 2:
            pe.wait_ge(S.h_ready, 5 * g + n)
        if n == 1:
            pe.wait_ge(S.hs_in, 16 * g + 16)
        mm(state, m.btok[0:q, k, :], m.xw[0:q, k, :].rearrange("p (h d) -> p h d", d=HD), start=True, stop=True)
        for j in range(2):
            for p in range(2):
                e = 2 * j + p
                last = mm(yb[p * HD:(p + 1) * HD, j * Q:j * Q + q], m.xdt[0:q, k, e * HD:(e + 1) * HD],
                          m.dec[0:q, k, e, 0:q], start=True, stop=True)
            if n > 0:
                last = mm(yb[:, (2 + j) * Q:(2 + j) * Q + q], h[:, j * P:(j + 1) * P], m.act[:, 1, t0:t0 + q],
                          start=True, stop=True)
        last.then_inc(S.s_done, 1)

    def mean_squares(g):
        pe.wait_ge(S.sq_sum, g + 1)
        for h in range(2):
            last = mm(m.ps[:, 6 + h, 0:HT], m.ones[:, :], m.y[:, 0, h * HT:(h + 1) * HT], start=True, stop=True)
        last.then_inc(S.ms_done, 1)

    def group(g, even, first=False, last=False):
        def nxt(j):
            if last:
                run_few(U_WOUT + j, 1, m.hh[:, 0:8], m.hl[:, 0:8])
            else:
                u0 = U_SSD + 6 + j
                unit(6 * g + u0, (u0 + (0 if even else 6)) % RING, 3 * g + slot_turn(u0), m.xh, m.xl)

        chunk_in(g, 0)
        if not first:
            mean_squares(g - 1)
        chunk_in(g, 1)
        nxt(0)
        chunk_out(g, 0)
        chunk_out(g, 1)
        chunk_in(g, 2)
        nxt(1)
        chunk_out(g, 2)
        chunk_in(g, 3)
        nxt(2)
        chunk_out(g, 3)
        chunk_in(g, 4)
        nxt(3)
        chunk_out(g, 4)
        nxt(4)
        if last:
            mean_squares(g)
        nxt(5)

    group(0, True, first=True)
    with pe.Fori(0, (GROUPS - 2) // 2) as i:
        group(2 * i + 1, False)
        group(2 * i + 2, True)
    pe.wait_ge(S.yn_lo, GROUPS // 2)
    group(GROUPS - 1, False, last=True)
    run_few(U_WOUT + 6, 2, m.hh[:, 0:8], m.hl[:, 0:8])
    pe.wait_ge(S.yn_lo, GROUPS)
    last_block(0, U_WOUT + 8, m.hh[:, 8:16], m.hl[:, 8:16])

    def ffn(layer, u0):
        n = 2 * layer
        first_pair(n, u0)
        run_few(u0 + 2, 2, m.xh, m.xl)
        run(u0 + 4, 3, m.xh, m.xl)
        for b, (kind, c) in enumerate(FFN_BLOCKS):
            k = 8 * (c % 2)
            if kind == "down":
                pe.wait_ge(S.hid_lo, 32 * layer + 8 * (c + 1))
                if c == 3:
                    last_block(n + 1, u0 + 8 * b, m.hh[:, k:k + 8], m.hl[:, k:k + 8])
                else:
                    run(u0 + 8 * b, 2, m.hh[:, k:k + 8], m.hl[:, k:k + 8])
            elif b > 1:
                run(u0 + 8 * b, 2, m.xh, m.xl)

    ffn(0, U_FFN0)

    def v_products(t, kp, kk):
        n = TS if t == 4 else P
        s, k = (U_V + kp) % RING, 2 * kp + kk
        out = m.ps[0:n, V_BANK[t], :]
        x_hi, x_lo = m.xh[:, k, t * P:t * P + n], m.xl[:, k, t * P:t * P + n]
        w_hi, w_lo = m.wh[:, s, kk * 512:kk * 512 + 512], m.wl[:, s, kk * 512:kk * 512 + 512]
        mm(out, x_hi, w_hi, start=(k == 0), stop=False)
        mm(out, x_hi, w_lo, start=False, stop=False)
        return mm(out, x_lo, w_hi, start=False, stop=(k == KT - 1))

    def v_first():
        layer_norm_sums(1, 1)
        for tiles_of in ((0, 1), (2, 3, 4)):
            h = 0 if tiles_of[0] == 0 else 1
            for k in range(KT):
                wait_x(pe, m, 1, h, k)
                pe.wait_ge(S.w_ready, U_V + k // 2 + 1)
                for t in tiles_of:
                    last = v_products(t, k // 2, k % 2)
                    if t == 4 and k % 2:
                        last.then_inc(S.gemm_done, 1)
                    elif t < 4 and k == KT - 1:
                        last.then_inc(S.v_done, 1)

    def v_block(b):
        for kp in range(4):
            pe.wait_ge(S.w_ready, 4 * b + (U_V + kp + 1))
            for t in range(NTOK):
                if kp == 0:
                    pe.wait_ge(S.v_gelu, 5 * b + (t - 4))
                for kk in range(2):
                    last = v_products(t, kp, kk)
                if kp == 3 and t < 4:
                    last.then_inc(S.v_done, 1)
            last.then_inc(S.gemm_done, 1)

    v_first()
    with pe.Fori(1, 4) as b:
        v_block(b)

    pe.wait_ge(S.v_gelu, 5 * 3 + 4)
    with pe.Fori(0, 4) as i:
        for n in range(4):
            u, j = U_U + n, n % 2
            unit(4 * i + u, u % RING, 2 * i + slot_turn(u), m.xh, m.xl)
            pe.wait_ge(S.wsm_ready, 2 * i + (n // 2 + 1))
            pe.wait_ge(S.vm_ready, 4 * i + (n + 1))
            for t in range(4):
                mm(m.ps[:, 4 + 2 * j, t * BLK:(t + 1) * BLK], m.vm[:, j, t, :], m.wsm[:, :], start=True, stop=True)
            mm(m.ps[:, 5 + 2 * j, 0:TS], m.vm[0:TS, j, 4, :], m.wsm[0:TS, 0:TS],
               start=True, stop=True).then_inc(S.mix_done, 1)
    pe.wait_ge(S.uv_lo, 8)
    run(U_CMOUT, 2, m.hh[:, 0:8], m.hl[:, 0:8])
    pe.wait_ge(S.uv_lo, 16)
    last_block(2, U_CMOUT + 8, m.hh[:, 8:16], m.hl[:, 8:16])
    ffn(1, U_FFN1)
    layer_norm_sums(3, 1)



def scalar_program(act, m, A):
    S = m.sem
    f = act.activation

    act.dma_start(m.pv[:, :], A["pv"]).then_inc(S.pv_in, 16)
    act.dma_start(m.chalo[:, :, :, :], A["conv_halo"]).then_inc(S.chalo_in, 16)
    act.wait_ge(m.w_in[0], 16)
    f(m.wh[:, 0], m.wraw[:, 0], ACT.Copy).then_inc(S.w_hi, 1)
    for k in range(KT):
        act.wait_ge(m.x_in[k // 2], 16)
        f(m.xh[:, k], m.xr[:, k], ACT.Copy).then_inc(S.x_hi, 1)
    act.wait_ge(S.pv_in, 16)
    f(m.nega[:, :], m.pv[:, PV_ALOG:PV_ALOG + 1], ACT.Exp).then_inc(S.dt_act, 1)
    act.wait_ge(m.slot_evac[0], 1)
    f(m.dtt[:, 1], m.dtt[:, 0], ACT.Abs).then_inc(S.dt_act, 1)
    act.wait_ge(S.dt_act, 2)
    f(m.dtt[:, 2], m.dtt[:, 1], ACT.Exp, scale=-1.0).then_inc(S.dt_act, 1)
    act.wait_ge(S.dt_dve, 2)
    f(m.dtt[:, 4], m.dtt[:, 3], ACT.Ln).then_inc(S.dt_act, 1)

    def raw_tile(g, j, u):
        s = u % 2 if isinstance(u, int) else (U_SSD + j) % 2
        k = j % 2
        act.wait_ge(S.gemm_done, u + 1)
        wait(act, S.conv_tap, 16 * g + 4 * (j - 1))
        r = m.raw[:, k]
        halo = m.chalo[:, g, j] if isinstance(g, int) else m.chalo[:, bass.ds(g, 1), j].rearrange("p a c -> p (a c)")
        f(r[:, HALO + TP:2 * HALO + TP], halo, ACT.Copy)
        f(r[:, HALO:HALO + HT], m.ps[:, 2 * s, 0:HT], ACT.Copy)
        f(r[:, HALO + HT:HALO + TP], m.ps[:, 2 * s + 1, 0:TP - HT], ACT.Copy)
        f(r[:, 2 * HALO + TP:RAW], m.ps[:, 2 * s + 1, TP - HT:HT], ACT.Copy).then_inc(m.slot_evac[s], 1)

    def silu_z(g, j, u):
        s = (U_SSD + 4 + j) % 2
        act.wait_ge(S.gemm_done, u + 1)
        wait(act, S.gate_ready, g)
        f(halves(m.zs[:, j]), bank_pair(m, s), ACT.Silu).then_inc(m.slot_evac[s], 1)

    def silu_conv(g):
        wait(act, S.h_ready, 5 * g)
        for b in range(2):
            act.wait_ge(S.conv_tap, 16 * g + (8 * b + 8))
            f(m.act[:, 2 * b:2 * b + 2, 0:TP], m.acc[:, 2 * b:2 * b + 2, 0:TP], ACT.Silu).then_inc(S.silu_ready, 1)
            f(m.act[:, 2 * b:2 * b + 2, TP:T], m.acc[:, 2 * b:2 * b + 2, TP + HALO:CONV],
              ACT.Silu).then_inc(S.silu_ready, 1)

    def load_group(g):
        rows = A["acum"][4 * g:4 * g + 4] if isinstance(g, int) else A["acum"][bass.ds(4 * g, 4)]
        wait(act, S.dec_arg, 5 * g)
        act.dma_start(m.acb[:, :, :], rows.unsqueeze(0).to_broadcast([P, HPG, T])).then_inc(S.acb_in, 16)
        wait(act, S.h_ready, 5 * g - 3)
        src = A["ssm_in"][:, bass.ds(HPG * HD * g, HPG * HD)] if not isinstance(g, int) else \
            A["ssm_in"][:, HPG * HD * g:HPG * HD * (g + 1)]
        act.dma_start(m.hs[:, :], src).then_inc(S.hs_in, 16)

    def exp_acum(g):
        act.wait_ge(S.acb_in, 16 * g + 16)
        wait(act, S.h_ready, 5 * g)
        for p in range(2):
            at = slice(p * HD, (p + 1) * HD)
            f(m.eab[at, :, :], m.acb[at, :, :].rearrange("p (j e) t -> p e j t", e=2)[:, p], ACT.Exp)
        f(m.elast[:, :, 0:4], m.acb[:, :, 0:TP].rearrange("p h (c q) -> p h c q", q=Q)[:, :, :, Q - 1], ACT.Exp)
        f(m.elast[:, :, 4], m.acb[:, :, T - 1], ACT.Exp).then_inc(S.ea_ready, 1)

    def exp_win(g):
        act.wait_ge(S.win_arg, 2 * g + 2)
        f(m.win[:, :, :], m.win[:, :, :], ACT.Exp).then_inc(S.win_exp, 1)

    def exp_decay(g, n):
        q = cols(n)[1]
        act.wait_ge(S.dec_arg, 5 * g + (n + 1))
        f(m.dec[0:q, n % 2, :, 0:q], m.dec[0:q, n % 2, :, 0:q], ACT.Exp).then_inc(S.dec_exp, 1)

    def rms(g):
        act.wait_ge(S.ms_done, g + 1)
        wait(act, S.yn_f, 2 * g)
        f(halves(m.rms[:, :]), m.ps[:, 6:8, 0:HT], ACT.Ln, bias=m.eps[:, :], scale=1.0 / (HPG * HD)).then_inc(S.ms_ln, 1)
        act.wait_ge(S.ms_ln, g + 1)
        f(m.rms[:, :], m.rms[:, :], ACT.Exp, scale=-0.5).then_inc(S.rms_ready, 1)

    def round_y(g):
        at = slice(2 * g, 2 * g + 2) if isinstance(g, int) else bass.ds(2 * g, 2)
        act.wait_ge(S.yn_f, 2 * g + 2)
        f(m.hh[:, at], m.gy[:, :, :], ACT.Copy).then_inc(S.yn_hi, 1)

    act.wait_ge(S.x_lo, KT)
    act.wait_ge(S.chalo_in, 16)
    for j in range(4):
        raw_tile(0, j, U_SSD + j)
    act.wait_ge(S.dt_dve, DT_ACUM)
    act.dma_start(A["acum"], m.dtt[32:64, DT_OUT, :]).then_inc(S.acum_out, 16)
    act.wait_ge(S.acum_out, 16)
    load_group(0)
    act.wait_ge(S.consts, 6)
    exp_win(0)
    silu_z(0, 0, U_SSD + 4)
    act.wait_ge(S.tok_t, 1)
    silu_conv(0)
    silu_z(0, 1, U_SSD + 5)

    def group(g, more, first=False):
        if not first:
            exp_win(g)
        exp_decay(g, 0)
        exp_decay(g, 1)
        if not first:
            rms(g - 1)
        exp_acum(g)
        for n in range(2, 5):
            if more:
                raw_tile(g + 1, n - 2, 6 * g + (U_SSD + 4 + n))
            exp_decay(g, n)
            if n == 3 and not first:
                round_y(g - 1)
        if more:
            load_group(g + 1)
        dst = A["ssm_s"][:, bass.ds(HPG * HD * g, HPG * HD)] if not isinstance(g, int) else \
            A["ssm_s"][:, HPG * HD * g:HPG * HD * (g + 1)]
        act.wait_ge(S.h_ready, 5 * g + 2)
        act.dma_start(dst, m.hsn[:, :]).then_inc(S.hs_out, 16)
        if more:
            raw_tile(g + 1, 3, 6 * g + (U_SSD + 9))
        dst = A["ssm_p"][:, bass.ds(HPG * HD * g, HPG * HD)] if not isinstance(g, int) else \
            A["ssm_p"][:, HPG * HD * g:HPG * HD * (g + 1)]
        act.wait_ge(S.h_ready, 5 * g + 5)
        act.dma_start(dst, m.hp[:, :]).then_inc(S.hp_out, 16)
        act.wait_ge(S.gate_ready, g + 1)
        f(m.y[:, :, :], m.gy[:, :, :], ACT.Square).then_inc(S.sq_ready, 1)
        if more:
            silu_conv(g + 1)
            silu_z(g + 1, 0, 6 * g + (U_SSD + 10))
            silu_z(g + 1, 1, 6 * g + (U_SSD + 11))

    group(0, True, first=True)
    with act.Fori(1, GROUPS - 1) as g:
        group(g, True)
    group(GROUPS - 1, False)
    rms(GROUPS - 1)
    round_y(GROUPS - 1)
    act.wait_ge(S.ctail_ready, 2 * 4 * GROUPS)
    act.dma_start(A["conv_tail"], m.ctail[:, :, :, :, :]).then_inc(S.tail_out, 16)

    def square(n, idx):
        wait(act, S.sum2_ready, 10 * n + (idx - 1))
        j = idx % 2
        out, src = (m.sqm[:, j], m.r[:, idx]) if idx < 6 else \
            (half_of(m.sqm, j, 0), half_of(m.r, idx, 0))
        f(out, src, ACT.Square).then_inc(S.sqr_ready, 1)

    def layer_norm(n, u0, between=None):
        act.wait_ge(S.stat_zero, 2 * n + 2)
        for k in range(6):
            act.wait_ge(m.slot_evac[(u0 + k) % 2], slot_turn(u0 + k) + 1)
            square(n, k)

        def square_half(j):
            act.wait_ge(S.res_half, 2 * n + j + 1)
            square(n, 6 + j)

        def square_b7():
            u = u0 + 7
            act.wait_ge(m.slot_evac[u % 2], slot_turn(u) + 1)
            f(half_of(m.sqm, 1, 1), half_of(m.r, 7, 1), ACT.Square).then_inc(S.sqr_ready, 1)

        def mean_squared(h):
            act.wait_ge(S.stat_done, 2 * n + h + 1)
            f(m.msq[:, h], m.ps[:, 4 + h, 0:HT], ACT.Square, scale=1.0 / D).then_inc(S.msq_ready, 1)

        def log_variance(h):
            act.wait_ge(S.var_ready, 4 * n + 2 * h + 2)
            f(m.msq[:, h], m.msq[:, h], ACT.Ln, bias=m.eps[:, :]).then_inc(S.var_ln, 1)

        def inverse_deviation(h):
            act.wait_ge(S.var_ln, 2 * n + h + 1)
            f(m.rstd[:, h], m.msq[:, h], ACT.Exp, scale=-0.5).then_inc(S.rstd_ready, 1)

        def tile(h, k):
            if n == 3 and not affine_by_act(n, h, k):
                return
            wait_centred(act, m, n, h, k)
            gain, bias = gain_and_bias(m, n, k)
            na = m.na[:, k % 4]
            if n == 3:
                f(half_of(m.r, k, h), na, ACT.Identity, bias=bias, scale=gain).then_inc(S.nrm_x, 1)
                return
            last = f(half_of(m.xh, k, h), na, ACT.Identity, bias=bias, scale=gain)
            if affine_by_act(n, h, k):
                wait_xf_slot(act, m, n, h, k)
                last = f(m.xf[:, k % 4], na, ACT.Identity, bias=bias, scale=gain)
            last.then_inc(S.nrm_x, 1)

        square_half(0)
        square_half(1)
        f(m.table_load[:, :], m.eps[:, :], ACT.Ln)
        mean_squared(0)
        log_variance(0)
        inverse_deviation(0)
        square_b7()
        if n < 3:
            tile(0, 0)
            tile(0, 1)
            mean_squared(1)
            tile(0, 2)
            log_variance(1)
            tile(0, 3)
            tile(0, 4)
            inverse_deviation(1)
            tile(0, 5)
        else:
            f(m.table_load[:, :], m.eps[:, :], ACT.Ln)
            mean_squared(1)
            log_variance(1)
            inverse_deviation(1)
            tile(0, 4)
            tile(0, 5)
        tile(0, 6)
        tile(0, 7)
        if between is not None:
            between()
        for k in range(KT):
            tile(1, k)

    def ffn(layer, u0):
        for b, (kind, c) in enumerate(FFN_BLOCKS):
            if kind == "up":
                with act.Fori(0, 4) as i:
                    for j in range(2):
                        u = u0 + 8 * b + j
                        before = 32 * layer + 8 * c + j
                        act.wait_ge(S.gemm_done, 2 * i + (u + 1))
                        if before >= 2:
                            act.wait_ge(S.hid_ready, 2 * i + (before - 1))
                        f(halves(m.rl[:, j]), bank_pair(m, u % 2), ACT.Relu).then_inc(m.slot_evac[u % 2], 1)
                        act.wait_ge(S.hid_ready, 2 * i + (before + 1))
                        f(one(m.hh, 2 * i + (8 * (c % 2) + j)), m.hq[:, j], ACT.Copy).then_inc(S.hid_hi, 1)

    act.wait_ge(S.tail_out, 16)
    layer_norm(0, U_WOUT + 8)
    ffn(0, U_FFN0)

    def load_v_bias():
        act.wait_ge(S.gemm_done, U_V)
        act.dma_start(m.bb[:, :], A["bias_v"].to_broadcast([P, CMW])).then_inc(S.bb_in, 16)

    layer_norm(1, U_V - 8, load_v_bias)
    wait_x(act, m, 1, 1, 6)
    wait_x(act, m, 1, 1, 7)
    act.dma_start(m.gam[:, :], A["ln_gain"].to_broadcast([P, CMW])).then_inc(S.gam_in, 16)
    act.dma_start(m.bet[:, :], A["ln_bias"].to_broadcast([P, CMW])).then_inc(S.bet_in, 16)
    act.dma_start(m.wst[:, :, :], A["w_spatial"]).then_inc(S.ws_in, 16)
    act.dma_start(m.bsb[:, :, :], A["b_spatial"].to_broadcast([P, 8 * BLK]).rearrange("p (g t) -> p g t", g=8)
                  ).then_inc(S.bs_in, 16)
    act.wait_ge(S.v_zero, 4)
    for part, place in ((0, "v1"), (1, "v2")):
        with act.Fori(0, 2) as i:
            for t in range(NTOK):
                n = TS if t == 4 else P
                act.wait_ge(S.v_bias, 5 * i + (10 * part + t + 1))
                if part == 0:
                    dst = m.v1[0:n, bass.ds(4 * i, 4), t, :]
                else:
                    dst = m.v2[0:n, bass.ds(i, 1), 8 * T:8 * T + 4 * NTOK * P].rearrange(
                        "p a (m t c) -> p (a m) t c", t=NTOK, c=P)[:, :, t, :]
                f(dst, m.ps[0:n, V_BANK[t], :].rearrange("p (m c) -> p m c", c=P), ACT.Gelu_apprx_tanh).then_inc(S.v_gelu, 1)
    act.wait_ge(S.v_mv, NTOK)
    f(m.vrs[:, :, :], m.vmv[:, :, 1:2], ACT.Ln, bias=m.eps[:, :]).then_inc(S.v_ln, 1)
    act.wait_ge(S.v_ln, 1)
    f(m.vrs[:, :, :], m.vrs[:, :, :], ACT.Exp, scale=-0.5).then_inc(S.v_rs, 1)

    def u_tile(i, j):
        u = U_U + j
        act.wait_ge(S.vm_ready, 2 * i + (j + 1))
        act.dma_start(A["v_rows"][:, bass.ds(2 * i + j, 1)].rearrange("p a c -> p (a c)") if not isinstance(i, int)
                      else A["v_rows"][:, 2 * i + j], m.vm[0:TS, j, 4, :]).then_inc(m.vrow_out[j], 16)
        act.wait_ge(S.gemm_done, 2 * i + (u + 1))
        wait(act, S.uv_ready, 2 * i + (j - 1))
        bias = m.pv[:, bass.ds(2 * i + (PV_BU + j), 1)] if not isinstance(i, int) else m.pv[:, PV_BU + j:PV_BU + j + 1]
        f(halves(m.ug[:, j]), bank_pair(m, u % 2), ACT.Gelu_apprx_tanh, bias=bias).then_inc(m.slot_evac[u % 2], 1)
        act.wait_ge(S.uv_ready, 2 * i + (j + 1))
        f(one(m.hh, 2 * i + j), m.sb[:, j], ACT.Copy).then_inc(S.uv_hi, 1)

    u_tile(0, 0)
    u_tile(0, 1)
    with act.Fori(1, 8) as i:
        u_tile(i, 0)
        u_tile(i, 1)
    layer_norm(2, U_CMOUT + 8)
    ffn(1, U_FFN1)
    layer_norm(3, UNITS - 8)



def vector_program(dve, m, A):
    S = m.sem
    tt, ts, stt, cp = dve.tensor_tensor, dve.tensor_scalar, dve.scalar_tensor_tensor, dve.tensor_copy

    dve.wait_ge(S.w_hi, 1)
    tt(m.wl[:, 0], m.wraw[:, 0], m.wh[:, 0], ALU.subtract).then_inc(S.w_ready, 1)
    for k in range(KT):
        dve.wait_ge(S.x_hi, k + 1)
        tt(m.xl[:, k], m.xr[:, k], m.xh[:, k], ALU.subtract).then_inc(S.x_lo, 1)
    dve.wait_ge(S.x_lo, KT)
    dve.memset(m.raw[:, :, 0:HALO], 0.0).then_inc(S.raw_zero, 1)

    d = m.dtt
    dve.wait_ge(S.pv_in, 16)
    dve.wait_ge(S.dt_act, 1)
    ts(m.nega[:, :], m.nega[:, :], -1.0, None, ALU.mult).then_inc(S.dt_dve, 1)
    dve.wait_ge(S.gemm_done, 1)
    ts(halves(d[:, 0]), bank_pair(m, 0), m.pv[:, PV_DTB:PV_DTB + 1], None, ALU.add).then_inc(m.slot_evac[0], 1)
    dve.wait_ge(S.dt_act, 3)
    ts(d[:, 3], d[:, 2], 1.0, None, ALU.add).then_inc(S.dt_dve, 1)
    dve.wait_ge(S.dt_dve, 2)
    ts(d[:, 5], d[:, 3], 1.0, None, ALU.subtract).then_inc(S.dt_dve, 1)
    dve.reciprocal(d[:, 6], d[:, 3]).then_inc(S.dt_dve, 1)
    dve.wait_ge(S.dt_dve, 4)
    tt(d[:, 5], d[:, 2], d[:, 5], ALU.subtract).then_inc(S.dt_dve, 1)
    dve.wait_ge(S.dt_dve, 5)
    tt(d[:, 5], d[:, 5], d[:, 6], ALU.mult).then_inc(S.dt_dve, 1)
    dve.wait_ge(S.dt_dve, 6)
    dve.wait_ge(S.dt_act, 4)
    stt(d[:, 1], d[:, 0], 0.0, d[:, 5], ALU.max, ALU.add).then_inc(S.dt_dve, 1)
    dve.wait_ge(S.dt_dve, 7)
    tt(d[:, 1], d[:, 1], d[:, 4], ALU.add).then_inc(S.dt_dve, 1)
    dve.wait_ge(S.dt_dve, 8)
    ts(d[:, 2], d[:, 1], m.nega[:, :], None, ALU.mult).then_inc(S.dt_dve, 1)
    dve.wait_ge(S.dt_dve, 9)
    dve.wait_ge(S.consts, 6)
    for c in range(NCH):
        q = TS if c == 4 else Q
        dve.tensor_tensor_scan(d[:, DT_OUT, c * Q:c * Q + q], m.ones[:, 0:q], d[:, 2, c * Q:c * Q + q],
                               0.0, ALU.mult, ALU.add).then_inc(S.dt_dve, 1)
    dve.wait_ge(S.dt_dve, DT_ACUM)
    cp(d[0:32, DT_OUT, :], d[0:32, 1, :]).then_inc(S.dt_dve, 1)

    def conv_params(g):
        a = 20 * g + PV_CONV
        src = m.pv[:, a:a + 20] if isinstance(g, int) else m.pv[:, bass.ds(a, 20)]
        wait(dve, S.conv_tap, 16 * g)
        cp(m.cpar[:, :, :].rearrange("p a b -> p (a b)"), src).then_inc(S.cpar_ready, 1)

    def conv(g, j):
        s = (U_SSD + j) % 2
        u = U_SSD + j
        r, a = m.raw[:, j % 2], m.acc[:, j]
        turn = slot_turn(u)
        dve.wait_ge(m.slot_evac[s], 3 * g + (turn + 1))
        dve.wait_ge(S.cpar_ready, g + 1)
        for b, at in enumerate((TP, RAW - HALO)):
            dst = m.ctail[:, g, j, b] if isinstance(g, int) else \
                m.ctail[:, bass.ds(g, 1), j, b].rearrange("p a c -> p (a c)")
            cp(dst, r[:, at:at + HALO]).then_inc(S.ctail_ready, 1)
        if j == 0:
            wait(dve, S.silu_ready, 4 * g)
            dve.wait_ge(S.raw_zero, 1)
        ts(a, r[:, 0:CONV], m.cpar[:, j, 0:1], m.cpar[:, j, 4:5], ALU.mult, ALU.add).then_inc(S.conv_tap, 1)
        for k in range(1, 4):
            dve.wait_ge(S.conv_tap, 16 * g + (4 * j + k))
            stt(a, r[:, k:k + CONV], m.cpar[:, j, k:k + 1], a, ALU.mult, ALU.add).then_inc(S.conv_tap, 1)

    def group_columns(g):
        dve.wait_ge(S.tokd_ready, 2)
        for dst, at in ((m.gdt, 0), (m.gac, HEADS)):
            src = m.tokd[:, :, at + 4 * g:at + 4 * g + 4] if isinstance(g, int) else \
                m.tokd[:, :, bass.ds(4 * g + at, 4)]
            wait(dve, S.m_ready, 5 * g)
            cp(dst[:, :, :], src).then_inc(S.gdt_ready, 1)
        dve.wait_ge(S.gdt_ready, 2 * g + 2)
        dve.wait_ge(S.acb_in, 16 * g + 16)
        last = m.acb[:, :, 0:TP].rearrange("p h (c q) -> p c h q", q=Q)[:, :, :, Q - 1]
        tt(m.win[:, 0:4, :], last, m.gac[:, 0:4, :], ALU.subtract).then_inc(S.win_arg, 1)
        tt(m.win[:, 4, :], m.acb[:, :, T - 1], m.gac[:, 4, :], ALU.subtract).then_inc(S.win_arg, 1)

    def window(g):
        dve.wait_ge(S.win_exp, g + 1)
        tt(m.dtw[:, :, :], m.gdt[:, :, :], m.win[:, :, :], ALU.mult).then_inc(S.dtw_ready, 1)

    def skip_params(g):
        a = 4 * g + PV_GRP
        wait(dve, S.y_skip, 5 * g)
        cp(m.skip[:, :], m.pv[:, a:a + 2] if isinstance(g, int) else m.pv[:, bass.ds(a, 2)]).then_inc(S.skip_ready, 1)

    def norm_params(g):
        a = 4 * g + (PV_GRP + 2)
        wait(dve, S.yn_f, 2 * g)
        cp(m.normw[:, :], m.pv[:, a:a + 2] if isinstance(g, int) else m.pv[:, bass.ds(a, 2)]).then_inc(S.normw_ready, 1)

    conv_params(0)
    conv(0, 0)
    conv(0, 1)
    conv(0, 2)
    conv(0, 3)
    dve.wait_ge(S.tok_t, 1)
    dve.wait_ge(S.tokd_zero, 1)
    cp(m.tokd[:, 0:4, :], m.ps[:, 4, :].rearrange("p (c e) -> p c e", e=P)[:, :, 0:2 * HEADS]).then_inc(S.tokd_ready, 1)
    cp(m.tokd[0:TS, 4, :], m.ps[0:TS, 5, 0:2 * HEADS]).then_inc(S.tokd_ready, 1)
    group_columns(0)
    window(0)
    skip_params(0)

    def before(g, n):
        t0, q = cols(n)
        k = n % 2
        if n == 0:
            dve.wait_ge(S.acb_in, 16 * g + 16)
            dve.wait_ge(S.gdt_ready, 2 * g + 2)
            wait(dve, S.s_done, 5 * g)
        if n >= 2:
            dve.wait_ge(S.s_done, 5 * g + (n - 1))
        for e in range(HPG):
            last = ts(m.dec[0:q, k, e, 0:q], m.acb[0:q, e, t0:t0 + q], m.gac[0:q, ORDER[n], e:e + 1], 0.0,
                      ALU.subtract, ALU.min)
        last.then_inc(S.dec_arg, 1)

    def operands(g, n):
        t0, q = cols(n)
        k = n % 2
        c = ORDER[n]
        b = m.ps[:, 4 + k, :]
        dve.wait_ge(S.s1_done, 5 * g + (n + 1))
        dve.wait_ge(S.consts, 6)
        tt(m.cbm[0:q, k, 0:q], b[0:q, 0:q], m.causal[0:q, 0:q], ALU.mult).then_inc(S.cbm_ready, 1)
        cp(m.btok[0:q, k, :], b[0:q, P:2 * P])
        xt = b[0:q, 2 * P:4 * P].rearrange("p (h d) -> p h d", d=HD)
        tt(m.xdt[0:q, k, :].rearrange("p (h d) -> p h d", d=HD), xt, spread(m.gdt[0:q, c, :], HD), ALU.mult)
        dve.wait_ge(S.dtw_ready, g + 1)
        tt(m.xw[0:q, k, :].rearrange("p (h d) -> p h d", d=HD), xt, spread(m.dtw[0:q, c, :], HD),
           ALU.mult).then_inc(S.xw_ready, 1)
        dve.wait_ge(S.dec_exp, 5 * g + (n + 1))
        dve.wait_ge(S.cbm_ready, 5 * g + (n + 1))
        dec = m.dec[0:q, k, :, 0:q]
        tt(dec, dec, repeat(m.cbm[0:q, k, 0:q], HPG), ALU.mult).then_inc(S.m_ready, 1)

    def after(g, n):
        t0, q = cols(n)
        k = n % 2
        yb = m.ps[:, 5 if n == 1 else 6, :]
        if n == 0:
            wait(dve, S.ms_done, g)
            dve.wait_ge(S.skip_ready, g + 1)
        dve.wait_ge(S.s_done, 5 * g + (n + 1))
        new = state_out(m, n)
        old, out = (m.hs, m.hsn) if n == 1 else (m.hp, m.hp)
        hv = lambda x: x[:, :].rearrange("p (h d) -> p h d", d=HD)
        y = m.y[:, :, t0:t0 + q]
        off = m.yo[:, k, :, 0:q]
        if n > 0:
            if n == 1:
                dve.wait_ge(S.hs_in, 16 * g + 16)
                dve.wait_ge(S.ea_ready, g + 1)
            tt(hv(m.hdec), hv(old), m.elast[:, :, ORDER[n]:ORDER[n] + 1].to_broadcast([P, HPG, HD]), ALU.mult
               ).then_inc(S.hdec_ready, 1)
            tt(off, yb.rearrange("p (j t) -> p j t", t=Q)[:, 2:4, 0:q], m.eab[:, :, t0:t0 + q], ALU.mult
               ).then_inc(S.yo_ready, 1)
        for j in range(2):
            last = stt(m.y[:, j, t0:t0 + q], m.act[:, 2 + j, t0:t0 + q], m.skip[:, j:j + 1], yb[:, j * Q:j * Q + q],
                       ALU.mult, ALU.add)
        last.then_inc(S.y_skip, 1)
        if n > 0:
            dve.wait_ge(S.hdec_ready, 4 * g + n)
            if n == 1:
                wait(dve, S.hs_out, 16 * g)
            dve.wait_ge(S.y_skip, 5 * g + (n + 1))
            dve.wait_ge(S.yo_ready, 4 * g + n)
            tt(y, y, off, ALU.add).then_inc(S.y_evac, 1)
            tt(hv(out), new, hv(m.hdec), ALU.add).then_inc(S.h_ready, 1)
        else:
            wait(dve, S.hp_out, 16 * g)
            cp(hv(out), new).then_inc(S.h_ready, 1)

    def gate(g):
        for j in range(2):
            s = (U_SSD + 4 + j) % 2
            dve.wait_ge(m.slot_evac[s], 3 * g + (slot_turn(U_SSD + 4 + j) + 1))
        dve.wait_ge(S.y_evac, 4 * g + 4)
        wait(dve, S.yn_lo, g)
        tt(m.gy[:, :, :], m.y[:, :, :], m.zs[:, :, :], ALU.mult).then_inc(S.gate_ready, 1)

    def sum_squares(g):
        dve.wait_ge(S.sq_ready, g + 1)
        tt(m.y[:, 0], m.y[:, 0], m.y[:, 1], ALU.add).then_inc(S.sq_sum, 1)

    def scale(g):
        dve.wait_ge(S.rms_ready, g + 1)
        dve.wait_ge(S.normw_ready, g + 1)
        for j in range(2):
            stt(m.gy[:, j], m.gy[:, j], m.normw[:, j:j + 1], m.rms[:, :], ALU.mult, ALU.mult).then_inc(S.yn_f, 1)

    def split(g):
        at = slice(2 * g, 2 * g + 2) if isinstance(g, int) else bass.ds(2 * g, 2)
        dve.wait_ge(S.yn_hi, g + 1)
        tt(m.hl[:, at], m.gy[:, :, :], m.hh[:, at], ALU.subtract).then_inc(S.yn_lo, 1)

    def residual_first(u0, i, j, k=None):
        u = u0 + j
        s = u % 2
        k = 2 * i + j if k is None else k
        dve.wait_ge(S.gemm_done, 2 * i + (u + 1))
        stt(halves(one(m.r, k)), halves(one(m.xh, k).bitcast(F32)), ALPHA, bank_pair(m, s),
            ALU.mult, ALU.add).then_inc(m.slot_evac[s], 1)
        dve.wait_ge(m.slot_evac[s], i + (slot_turn(u) + 1))
        stt(one(m.r, k), one(m.xl, k).bitcast(F32), ALPHA, one(m.r, k), ALU.mult, ALU.add
            ).then_inc(S.res_ready, 1)

    def group(g, more, first=False):
        def nxt(j):
            if more:
                conv(g + 1, j)
            else:
                residual_first(U_WOUT, 0, j, j)

        before(g, 0)
        before(g, 1)
        if not first:
            window(g)
            skip_params(g)
            norm_params(g - 1)
        operands(g, 0)
        operands(g, 1)
        if more:
            conv_params(g + 1)
        after(g, 0)
        before(g, 2)
        after(g, 1)
        operands(g, 2)
        if not first:
            scale(g - 1)
        nxt(0)
        before(g, 3)
        after(g, 2)
        operands(g, 3)
        nxt(1)
        before(g, 4)
        after(g, 3)
        operands(g, 4)
        if not first:
            split(g - 1)
        nxt(2)
        after(g, 4)
        gate(g)
        nxt(3)
        sum_squares(g)
        if more:
            group_columns(g + 1)
        else:
            norm_params(g)
            nxt(4)
            scale(g)
            split(g)
            nxt(5)

    group(0, True, first=True)
    with dve.Fori(1, GROUPS - 1) as g:
        group(g, True)
    group(GROUPS - 1, False)

    def residual_add(u0, i, j, k=None):
        u = u0 + j
        s = u % 2
        r = halves(one(m.r, 2 * i + j if k is None else k))
        dve.wait_ge(S.gemm_done, 2 * i + (u + 1))
        dve.wait_ge(m.slot_evac[1 - s], i + (slot_turn(u - 1) + 1))
        tt(r, bank_pair(m, s), r, ALU.add).then_inc(m.slot_evac[s], 1)

    def block(u0, kind, n=0):
        if kind == "first":
            with dve.Fori(0, 4) as i:
                residual_first(u0, i, 0)
                residual_first(u0, i, 1)
        else:
            dve.wait_ge(S.res_ready, 8 * (n + 1))
            with dve.Fori(0, 4) as i:
                residual_add(u0, i, 0)
                residual_add(u0, i, 1)

    def sums(n, idx, j, s1, s2, tile, sq):
        wait(dve, S.sum1_ready, 10 * n + idx)
        tt(s1, s1, tile, ALU.add).then_inc(S.sum1_ready, 1)
        if idx == 8:
            dve.wait_ge(S.sqr_b_ready, n + 1)
        else:
            dve.wait_ge(S.sqr_ready, 9 * n + min(idx, 8) + 1)
        wait(dve, S.sum2_ready, 10 * n + idx)
        tt(s2, s2, sq, ALU.add).then_inc(S.sum2_ready, 1)

    def layer_norm(n, u0):
        dve.wait_ge(S.res_ready, 8 * (n + 1))
        dve.memset(m.s1[:, :, :], 0.0).then_inc(S.stat_zero, 1)
        dve.memset(m.s2[:, :, :], 0.0).then_inc(S.stat_zero, 1)
        dve.wait_ge(S.stat_zero, 2 * n + 2)
        for k in range(6):
            u = u0 + k
            residual_add(u, 0, 0, k)
            dve.wait_ge(m.slot_evac[u % 2], slot_turn(u) + 1)
            sums(n, k, k % 2, m.s1[:, :, :], m.s2[:, :, :], halves(m.r[:, k]), halves(m.sqm[:, k % 2]))

        def add_a(j):
            s = (u0 + 6 + j) % 2
            r = half_of(m.r, 6 + j, 0)
            dve.wait_ge(S.half_done, 2 * n + j + 1)
            tt(r, m.ps[:, 2 * s, 0:HT], r, ALU.add).then_inc(S.res_half, 1)
            dve.wait_ge(S.res_half, 2 * n + j + 1)
            sums(n, 6 + j, j, m.s1[:, 0], m.s2[:, 0], r, half_of(m.sqm, j, 0))

        def add_b(j):
            u = u0 + 6 + j
            r = half_of(m.r, 6 + j, 1)
            dve.wait_ge(S.gemm_done, u + 1)
            tt(r, m.ps[:, 2 * (u % 2) + 1, 0:HT], r, ALU.add).then_inc(m.slot_evac[u % 2], 1)

        def sums_b(j):
            u = u0 + 6 + j
            dve.wait_ge(m.slot_evac[u % 2], slot_turn(u) + 1)
            sums(n, 8 + j, j, m.s1[:, 1], m.s2[:, 1], half_of(m.r, 6 + j, 1), half_of(m.sqm, j, 1))

        def variance(h):
            dve.wait_ge(S.msq_ready, 2 * n + h + 1)
            stt(m.msq[:, h], m.ps[:, 6 + h, 0:HT], 1.0 / D, m.msq[:, h], ALU.mult, ALU.subtract).then_inc(S.var_ready, 1)
            dve.wait_ge(S.var_ready, 4 * n + 2 * h + 1)
            ts(m.msq[:, h], m.msq[:, h], 0.0, None, ALU.max).then_inc(S.var_ready, 1)

        def scaled_mean(h):
            dve.wait_ge(S.rstd_ready, 2 * n + h + 1)
            stt(m.mr[:, h], m.ps[:, 4 + h, 0:HT], 1.0 / D, m.rstd[:, h], ALU.mult, ALU.mult).then_inc(S.mr_ready, 1)
            dve.wait_ge(S.mr_ready, 2 * n + h + 1)

        def affine(h, k):
            if affine_by_act(n, h, k):
                return
            wait_centred(dve, m, n, h, k)
            gain, bias = gain_and_bias(m, n, k)
            if n < 3:
                wait_xf_slot(dve, m, n, h, k)
            ts(m.xf[:, k % 4] if n < 3 else half_of(m.r, k, h), m.na[:, k % 4], gain, bias, ALU.mult, ALU.add).then_inc(S.nrm_f, 1)

        def tiles_normed(h, after_first=None, before_second=None):
            for k in range(0, KT, 2):
                na = m.na[:, k % 4:k % 4 + 2]
                if (n, h) != (0, 0) or k >= 4:
                    wait_affine(dve, m, *four_before(n, h, k + 1))
                tt(na, m.r[:, k:k + 2, h * HT:(h + 1) * HT], repeat(m.rstd[:, h], 2), ALU.mult).then_inc(S.nrm_a, 1)
                if k > 0:
                    affine(h, k - 2)
                    affine(h, k - 1)
                if k == 2 and before_second is not None:
                    before_second()
                dve.wait_ge(S.nrm_a, 8 * n + 4 * h + k // 2 + 1)
                if n < 3:
                    tt(na, na, repeat(m.mr[:, h], 2), ALU.subtract).then_inc(S.nrm_b, 1)
                else:
                    tt(na[:, 0], na[:, 0], m.mr[:, h], ALU.subtract).then_inc(S.nrm_b, 1)
                if k == 0 and after_first is not None:
                    after_first()
            affine(h, KT - 2)
            affine(h, KT - 1)

        add_a(0)
        add_a(1)
        variance(0)
        add_b(0)
        sums_b(0)
        scaled_mean(0)
        add_b(1)
        if n < 3:
            tiles_normed(0, after_first=lambda: sums_b(1), before_second=lambda: variance(1))
        else:
            sums_b(1)
            tiles_normed(0, before_second=lambda: variance(1))
        scaled_mean(1)
        tiles_normed(1)

    def ffn(layer, u0):
        for b, (kind, c) in enumerate(FFN_BLOCKS):
            if kind == "up":
                with dve.Fori(0, 4) as i:
                    for j in range(2):
                        u = u0 + 8 * b + j
                        done = 32 * layer + 8 * c + j
                        dve.wait_ge(m.slot_evac[u % 2], i + (slot_turn(u) + 1))
                        if done >= 2:
                            dve.wait_ge(S.hid_lo, 2 * i + (done - 1))
                        tt(m.hq[:, j], m.rl[:, j], m.rl[:, j], ALU.mult).then_inc(S.hid_ready, 1)
                        dve.wait_ge(S.hid_hi, 2 * i + (done + 1))
                        k = 2 * i + (8 * (c % 2) + j)
                        tt(one(m.hl, k), m.hq[:, j], one(m.hh, k), ALU.subtract).then_inc(S.hid_lo, 1)
            elif c == 3:
                layer_norm(2 * layer + 1, u0 + 8 * b)
            else:
                block(u0 + 8 * b, "first" if c == 0 else "add", 2 * layer + 1)

    residual_first(U_WOUT + 6, 0, 0, 6)
    residual_first(U_WOUT + 6, 0, 1, 7)
    layer_norm(0, U_WOUT + 8)
    ffn(0, U_FFN0)

    wait_x(dve, m, 1, 1, 6)
    wait_x(dve, m, 1, 1, 7)
    dve.memset(m.v1[TS:P, :, 4, :], 0.0).then_inc(S.v_zero, 1)
    dve.wait_ge(S.gemm_done, U_V)
    v2 = m.v2[TS:P, :, 8 * T:8 * T + 4 * NTOK * P].rearrange("p a (m t c) -> p a m t c", t=NTOK, c=P)
    for a in range(2):
        dve.memset(v2[:, a, :, 4, :], 0.0).then_inc(S.v_zero, 1)
    dve.memset(m.vmv[:, :, :], 0.0).then_inc(S.v_zero, 1)
    dve.wait_ge(S.bb_in, 16)

    def v_bias(b, t):
        n = TS if t == 4 else P
        if t < 4:
            dve.wait_ge(S.v_done, 4 * b + (t + 1))
        else:
            dve.wait_ge(S.gemm_done, 4 * b + (U_V + 4))
        bank = m.ps[0:n, V_BANK[t], :]
        row = m.bb[0:n, bass.ds(512 * b, 512)] if not isinstance(b, int) else m.bb[0:n, 512 * b:512 * (b + 1)]
        tt(bank, bank, row, ALU.add).then_inc(S.v_bias, 1)

    for part in range(2):
        with dve.Fori(0, 2) as i:
            for t in range(NTOK):
                v_bias(i + 2 * part, t)
                if t > 0:
                    v_stats(dve, m, part, i, t - 1)
            v_stats(dve, m, part, i, NTOK - 1)
    dve.wait_ge(S.v_stat, 20)
    dve.wait_ge(S.v_zero, 4)
    for t in range(NTOK):
        n = TS if t == 4 else P
        dve.bn_aggr(m.vmv[0:n, t, :], m.vst[0:n, t, :, :].rearrange("p a b -> p (a b)")).then_inc(S.v_mv, 1)
    dve.wait_ge(S.v_rs, 1)
    dve.wait_ge(S.v_mv, NTOK)
    dve.wait_ge(S.gam_in, 16)
    dve.wait_ge(S.bet_in, 16)
    dve.wait_ge(S.bs_in, 16)

    def norm_v(k, kv, j):
        if not isinstance(k, int):
            dve.wait_ge(m.vrow_out[j], 8 * (k - j))
        for t in range(NTOK):
            src = m.v1[:, kv, t, :] if isinstance(kv, int) else m.v1[:, bass.ds(kv, 1), t, :].rearrange("p a c -> p (a c)")
            o = ts(m.vm[:, j, t, :], src, m.vmv[:, t, 0:1], m.vrs[:, t, 0:1], ALU.subtract, ALU.mult)
        o.then_inc(S.vm_n, 1)
        cut = (lambda x: x[:, k * P:(k + 1) * P]) if isinstance(k, int) else (lambda x: x[:, bass.ds(P * k, P)])
        dve.wait_ge(S.vm_n, k + 1)
        tt(m.vm[:, j], m.vm[:, j], repeat(cut(m.gam), NTOK), ALU.mult).then_inc(S.vm_g, 1)
        dve.wait_ge(S.vm_g, k + 1)
        tt(m.vm[:, j], m.vm[:, j], repeat(cut(m.bet), NTOK), ALU.add).then_inc(S.vm_ready, 1)

    def spatial_weights(g):
        cp(m.wsm[:, :], m.wst[:, g, :] if isinstance(g, int) else m.wst[:, bass.ds(g, 1), :].rearrange("p a c -> p (a c)")
           ).then_inc(S.wsm_ready, 1)

    def mix(i, j):
        row = m.bsb[:, bass.ds(i, 1), :].rearrange("p a c -> p (a c)") if not isinstance(i, int) else m.bsb[:, i, :]
        u = U_U + j
        dve.wait_ge(S.mix_done, 2 * i + (j + 1))
        tt(m.sb[:, j, 0:TP].rearrange("p (n t) -> p n t", t=BLK),
           m.ps[:, 4 + 2 * j, :].rearrange("p (n t) -> p n t", t=BLK), repeat(row, 4), ALU.add).then_inc(S.s_bias, 1)
        tt(m.sb[:, j, TP:T], m.ps[:, 5 + 2 * j, 0:TS], row[:, 0:TS], ALU.add).then_inc(S.s_bias, 1)
        dve.wait_ge(S.s_bias, 4 * i + (2 * j + 2))
        dve.wait_ge(m.slot_evac[u % 2], i + (slot_turn(u) + 1))
        tt(m.sb[:, j], m.sb[:, j], m.ug[:, j], ALU.mult).then_inc(S.uv_ready, 1)
        dve.wait_ge(S.uv_hi, 2 * i + (j + 1))
        k = 2 * i + j
        tt(one(m.hl, k), m.sb[:, j], one(m.hh, k), ALU.subtract).then_inc(S.uv_lo, 1)

    dve.wait_ge(S.ws_masked, 1)
    spatial_weights(0)
    norm_v(0, 0, 0)
    norm_v(1, 1, 1)
    with dve.Fori(0, 3) as i:
        mix(i, 0)
        norm_v(2 * i + 2, 2 * i + 2, 0)
        mix(i, 1)
        spatial_weights(i + 1)
        norm_v(2 * i + 3, 2 * i + 3, 1)
    dve.wait_ge(S.vm_ready, 8)
    for a in range(2):
        cp(m.v1[:, 4 * a:4 * a + 4].rearrange("p m t c -> p (m t c)"), m.v2[:, a, 8 * T:8 * T + 4 * NTOK * P]
           ).then_inc(S.v_moved, 1)
    dve.wait_ge(S.v_moved, 2)
    with dve.Fori(3, 7) as i:
        mix(i, 0)
        norm_v(2 * i + 2, 2 * i - 6, 0)
        mix(i, 1)
        spatial_weights(i + 1)
        norm_v(2 * i + 3, 2 * i - 5, 1)
    mix(7, 0)
    mix(7, 1)
    block(U_CMOUT, "first")
    for j in range(2):
        dve.wait_ge(m.vrow_out[j], 16 * 8)
    layer_norm(2, U_CMOUT + 8)
    ffn(1, U_FFN1)


def v_stats(dve, m, part, i, t):
    S = m.sem
    n = TS if t == 4 else P
    dve.wait_ge(S.v_gelu, 5 * i + (10 * part + t + 1))
    if part == 0:
        src = m.v1[0:n, bass.ds(4 * i, 4), t, :]
    else:
        src = m.v2[0:n, bass.ds(i, 1), 8 * T:8 * T + 4 * NTOK * P].rearrange(
            "p a (m t c) -> p (a m) t c", t=NTOK, c=P)[:, :, t, :]
    dst = m.vst[0:n, t, bass.ds(i + 2 * part, 1), :].rearrange("p a b -> p (a b)")
    dve.bn_stats(dst, src).then_inc(S.v_stat, 1)



def encoder_program(nc, A):
    with ExitStack() as ctx:
        m = Memory(nc, ctx)
        A = dict(A, acum=m.acum_dram)
        block = ctx.enter_context(nc.Block())

        @block.sync
        def _(eng):
            sync_program(eng, m, A)

        @block.gpsimd
        def _(eng):
            pool_program(eng, m, A)

        @block.scalar
        def _(eng):
            scalar_program(eng, m, A)

        @block.tensor
        def _(eng):
            tensor_program(eng, m, A)

        @block.vector
        def _(eng):
            vector_program(eng, m, A)



def stream_units(w):
    k, n = w.shape
    return w.reshape(k // UNIT, KT, P, n // P, P).transpose(0, 3, 2, 1, 4).reshape(-1, P, UNIT)


def tiles(v):
    return v.reshape(v.shape[:-1] + (-1, P)).transpose((len(v.shape),) + tuple(range(len(v.shape))))


def kernel(x_prompt, x_sample, state_ssm, state_conv, ssd_w_in, ssd_conv_w, ssd_conv_b, ssd_dt_bias, ssd_a_log, ssd_d,
           ssd_norm_w, ssd_w_out, cm_w_in, cm_b_in, cm_ln_g, cm_ln_b, cm_w_s, cm_b_s, cm_w_out, ffn_w1, ffn_w2,
           ln1_g, ln1_b, ln2_g, ln2_b):
    import numpy as np
    import concourse.bacc as bacc
    from concourse.bass_utils import run_bass_kernel_spmd

    f = np.ascontiguousarray
    di = 2 * D
    w_in = ssd_w_in[0]
    z, x, b, c = (stream_units(w_in[:, at:at + n]) for at, n in
                  ((0, di), (di, di), (2 * di, GROUPS * NST), (2 * di + GROUPS * NST, GROUPS * NST)))
    dt = stream_units(np.concatenate([w_in[:, -HEADS:]] * 4, axis=1))
    parts = [dt]
    for g in range(GROUPS):
        parts += [b[g:g + 1], c[g:g + 1], x[2 * g:2 * g + 2], z[2 * g:2 * g + 2]]
    parts.append(stream_units(ssd_w_out[0]))

    def ffn(layer):
        up, down = stream_units(ffn_w1[layer]), stream_units(ffn_w2[layer])
        return [(up if kind == "up" else down)[8 * k:8 * k + 8] for kind, k in FFN_BLOCKS]

    parts += ffn(0)
    v = cm_w_in[0][:, CMW:]
    parts.append(v.reshape(4, 2, P, 4, 512).transpose(3, 0, 2, 1, 4).reshape(16, P, UNIT))
    parts.append(stream_units(cm_w_in[0][:, :CMW]))
    parts.append(stream_units(cm_w_out[0]))
    parts += ffn(1)
    wstream = f(np.concatenate(parts))

    conv = np.concatenate([ssd_conv_w[0], ssd_conv_b], axis=0)
    by_tile = tiles(conv).transpose(0, 2, 1)
    conv_g = np.stack([by_tile[:, [16 + g, 24 + g, 2 * g, 2 * g + 1]] for g in range(GROUPS)], axis=1)
    skip = tiles(np.repeat(ssd_d[0], HD))
    grp = np.concatenate([skip.reshape(P, GROUPS, 2), tiles(ssd_norm_w[0]).reshape(P, GROUPS, 2)], axis=2)
    lns = np.stack([np.concatenate([tiles(a[i]), tiles(q[i])], axis=1)
                    for i in range(2) for a, q in ((ln1_g, ln1_b), (ln2_g, ln2_b))], axis=1)
    pv = f(np.concatenate([
        conv_g.reshape(P, -1), grp.reshape(P, -1), tiles(cm_b_in[0, :CMW]), lns.reshape(P, -1),
        np.concatenate([ssd_dt_bias[0]] * 4)[:, None], np.concatenate([ssd_a_log[0]] * 4)[:, None]], axis=1))
    assert pv.shape == (P, PV_N)

    halo = tiles(state_conv[0, 0]).transpose(0, 2, 1)
    halo = np.stack([halo[:, [16 + g, 24 + g, 2 * g, 2 * g + 1]] for g in range(GROUPS)], axis=1)
    xt = np.concatenate([x_prompt[0], x_sample[0]], axis=0)
    arrays = {
        "wstream": wstream,
        "x": f(xt.T.reshape(KT, P, T).transpose(1, 0, 2)),
        "pv": pv,
        "conv_halo": f(halo),
        "ssm_in": f(state_ssm[0, 0].transpose(2, 0, 1).reshape(NST, HEADS * HD)),
        "bias_v": f(cm_b_in[:, CMW:]),
        "ln_gain": f(cm_ln_g),
        "ln_bias": f(cm_ln_b),
        "w_spatial": f(cm_w_s[0].transpose(2, 0, 1)),
        "b_spatial": f(cm_b_s[0].reshape(1, -1)),
    }
    outs = {
        "y": (P, KT, T), "ssm_p": (NST, HEADS * HD), "ssm_s": (NST, HEADS * HD),
        "conv_tail": (P, GROUPS, 4, 2, HALO), "v_rows": (TS, 16, P),
    }
    nc = bacc.Bacc("TRN2", target_bir_lowering=False, num_devices=1)
    A = {n: nc.dram_tensor(n, a.shape, mybir.dt.from_np(a.dtype), kind="ExternalInput").ap() for n, a in arrays.items()}
    A.update({n: nc.dram_tensor("out_" + n, s, F32, kind="ExternalOutput").ap() for n, s in outs.items()})
    encoder_program(nc, A)
    got = run_bass_kernel_spmd(nc, [arrays], core_ids=[0]).results[0]

    y = got["out_y"].transpose(1, 0, 2).reshape(D, T).T
    tail = got["out_conv_tail"]
    rows = tail.transpose(3, 4, 1, 2, 0)
    xs = rows[:, :, :, 2:4].reshape(2, HALO, di)
    bs = rows[:, :, :, 0].reshape(2, HALO, -1)
    cs = rows[:, :, :, 1].reshape(2, HALO, -1)
    new_rows = np.concatenate([xs, bs, cs], axis=2)
    ssm = [got[n].reshape(NST, HEADS, HD).transpose(1, 2, 0)[None, None] for n in ("out_ssm_p", "out_ssm_s")]
    return (f(y[None, :TP]), f(y[None, TP:]), f(ssm[0]), f(new_rows[0][None, None]), f(ssm[1]), f(new_rows[1][None, None]),
            f(got["out_v_rows"].reshape(1, 1, TS, CMW)))
```
